# Optimizing a Trainium2 kernel written in Bass

```python
import math
import jax, jax.numpy as jnp
from jax import lax
import numpy as np

D_MODEL = 1024
BATCH = 1
SEQ = 512
DEPTH = 2
DEC_BATCH = 8
DEC_SEQ = 4
PAST_LEN = 1024
PAGE_SIZE = 128

N_A_LAYERS = DEPTH // 2
N_B_LAYERS = DEPTH - N_A_LAYERS
RET_HEADS = 4
RET_DK = D_MODEL // RET_HEADS
RET_DV = 2 * D_MODEL // RET_HEADS
RET_CHUNK = 128
ROPE_BASE = 10000.0
FOX_HEADS = 16
FOX_HD = D_MODEL // FOX_HEADS
Q_BLOCK = 128
D_FF = -(-8 * D_MODEL // (3 * 256)) * 256
EPS = 1e-6
FORGET_BIAS_INIT = 6.0

kernel_name = 'yoco_retention_fox_decoder_step'

def _rmsnorm(x, g):
    xf = x.astype(jnp.float32)
    y = xf * lax.rsqrt(jnp.mean(xf * xf, axis=-1, keepdims=True) + EPS)
    return (y * g.astype(jnp.float32)).astype(x.dtype)

def _modulate(h, shift, scale):
    return h * (1 + scale[:, None, :]) + shift[:, None, :]

def _rotary(x, pos):
    half = x.shape[-1] // 2
    freqs = ROPE_BASE ** (-jnp.arange(half, dtype=jnp.float32) / half)
    ang = pos.astype(jnp.float32)[:, None] * freqs[None, :]
    cos = jnp.cos(ang)[None, :, None, :]
    sin = jnp.sin(ang)[None, :, None, :]
    xf = x.astype(jnp.float32)
    x1, x2 = xf[..., :half], xf[..., half:]
    return jnp.concatenate([x1 * cos - x2 * sin, x1 * sin + x2 * cos], axis=-1).astype(x.dtype)

def _retention_scan(q, k, v, s0):
    B, T, H, DK = q.shape
    DV = v.shape[-1]
    C = math.gcd(T, RET_CHUNK)
    n = T // C
    log_g = jnp.log1p(-jnp.exp2(-5.0 - jnp.arange(H, dtype=jnp.float32)))
    i = jnp.arange(C, dtype=jnp.float32)
    diff = i[:, None] - i[None, :]
    inner = jnp.where(diff[None] >= 0, jnp.exp(log_g[:, None, None] * jnp.maximum(diff, 0.0)[None]), 0.0)
    cross = jnp.exp(log_g[None, :] * (i[:, None] + 1.0))
    kdec = jnp.exp(log_g[None, :] * (C - 1.0 - i)[:, None])
    cdec = jnp.exp(log_g * C)

    def to_chunks(a):
        return a.astype(jnp.float32).reshape(B, n, C, H, a.shape[-1]).transpose(1, 0, 2, 3, 4)

    def step(S, inp):
        qc, kc, vc = inp
        sc = jnp.einsum('bihd,bjhd->bhij', qc, kc) * inner[None]
        o = (jnp.einsum('bhij,bjhe->bihe', sc, vc)
             + jnp.einsum('bihd,bhde->bihe', qc, S) * cross[None, :, :, None])
        S = S * cdec[None, :, None, None] + jnp.einsum('bjhd,bjhe->bhde', kc * kdec[None, :, :, None], vc)
        return S, o

    S, o = lax.scan(step, s0.astype(jnp.float32), (to_chunks(q), to_chunks(k), to_chunks(v)))
    o = o.transpose(1, 0, 2, 3, 4).reshape(B, T, H, DV)
    return o, S

def _retention_mixer(h, pos, s0, w_in, w_out):
    B, T, _ = h.shape
    proj = h @ w_in
    q, k, v, g = jnp.split(proj, [D_MODEL, 2 * D_MODEL, 4 * D_MODEL], axis=-1)
    q = _rotary(q.reshape(B, T, RET_HEADS, RET_DK), pos)
    k = _rotary(k.reshape(B, T, RET_HEADS, RET_DK), pos) * (RET_DK ** -0.5)
    v = v.reshape(B, T, RET_HEADS, RET_DV)
    o, S = _retention_scan(q, k, v, s0)
    o = o * lax.rsqrt(jnp.mean(o * o, axis=-1, keepdims=True) + EPS)
    o = o.reshape(B, T, RET_HEADS * RET_DV).astype(h.dtype) * jax.nn.silu(g)
    return o @ w_out, S.astype(s0.dtype)

def _shared_kvf(x, c_act, kv_norm_g, w_kvmod, b_kvmod, w_kvf, b_f, k_norm_g):
    B, T, _ = x.shape
    shift, scale = jnp.split(c_act @ w_kvmod + b_kvmod, 2, axis=-1)
    h = _modulate(_rmsnorm(x, kv_norm_g), shift, scale)
    k, v, fl = jnp.split(h @ w_kvf, [D_MODEL, 2 * D_MODEL], axis=-1)
    k = _rmsnorm(k.reshape(B, T, FOX_HEADS, FOX_HD), k_norm_g)
    v = v.reshape(B, T, FOX_HEADS, FOX_HD)
    logf = jax.nn.log_sigmoid((fl + b_f).astype(jnp.float32)).astype(x.dtype)
    return k, v, logf

def _fox_prompt(q, k, v, logf):
    B, T, H, HD = q.shape
    nb = T // Q_BLOCK
    scale = HD ** -0.5
    F = jnp.cumsum(logf.astype(jnp.float32), axis=1).transpose(0, 2, 1)
    kpos = jnp.arange(T)
    qb = q.reshape(B, nb, Q_BLOCK, H, HD).transpose(1, 0, 2, 3, 4)
    Fb = F.reshape(B, H, nb, Q_BLOCK).transpose(2, 0, 1, 3)
    pb = kpos.reshape(nb, Q_BLOCK)

    def block(args):
        qi, Fi, pi = args
        s = (jnp.einsum('bqhd,bkhd->bhqk', qi, k).astype(jnp.float32) * scale
             + Fi[..., None] - F[:, :, None, :])
        s = jnp.where(pi[:, None] >= kpos[None, :], s, -jnp.inf)
        p = jax.nn.softmax(s, axis=-1).astype(v.dtype)
        return jnp.einsum('bhqk,bkhd->bqhd', p, v)

    o = lax.map(block, (qb, Fb, pb))
    return o.transpose(1, 0, 2, 3, 4).reshape(B, T, H, HD)

def _fox_sample(q, k, v, logf, pk, pv, R):
    T = q.shape[1]
    P = pk.shape[1]
    scale = q.shape[-1] ** -0.5
    Fn = jnp.cumsum(logf.astype(jnp.float32), axis=1).transpose(0, 2, 1)
    s_past = (jnp.einsum('bqhd,bkhd->bhqk', q, pk).astype(jnp.float32) * scale
              + Fn[..., None] + R[:, :, None, :])
    s_new = (jnp.einsum('bqhd,bkhd->bhqk', q, k).astype(jnp.float32) * scale
             + Fn[..., None] - Fn[:, :, None, :])
    t = jnp.arange(T)
    s_new = jnp.where(t[:, None] >= t[None, :], s_new, -jnp.inf)
    p = jax.nn.softmax(jnp.concatenate([s_past, s_new], axis=-1), axis=-1).astype(v.dtype)
    return (jnp.einsum('bhqk,bkhd->bqhd', p[..., :P], pv)
            + jnp.einsum('bhqk,bkhd->bqhd', p[..., P:], v))

def _trunk(x, c, pos, ret_s0, past, w_mod, b_mod, ret_norm_g, w_ret_in, w_ret_out,
           attn_norm_g, w_q, q_norm_g, w_o, ffn_norm_g, w_ffn_in, w_ffn_out,
           kv_norm_g, w_kvmod, b_kvmod, w_kvf, b_f, k_norm_g):
    B, T, _ = x.shape
    c_act = jax.nn.silu(c)
    ret_states = []
    shared = None
    for l in range(DEPTH):
        sh1, sc1, g1, sh2, sc2, g2 = jnp.split(c_act @ w_mod[l] + b_mod[l], 6, axis=-1)
        if l < N_A_LAYERS:
            h = _modulate(_rmsnorm(x, ret_norm_g[l]), sh1, sc1)
            out, S = _retention_mixer(h, pos, ret_s0[l], w_ret_in[l], w_ret_out[l])
            ret_states.append(S)
        else:
            if shared is None:
                shared = _shared_kvf(x, c_act, kv_norm_g, w_kvmod, b_kvmod, w_kvf, b_f, k_norm_g)
            k, v, logf = shared
            j = l - N_A_LAYERS
            h = _modulate(_rmsnorm(x, attn_norm_g[j]), sh1, sc1)
            q = _rmsnorm((h @ w_q[j]).reshape(B, T, FOX_HEADS, FOX_HD), q_norm_g[j])
            if past is None:
                o = _fox_prompt(q, k, v, logf)
            else:
                o = _fox_sample(q, k, v, logf, past[0], past[1], past[2])
            out = o.reshape(B, T, D_MODEL) @ w_o[j]
        x = x + (1 + g1[:, None, :]) * out
        h = _modulate(_rmsnorm(x, ffn_norm_g[l]), sh2, sc2)
        gate, up = jnp.split(h @ w_ffn_in[l], 2, axis=-1)
        x = x + (1 + g2[:, None, :]) * ((jax.nn.silu(gate) * up) @ w_ffn_out[l])
    k, v, logf = shared
    return x, jnp.stack(ret_states), k, v, logf

def setup_inputs(seed: int = 0) -> dict:
    key = jax.random.key(seed)
    ks = jax.random.split(key, 32)
    f32 = jnp.float32

    def nrm(k, shape, scale):
        return jax.random.normal(k, shape, f32) * scale

    n_pages = PAST_LEN // PAGE_SIZE
    n_used = DEC_BATCH * n_pages
    n_pool = n_used + max(1, n_used // 4)
    perm = jax.random.permutation(ks[0], n_pool)
    page_table = perm[:n_used].reshape(DEC_BATCH, n_pages).astype(jnp.int32)
    D = D_MODEL
    return {
        'x_prompt': nrm(ks[1], (BATCH, SEQ, D), 1.0),
        'x_sample': nrm(ks[2], (DEC_BATCH, DEC_SEQ, D), 1.0),
        'cache_k': nrm(ks[3], (n_pool, PAGE_SIZE, FOX_HEADS, FOX_HD), 1.0),
        'cache_v': nrm(ks[4], (n_pool, PAGE_SIZE, FOX_HEADS, FOX_HD), 1.0),
        'cache_logf': jax.nn.log_sigmoid(FORGET_BIAS_INIT + 1.5 + nrm(ks[5], (n_pool, PAGE_SIZE, FOX_HEADS), 0.5)),
        'state_ret': nrm(ks[6], (N_A_LAYERS, DEC_BATCH, RET_HEADS, RET_DK, RET_DV), 0.3),
        'page_table': page_table,
        'c_prompt': nrm(ks[7], (BATCH, D), 1.0),
        'c_sample': nrm(ks[8], (DEC_BATCH, D), 1.0),
        'w_mod': nrm(ks[9], (DEPTH, D, 6 * D), 0.5 * D ** -0.5),
        'b_mod': nrm(ks[10], (DEPTH, 6 * D), 0.01),
        'ret_norm_g': 1.0 + nrm(ks[11], (N_A_LAYERS, D), 0.02),
        'w_ret_in': nrm(ks[12], (N_A_LAYERS, D, 6 * D), D ** -0.5),
        'w_ret_out': nrm(ks[13], (N_A_LAYERS, 2 * D, D), (2 * D) ** -0.5),
        'attn_norm_g': 1.0 + nrm(ks[14], (N_B_LAYERS, D), 0.02),
        'w_q': nrm(ks[15], (N_B_LAYERS, D, D), D ** -0.5),
        'q_norm_g': 1.0 + nrm(ks[16], (N_B_LAYERS, FOX_HD), 0.02),
        'w_o': nrm(ks[17], (N_B_LAYERS, D, D), D ** -0.5),
        'ffn_norm_g': 1.0 + nrm(ks[18], (DEPTH, D), 0.02),
        'w_ffn_in': nrm(ks[19], (DEPTH, D, 2 * D_FF), D ** -0.5),
        'w_ffn_out': nrm(ks[20], (DEPTH, D_FF, D), D_FF ** -0.5),
        'kv_norm_g': 1.0 + nrm(ks[21], (D,), 0.02),
        'w_kvmod': nrm(ks[22], (D, 2 * D), 0.5 * D ** -0.5),
        'b_kvmod': nrm(ks[23], (2 * D,), 0.01),
        'w_kvf': nrm(ks[24], (D, 2 * D + FOX_HEADS), D ** -0.5),
        'b_f': FORGET_BIAS_INIT + nrm(ks[25], (FOX_HEADS,), 0.1),
        'k_norm_g': 1.0 + nrm(ks[26], (FOX_HD,), 0.02),
    }

def reference(x_prompt, x_sample, cache_k, cache_v, cache_logf, state_ret, page_table,
              c_prompt, c_sample, w_mod, b_mod, ret_norm_g, w_ret_in, w_ret_out,
              attn_norm_g, w_q, q_norm_g, w_o, ffn_norm_g, w_ffn_in, w_ffn_out,
              kv_norm_g, w_kvmod, b_kvmod, w_kvf, b_f, k_norm_g):
    params = (w_mod, b_mod, ret_norm_g, w_ret_in, w_ret_out, attn_norm_g, w_q, q_norm_g, w_o,
              ffn_norm_g, w_ffn_in, w_ffn_out, kv_norm_g, w_kvmod, b_kvmod, w_kvf, b_f, k_norm_g)
    n_pages = PAST_LEN // PAGE_SIZE
    past_len = n_pages * PAGE_SIZE
    Bp, Tp = x_prompt.shape[:2]
    Bd, Td = x_sample.shape[:2]

    s0_prompt = jnp.zeros((N_A_LAYERS, Bp, RET_HEADS, RET_DK, RET_DV), state_ret.dtype)
    y_prompt, st_p, k_p, v_p, lf_p = _trunk(x_prompt, c_prompt, jnp.arange(Tp), s0_prompt, None, *params)

    pk = cache_k[page_table].reshape(Bd, past_len, FOX_HEADS, FOX_HD)
    pv = cache_v[page_table].reshape(Bd, past_len, FOX_HEADS, FOX_HD)
    plf = cache_logf[page_table].reshape(Bd, past_len, FOX_HEADS).astype(jnp.float32)
    R = (lax.cumsum(plf, axis=1, reverse=True) - plf).transpose(0, 2, 1)
    pos_s = PAST_LEN + jnp.arange(Td)
    y_sample, st_s, k_s, v_s, lf_s = _trunk(x_sample, c_sample, pos_s, state_ret, (pk, pv, R), *params)

    return (y_prompt, y_sample, st_p, st_s, k_p, v_p, lf_p, k_s, v_s, lf_s)


_drawn_inputs = setup_inputs


def setup_inputs(seed=0):
    import zlib

    import numpy as np

    out = dict(_drawn_inputs(seed))
    spreads = {}
    factors = {'cache_logf': 64.0,
     'attn_norm_g': 24.812,
     'q_norm_g': 8.0,
     'ffn_norm_g': 2.746,
     'b_kvmod': 3.702,
     'k_norm_g': 9.892}
    for name, (base, spread) in spreads.items():
        noise = np.random.default_rng([zlib.crc32(name.encode()), seed]).standard_normal(out[name].shape)
        drawn = base * np.exp(spread * noise) if base else spread * noise
        out[name] = __import__('jax').numpy.asarray(drawn.astype(out[name].dtype))
    for name, factor in factors.items():
        out[name] = (out[name] * factor).astype(out[name].dtype)
    return out
```

```python
from contextlib import ExitStack

import numpy as np
import concourse.bass as bass
from concourse import mybir

F32 = mybir.dt.float32
F32R = mybir.dt.float32r
BF16 = mybir.dt.bfloat16
I32 = mybir.dt.int32
ALU = mybir.AluOpType
ACT = mybir.ActivationFunctionType
AX = mybir.AxisListType

P = 128
D = 1024
DT = D // P
SEQ = 512
DEC_B, DEC_T = 8, 4
NS = DEC_B * DEC_T
NT = SEQ + NS
HALF = NT // 2
RT = SEQ // P
NC = 1 + DEC_B
RH = 4
DK, DV = 256, 512
FH, HD = 16, 64
NPAIR = FH // 2
FF = 2816
FFT = FF // P // 2
PAST, PAGE = 1024, 128
NPG = PAST // PAGE
EPS = 1e-6
SLAB = 8
RAW, SPL = 4, 2
PRING = 2
MRING = 2
NMOD = 14 * DT
MOD_FIRST = 2 * DT
MOD_PER_HEAD = (NMOD - MOD_FIRST) // RH
BIG = 1e30

V_B = 0
V_RET = NMOD
V_ATT = V_RET + DT
V_FFN = V_ATT + DT
V_KV = V_FFN + 2 * DT
V_QN = V_KV + DT
V_KN = V_QN + 1
V_BF = V_KN + 1
NV = V_BF + 1

C_ID = 0
C_BD = C_ID + P
C_US = C_BD + P
C_CM = C_US + P
C_NM = C_CM + P
C_END = C_NM + NS
R_COS = 0
R_SIN = NT
R_CR = 2 * NT
R_KP = R_CR + RH * NS
R_KS = R_KP + RH * RT
R_DS = R_KS + RH * DEC_B
R_CD = R_DS + RH * NS
R_END = R_CD + RH


def constants():
    f = np.float32
    c = np.zeros((P, C_END), f)
    i = np.arange(P)
    c[:, C_ID:C_ID + P] = np.eye(P)
    c[:, C_BD:C_BD + P] = (i[:, None] // HD) == (i[None, :] // HD)
    c[:, C_US:C_US + P] = i[:, None] > i[None, :]
    c[:, C_CM:C_CM + P] = np.where(i[None, :] <= i[:, None], 0, -BIG)
    j, q = np.arange(NS)[:, None], np.arange(NS)[None, :]
    same = (j // DEC_T == q // DEC_T) & (j % DEC_T <= q % DEC_T)
    c[:NS, C_NM:C_NM + NS] = np.where(same, 0, -BIG)

    r = np.zeros((P, R_END), f)
    dec = np.zeros((RH, P, SEQ), f)
    half = DK // 2
    freqs = f(10000.0) ** (-np.arange(half, dtype=f) / f(half))
    pos = np.concatenate([np.arange(SEQ), np.tile(PAST + np.arange(DEC_T), DEC_B)]).astype(f)
    ang = (freqs[:, None] * pos[None, :]).astype(f)
    r[:, R_COS:R_COS + NT] = np.cos(ang)
    r[:, R_SIN:R_SIN + NT] = np.sin(ang)
    log_g = np.log1p(-np.exp2(-5.0 - np.arange(RH)))
    t = np.arange(NS) % DEC_T
    b = np.arange(NS) // DEC_T
    for h in range(RH):
        r[:, R_CR + h * NS:R_CR + (h + 1) * NS] = np.exp(log_g[h] * (t + 1))[None, :]
        for rt in range(RT):
            r[:, R_KP + h * RT + rt] = np.exp(log_g[h] * (SEQ - 1 - rt * P - i))
        for bb in range(DEC_B):
            r[:NS, R_KS + h * DEC_B + bb] = np.where(b == bb, np.exp(log_g[h] * (DEC_T - 1 - t)), 0)
        r[:NS, R_DS + h * NS:R_DS + (h + 1) * NS] = np.where(same, np.exp(log_g[h] * np.maximum(q - j, 0)), 0)
        off = np.arange(SEQ)[None, :] - i[:, None]
        dec[h] = np.where(off >= 0, np.exp(log_g[h] * np.maximum(off, 0)), 0)
        r[:, R_CD + h] = np.exp(log_g[h] * DEC_T)
    return c, r, dec


def program(nc, A):
    ctx = ExitStack()

    def sb(name, shape, dt=F32, where=None):
        return (where or ctx).enter_context(nc.sbuf_tensor(name, shape, dt))

    def sem(name):
        return ctx.enter_context(nc.semaphore(name))

    with ctx:
        x = sb("x", [P, DT, NT])
        h_hi = sb("h_hi", [P, DT, NT], F32R)
        h_lo = sb("h_lo", [P, DT, NT], F32R)
        raw = sb("raw", [P, RAW, SLAB * P])
        w_hi = sb("w_hi", [P, SPL, SLAB * P], F32R)
        w_lo = sb("w_lo", [P, SPL, SLAB * P], F32R)
        mraw = sb("mraw", [P, MRING, SLAB * P])
        mod = sb("mod", [P, NMOD, NC])
        gain = sb("gain", [P, DT, NC])
        vec = sb("vec", [P, NV])
        cst = sb("cst", [P, C_END])
        ones = sb("ones", [P, P])
        cact = sb("cact", [P, DT, NC])
        ctmp = sb("ctmp", [P, DT, NC])
        var = sb("var", [P, NT])
        rstd = sb("rstd", [P, NT])
        newt = sb("newt", [P, NT])
        xs = sb("xs", [P, 2, NT])
        hf = sb("hf", [P, 2, NT])
        m0 = sb("q_gain", [P, 1])
        tabs = sb("tabs", [1, DEC_B * NPG], I32)
        ident = cst[:, C_ID:C_ID + P]

        pj = [ctx.enter_context(nc.psum_tensor(f"proj{i}", [P, 2, 512], F32)) for i in range(2)]
        bk = [ctx.enter_context(nc.psum_tensor(f"bank{i}", [P, 512], F32)) for i in range(4)]

        ret = ExitStack()
        rc = sb("rc", [P, R_END], where=ret)
        dec = sb("ret_dec", [P, 2, SEQ], where=ret)
        qT = sb("ret_q", [P, 2, NT], where=ret)
        kT = sb("ret_k", [P, 2, NT], where=ret)
        qx = sb("ret_qx", [P, 2, NS], where=ret)
        vT = sb("ret_vT", [P, 4, NT], where=ret)
        vtok = sb("ret_vtok", [P, RT, DV], where=ret)
        vs = sb("ret_vs", [NS, DV], where=ret)
        ktok = sb("ret_ktok", [P, RT, DK], where=ret)
        ks = sb("ret_ks", [NS, DK], where=ret)
        kb = sb("ret_kb", [NS, 2, DK], where=ret)
        att = sb("ret_att", [P, 1280], where=ret)
        atts = sb("ret_atts", [NS, NS], where=ret)
        gate = sb("ret_gate", [P, 4, NT], where=ret)
        oT = sb("ret_o", [P, 4, NT], where=ret)
        og_hi = sb("ret_og_hi", [P, 4, NT], F32R, where=ret)
        og_lo = sb("ret_og_lo", [P, 4, NT], F32R, where=ret)
        st = sb("ret_state", [P, 2, 2, DV], where=ret)
        ret.close()

        ff = ExitStack()
        hid_hi = sb("hid_hi", [P, FFT, NT], F32R, where=ff)
        hid_lo = sb("hid_lo", [P, FFT, NT], F32R, where=ff)
        hid = sb("hid", [P, 2, NT], where=ff)
        sig = sb("sig", [P, 2, NT], where=ff)
        ff.close()

        fx = ExitStack()
        fkT = sb("fox_kT", [P, NPAIR, NT], where=fx)
        fqT = sb("fox_qT", [P, NPAIR, NT], where=fx)
        fv = sb("fox_v", [P, RT, D], where=fx)
        fvs = sb("fox_vs", [NS, D], where=fx)
        lf = sb("fox_logf", [FH, NT], where=fx)
        negF = sb("fox_negF", [FH, NT], where=fx)
        nFs = sb("fox_nFs", [NS, FH], where=fx)
        Rb = sb("fox_R", [P, DEC_B, NPG, FH], where=fx)
        cmb = sb("fox_cmb", [P, P], BF16, where=fx)
        idb = sb("fox_idb", [P, P], BF16, where=fx)
        fxe = ExitStack()
        lfa = sb("fox_lfa", [FH, 4, NT], where=fxe)
        fraw = sb("fox_raw", [P, 2, NT], where=fxe)
        plf = sb("fox_plf", [P, DEC_B, NPG, FH], where=fxe)
        suf = sb("fox_suf", [P, DEC_B, NPG, FH], where=fxe)
        fxe.close()
        fxp = ExitStack()
        bias = sb("fox_bias", [P, 2, SEQ], where=fxp)
        pr = sb("fox_p", [P, 4, SEQ], where=fxp)
        pT = sb("fox_pT", [P, RT, SEQ], where=fxp)
        mx = sb("fox_mx", [P, 64], where=fxp)
        nmx = sb("fox_nmx", [P, 64], where=fxp)
        rs = sb("fox_rs", [P, 64], where=fxp)
        rsi = sb("fox_rsi", [P, 64], where=fxp)
        fxp.close()
        fxs = ExitStack()
        kpg = sb("fox_kpg", [P, PRING, D], where=fxs)
        vpg = sb("fox_vpg", [P, PRING, D], where=fxs)
        ssb = sb("fox_ssb", [P, 2, NPG, 64], where=fxs)
        sn = sb("fox_sn", [NS, DEC_B, NPAIR, 2, DEC_T], where=fxs)
        qbd = sb("fox_qbd", [P, NPAIR, DEC_B, 2 * DEC_T], where=fxs)
        m1 = sb("fox_m1", [P, 64], where=fxs)
        m2 = sb("fox_m2", [64, 1], where=fxs)
        dg = sb("fox_dg", [64, 64], where=fxs)
        li = sb("fox_li", [P, 64], where=fxs)
        fxs.close()
        fx.close()

        foT = fqT

        S = {}
        for n in """x_in cst_in rc_in dec_in0 dec_in1 c_in tab_in m_used m_psum m_done c_exp c_ready hi_split w_split w_tiles
                 sq_ready ms_ready var_ready ln_done r_exp r_ready scaled hmod hsample hi_ready h_ready x_done gains
                 dve_chain rope_done v_evac v_tr tr_ready tr_evac scores_ready decayed
                 o_ready o_evac os_ready os_evac upd_ready kb_ready upd_done st_saved0 st_saved1 st_in0 st_in1 sp_ready sp_evac sp_saved
                 osq_ready osq_used gated og_hi_ready og_ready silu_exp silu_done
                 hid_full hid_hi_ready hid_ready
                 fk_raw fk_sq fk_done fv_raw fv_saved0 fv_saved1 fvt_ready fvt_evac lf_raw lf_exp lf_done
                 nF_ready nFs_ready nFs_psum plf_in suf_ready R_psum R_done
                 bias_psum bias_ready s_psum s_max p_exp p_done pT_psum pT_ready fo_psum fo_done idb_ready
                 fo_hi_ready fo_ready
                 k_in0 k_in1 k_in2 k_in3 v_in0 v_in1 v_in2 v_in3 qbd_ready kpg_used vpg_used sn_psum sn_done ss_psum ss_done m1_ready m1_psum dg_ready mb_psum
                 ssub ss_exp l_psum so_psum so_done y_out k_out lf_out pair_free0 pair_free1 raw_in0 raw_in1 raw_in2 raw_in3 m_in0 m_in1 m_in2 m_in3""".split():
            S[n] = sem(n)
        block = ctx.enter_context(nc.Block())

        def two(ap):
            return ap.rearrange("p (h n) -> p h n", h=2)

        W_RET = RH * 16
        W_FF0 = W_RET
        W_KV = W_FF0 + 66
        W_Q = W_KV + 17
        W_O = W_Q + 8
        W_FF1 = W_O + 8
        W_ALL = W_FF1 + 66

        def ret_proj_slab(h):
            return 0 if h == 0 else 16 * h - 4

        def ret_out_slab(h):
            return 16 * h + 24 if h < RH - 1 else 16 * h + 12

        def ff_slab(layer, half):
            return (W_FF0 if layer == 0 else W_FF1) + 33 * half

        def ret_proj_tile(h):
            return 0 if h == 0 else 20 * h - 8

        def ret_out_tile(h):
            return 20 * h + 24 if h < RH - 1 else 20 * h + 12

        T_FF0 = RH * 20
        FFN_T = 2 * FFT + DT
        T_KV = T_FF0 + 2 * FFN_T
        T_Q = T_KV + 17
        T_O = T_Q + 8
        T_FF1 = T_O + 8

        def ff_done_tiles(u):
            return (ff_slab(u // 2, u % 2) + 33) * SLAB

        def tiles_after_out(h):
            return (ret_out_slab(h) + 4) * SLAB

        def ff_tile(layer, half):
            return (T_FF0 if layer == 0 else T_FF1) + FFN_T * half

        def pair_free(n):
            return S[f"pair_free{n % 2}"]

        def states_saved(eng):
            eng.wait_ge(S["st_saved0"], 16 * RH * DEC_B // 2)
            eng.wait_ge(S["st_saved1"], 16 * RH * DEC_B // 2)

        def keys_saved(eng):
            eng.wait_ge(S["k_out"], 16)
            eng.wait_ge(S["lf_out"], 16)

        def wait_tile(eng, tiles):
            eng.wait_ge(S["w_tiles"], tiles)

        def page(sp, what, n):
            ring = kpg if what == "k" else vpg
            if n >= PRING:
                sp.wait_ge(S[f"{what}pg_used"], n - PRING + 1)
            pg = nc.sync.value_load(tabs[0:1, n:n + 1], min_val=0, max_val=A["lf"].shape[0] - 1)
            sp.dma_start(ring[:, n % PRING, :].unsqueeze(1), A[what + "c"][bass.ds(pg, 1)].rearrange("a p n -> p a n"))\
                .then_inc(S[f"{what}_in{n % PRING}"], 16)

        @block.sync
        def _(sp):
            slab = [0]
            mslab = [0]

            def weights(n):
                for _ in range(n):
                    s = slab[0]
                    if s >= RAW:
                        sp.wait_ge(S["w_split"], s - RAW + 1)
                    sp.dma_start(raw[:, s % RAW, :], A["w"][s]).then_inc(S[f"raw_in{s % RAW}"], 16)
                    slab[0] += 1

            def mods(n):
                for _ in range(n):
                    m = mslab[0]
                    if m >= MRING:
                        sp.wait_ge(S["m_used"], m - MRING + 1)
                    sp.dma_start(mraw[:, m % MRING, :], A["wm"][m]).then_inc(S[f"m_in{m % MRING}"], 16)
                    mslab[0] += 1

            def states(h):
                for b in range(DEC_B):
                    n = h * DEC_B + b
                    if n >= 2:
                        sp.wait_ge(S[f"st_saved{n % 2}"], 16 * (n // 2))
                    sp.dma_start(st[:, n % 2], A["state"][h, b]).then_inc(S[f"st_in{n % 2}"], 16)
                    if b >= 1:
                        save_state(n - 1)
                save_state(h * DEC_B + DEC_B - 1)

            def save_state(n):
                sp.wait_ge(S["upd_done"], 2 * n + 2)
                sp.dma_start(A["st_s"][n // DEC_B, n % DEC_B], st[:, n % 2]).then_inc(S[f"st_saved{n % 2}"], 16)

            sp.dma_start(cact[:], A["cT"]).then_inc(S["c_in"], 16)
            sp.dma_start(vec[:], A["vec"]).then_inc(S["cst_in"], 16)
            sp.dma_start(cst[:], A["cst"]).then_inc(S["cst_in"], 16)
            sp.dma_start(x[:], A["xT"]).then_inc(S["x_in"], 16)
            sp.dma_start(tabs[:], A["table"]).then_inc(S["tab_in"], 16)
            mods(MOD_FIRST)
            sp.dma_start(rc[:], A["rc"]).then_inc(S["rc_in"], 16)
            weights(12)
            for h in range(RH):
                last = h == RH - 1
                if h >= 2:
                    sp.wait_ge(S["decayed"], 5 * (h - 1))
                sp.dma_start(dec[:, h % 2, :], A["dec"][h]).then_inc(S[f"dec_in{h % 2}"], 16)
                if not last:
                    weights(4)
                states(h)
                if not last:
                    weights(4)
                for _ in range(4):
                    if not last:
                        weights(1)
                    mods(2)
                for _ in range(4):
                    weights(1)
                    mods(4)
            weights(66 + 17 + 8)
            sp.wait_ge(S["tab_in"], 16)
            sp.wait_ge(S["h_ready"], DT * 3)
            with nc.sync.Fori(0, DEC_B) as b:
                for g in range(NPG):
                    pg = nc.sync.value_load(tabs[0:1, bass.ds(b * NPG + g, 1)], min_val=0, max_val=A["lf"].shape[0] - 1)
                    sp.dma_start(plf[:, bass.ds(b, 1), g, :], A["lf"][bass.ds(pg, 1)].rearrange("a p h -> p a h")).then_inc(S["plf_in"], 16)
            sp.wait_ge(S["fo_done"], FH)
            for n in range(NPG):
                page(sp, "k", n)
            for n in range(DEC_B * NPG):
                if n + NPG < DEC_B * NPG:
                    page(sp, "k", n + NPG)
                page(sp, "v", n)
            sp.dma_start(A["o_k"], fkT[:]).then_inc(S["k_out"], 16)
            sp.dma_start(A["o_lf"], lf[:]).then_inc(S["lf_out"], 16)
            weights(8)
            weights(66)
            sp.wait_ge(S["x_done"], 8 * (RH + 2 + 1 + 2))
            sp.dma_start(A["o_x"], x[:]).then_inc(S["y_out"], 16)
            sp.wait_ge(S["y_out"], 16)
            sp.wait_ge(S["k_out"], 16)
            sp.wait_ge(S["lf_out"], 16)
            sp.wait_ge(S["st_saved0"], 16 * RH * DEC_B // 2)
            sp.wait_ge(S["st_saved1"], 16 * RH * DEC_B // 2)
            sp.wait_ge(S["sp_saved"], 16 * 2 * RH)
            sp.wait_ge(S["fv_saved0"], 16 * NPAIR // 2)
            sp.wait_ge(S["fv_saved1"], 16 * NPAIR // 2)

        @block.gpsimd
        def _(g):
            nc.gpsimd.memset(ones[:], 1.0).then_inc(S["hi_split"], 1)
            g.wait_ge(S["hi_split"], 1)
            unit = ones[:, 0:1].to_broadcast([P, SLAB * P])

            def split(s, slot, ring, uses):
                g.wait_ge(S[f"raw_in{ring}"], 16 * uses)
                nc.gpsimd.tensor_tensor(w_hi[:, slot, :], raw[:, ring, :], unit, ALU.mult).then_inc(S["hi_split"], 1)
                g.wait_ge(S["hi_split"], s + 2)
                nc.gpsimd.tensor_tensor(w_lo[:, slot, :], raw[:, ring, :], w_hi[:, slot, :].bitcast(F32),
                                        ALU.subtract).then_inc(S["w_split"], 1)

            for s in range(RAW):
                if s >= SPL:
                    g.wait_ge(S["w_tiles"], SLAB * (s - SPL + 1))
                split(s, s % SPL, s, 1)
            with nc.gpsimd.Fori(1, W_ALL // RAW) as i:
                for r in range(RAW):
                    g.wait_ge(S["w_tiles"], (i * RAW + r - SPL + 1) * SLAB)
                    split(i * RAW + r, r % SPL, r, i + 1)
            for s in range(W_ALL // RAW * RAW, W_ALL):
                g.wait_ge(S["w_tiles"], SLAB * (s - SPL + 1))
                split(s, s % SPL, s % RAW, s // RAW + 1)

        @block.tensor
        def _(pe):
            mm = nc.tensor.matmul
            tiles = [0]
            tile_no = [0]
            chain = [0]
            msq = [0]

            def project(n, ktiles, hi, lo):
                for _ in range(n):
                    f = tile_no[0]
                    if f >= 2:
                        pe.wait_ge(pair_free(f), f // 2)
                    for k in range(ktiles):
                        t = tiles[0]
                        s = t // SLAB
                        if k == 0 or t % SLAB == 0:
                            pe.wait_ge(S["w_split"], s + 1)
                        c = (t % SLAB) * P
                        for half in range(2):
                            cols = slice(half * HALF, (half + 1) * HALF)
                            for i, (w, a) in enumerate(((w_lo, hi), (w_hi, lo), (w_hi, hi))):
                                last = mm(pj[f % 2][:, half, 0:HALF], w[:, s % SPL, c:c + P], a(k)[:, cols],
                                          start=k == 0 and i == 0, stop=k == ktiles - 1 and i == 2)
                        tiles[0] += 1
                        last.then_inc(S["w_tiles"], 1)
                    tile_no[0] += 1

            def from_h(n):
                project(n, DT, lambda k: h_hi[:, k, :], lambda k: h_lo[:, k, :])

            def modulation(first, n, bank, at=0):
                for m in range(first, first + n):
                    pe.wait_ge(S[f"m_in{m % MRING}"], 16 * (m // MRING + 1))
                    for k in range(DT):
                        last = mm(bank[:, (m - first + at) * NC:(m - first + at + 1) * NC], mraw[:, m % MRING, k * P:(k + 1) * P],
                                  cact[:, k, :], start=k == 0, stop=k == DT - 1)
                    last.then_inc(S["m_used"], 1)

            def sum_squares(src, n, wait_each, lhs=None):
                for k in range(n):
                    wait_each(k)
                    for half in range(2):
                        last = mm(bk[half][:, 0:HALF], lhs if lhs is not None else ones[:], src(k)[:, half * HALF:(half + 1) * HALF],
                                  start=k == 0, stop=k == n - 1)
                    if k < n - 1:
                        last.then_inc(S["osq_used"], 1)
                last.then_inc(S["ms_ready"], 1)

            def norm(z):
                def w(k):
                    pe.wait_ge(S["sq_ready"], z * DT + k + 1)
                sum_squares(lambda k: xs[:, k % 2, :], DT, w)
                pe.wait_ge(S["h_ready"], DT * (z + 1))

            pe.wait_ge(S["cst_in"], 32)
            pe.wait_ge(S["hi_split"], 1)
            pe.wait_ge(S["c_ready"], 1)
            modulation(0, MOD_FIRST, bk[3])
            norm(0)
            from_h(12)

            for h in range(RH):
                last_head = h == RH - 1
                pe.wait_ge(S["v_evac"], h + 1)
                pe.wait_ge(S["rope_done"], 2 * h + 2)
                if h:
                    pe.wait_ge(S["sp_evac"], 2 * h)
                    pe.wait_ge(S["os_evac"], h)
                    pe.wait_ge(S["m_done"], 2 * h + 1)
                    pe.wait_ge(S["og_ready"], 4 * h)
                    pe.wait_ge(S["upd_done"], 16 * h)
                for e in range(8):
                    if e >= 4:
                        pe.wait_ge(S["tr_evac"], 8 * h + e - 3)
                    if e < 4:
                        for f in range(4):
                            last = nc.tensor.transpose(bk[e][:, f * P:(f + 1) * P], vT[:, f, e * P:(e + 1) * P], ident)
                    elif e == 4:
                        for f in range(4):
                            last = nc.tensor.transpose(bk[0][0:NS, f * P:(f + 1) * P], vT[:, f, SEQ:NT], ident)
                    elif e < 7:
                        for r in range(2):
                            rt = 2 * (e - 5) + r
                            for d in range(2):
                                c = r * DK + d * P
                                last = nc.tensor.transpose(bk[e - 4][:, c:c + P], kT[:, d, rt * P:(rt + 1) * P], ident)
                    else:
                        for d in range(2):
                            last = nc.tensor.transpose(bk[3][0:NS, d * P:(d + 1) * P], kT[:, d, SEQ:NT], ident)
                    last.then_inc(S["tr_ready"], 1)
                for j in range(RT):
                    pe.wait_ge(S["tr_evac"], 8 * h + 5 + j)
                    n = SEQ - j * P
                    for d in range(2):
                        last = mm(bk[j][:, 0:n], kT[:, d, j * P:(j + 1) * P], qT[:, d, j * P:SEQ], start=d == 0, stop=d == 1)
                    if j == RT - 1:
                        for d in range(2):
                            last = mm(bk[3][0:NS, P:P + NS], kT[:, d, SEQ:NT], qT[:, d, SEQ:NT], start=d == 0, stop=d == 1)
                    last.then_inc(S["scores_ready"], 1)
                if not last_head:
                    from_h(4)
                pe.wait_ge(S["decayed"], 5 * h + 5)
                for e in range(4):
                    at = 0
                    for j in range(RT):
                        n = SEQ - j * P
                        last = mm(bk[e][:, j * P:SEQ], vtok[:, j, e * P:(e + 1) * P], att[:, at:at + n], start=j == 0, stop=j == RT - 1)
                        at += n
                    last.then_inc(S["o_ready"], 1)
                pe.wait_ge(S["o_evac"], 4 * h + 4)
                for e in range(4):
                    mm(bk[0][:, e * NS:(e + 1) * NS], vs[:, e * P:(e + 1) * P], atts[:], start=e == 0, stop=False, skip_group_check=True)
                for b in range(DEC_B):
                    n = h * DEC_B + b
                    pe.wait_ge(S[f"st_in{n % 2}"], 16 * (n // 2 + 1))
                    for e in range(4):
                        for d in range(2):
                            last = mm(bk[0][:, e * NS + b * DEC_T:e * NS + (b + 1) * DEC_T], st[:, n % 2, d, e * P:(e + 1) * P],
                                      qx[:, d, b * DEC_T:(b + 1) * DEC_T], start=False, stop=b == DEC_B - 1 and d == 1, skip_group_check=True)
                    if b == DEC_B - 1:
                        last.then_inc(S["os_ready"], 1)
                    pe.wait_ge(S["kb_ready"], n + 1)
                    for d in range(2):
                        if b:
                            pe.wait_ge(S["upd_done"], 2 * n + d - 1)
                        mm(bk[1 + d][:], kb[:, b % 2, d * P:(d + 1) * P], vs[:], start=True, stop=True).then_inc(S["upd_ready"], 1)
                for d in range(2):
                    if d:
                        pe.wait_ge(S["sp_evac"], 2 * h + 1)
                    for rt in range(RT):
                        last = mm(bk[3][:], ktok[:, rt, d * P:(d + 1) * P], vtok[:, rt, :], start=rt == 0, stop=rt == RT - 1)
                    last.then_inc(S["sp_ready"], 1)
                if not last_head:
                    from_h(4)
                pe.wait_ge(S["os_evac"], h + 1)
                pe.wait_ge(S["upd_done"], 16 * h + 16)

                def w(k):
                    pe.wait_ge(S["osq_ready"], 4 * h + k + 1)
                sum_squares(lambda k: xs[:, k % 2, :], 4, w)
                pe.wait_ge(S["sp_evac"], 2 * h + 2)
                m = MOD_FIRST + h * MOD_PER_HEAD
                pe.wait_ge(S["m_done"], 2 * h + 1)
                for i in range(4):
                    if not last_head:
                        from_h(1)
                    modulation(m + 2 * i, 2, bk[3], 2 * i)
                pe.wait_ge(S["og_ready"], 4 * h + 4)
                for i in range(4):
                    project(2, 4, lambda k: og_hi[:, k, :], lambda k: og_lo[:, k, :])
                    modulation(m + DT + 4 * i, 4, bk[2], 4 * i)

            def feed_forward(layer):
                for half in range(2):
                    u = 2 * layer + half
                    from_h(2 * FFT)
                    pe.wait_ge(S["hid_ready"], FFT * (u + 1))
                    project(DT, FFT, lambda k: hid_hi[:, k, :], lambda k: hid_lo[:, k, :])

            norm(1)
            feed_forward(0)

            BD = cst[:, C_BD:C_BD + P]
            norm(2)

            def head_norm(k):
                pe.wait_ge(S["fk_sq"], k + 1)
                for half in range(2):
                    last = mm(bk[half][:, 0:HALF], BD, xs[:, k % 2, half * HALF:(half + 1) * HALF], start=True, stop=True)
                last.then_inc(S["ms_ready"], 1)

            for p in range(NPAIR):
                from_h(1)
                if p:
                    pe.wait_ge(S["var_ready"], 3 + RH + p - 1)
                    head_norm(p - 1)
            pe.wait_ge(S["var_ready"], 3 + RH + NPAIR - 1)
            head_norm(NPAIR - 1)

            def v_rows(p):
                pe.wait_ge(S["fv_raw"], p + 1)
                if p:
                    pe.wait_ge(S["fvt_evac"], p)
                for rt in range(RT):
                    nc.tensor.transpose(bk[2][:, rt * P:(rt + 1) * P], fraw[:, p % 2, rt * P:(rt + 1) * P], ident)
                nc.tensor.transpose(bk[3][0:NS, 0:P], fraw[:, p % 2, SEQ:NT], ident).then_inc(S["fvt_ready"], 1)

            for p in range(NPAIR):
                from_h(1)
                if p:
                    v_rows(p - 1)
            from_h(1)
            v_rows(NPAIR - 1)

            norm(3)
            for p in range(NPAIR):
                from_h(1)
                if p:
                    pe.wait_ge(S["var_ready"], 4 + RH + NPAIR + p - 1)
                    head_norm(NPAIR + p - 1)
            pe.wait_ge(S["var_ready"], 4 + RH + 2 * NPAIR - 1)
            head_norm(2 * NPAIR - 1)

            pe.wait_ge(S["suf_ready"], 1)
            pe.wait_ge(S["fvt_evac"], NPAIR)
            half_b = DEC_B // 2
            for i in range(2):
                o = bk[2 + i][:].rearrange("p (b g h) -> p b g h", b=half_b, g=NPG)
                mm(o, cst[:, C_US:C_US + P], plf[:, i * half_b:(i + 1) * half_b], start=True, stop=False)
                mm(o, ones[:], suf[:, i * half_b:(i + 1) * half_b], start=False, stop=True).then_inc(S["R_psum"], 1)
            pe.wait_ge(S["R_done"], 2)
            pe.wait_ge(S["nF_ready"], 1)
            nc.tensor.transpose(bk[2][0:NS, 0:FH], negF[:, SEQ:NT], cst[0:FH, C_ID:C_ID + FH]).then_inc(S["nFs_psum"], 1)

            s_bank = [pj[0][:, 0, :], pj[0][:, 1, :]]
            o_bank = pj[1][:, 0, :]
            b_bank = pj[1][:, 1, :]
            pe.wait_ge(S["fk_done"], 2 * NPAIR)
            pe.wait_ge(S["idb_ready"], 2)
            pe.wait_ge(S["nFs_ready"], 1)
            pe.wait_ge(S["lf_done"], 1)

            def bias_row(h):
                if h:
                    pe.wait_ge(S["bias_ready"], h)
                mm(b_bank, cst[0:FH, C_ID + h:C_ID + h + 1].to_broadcast([FH, P]), negF[:, 0:SEQ], start=True, stop=True).then_inc(S["bias_psum"], 1)

            def score(h, qb):
                t = 4 * h + qb
                r = (h % 2) * HD
                if t >= 2:
                    pe.wait_ge(S["s_max"], t - 1)
                n = (qb + 1) * P
                mm(s_bank[t % 2][:, 0:n], fqT[r:r + HD, h // 2, qb * P:n], fkT[r:r + HD, h // 2, 0:n], start=True, stop=False)
                mm(s_bank[t % 2][:, qb * P:n], idb[:], cmb[:], start=False, stop=True).then_inc(S["s_psum"], 1)

            def turn(h, qb):
                t = 4 * h + qb
                pe.wait_ge(S["p_done"], t + 1)
                if qb == 0 and h:
                    pe.wait_ge(S["pT_ready"], 4 * h)
                for k in range(qb + 1):
                    last = nc.tensor.transpose(bk[k][:, qb * P:(qb + 1) * P], pr[:, t % 4, k * P:(k + 1) * P], ident)
                last.then_inc(S["pT_psum"], 1)

            def weigh(h):
                r = (h % 2) * HD
                if h:
                    pe.wait_ge(S["fo_done"], h)
                for k in range(RT):
                    pe.wait_ge(S["pT_ready"], 4 * h + k + 1)
                    last = mm(o_bank[r:r + HD, k * P:SEQ], fv[:, k, h * HD:(h + 1) * HD], pT[:, k, k * P:SEQ], start=k == 0, stop=k == RT - 1)
                last.then_inc(S["fo_psum"], 1)

            for h in range(FH + 1):
                if h < FH:
                    bias_row(h)
                for qb in range(RT):
                    if h < FH:
                        score(h, qb)
                    t = 4 * h + qb - 2
                    if 0 <= t < 4 * FH:
                        turn(t // 4, t % 4)
                    if qb == 3 and h:
                        weigh(h - 1)

            pe.wait_ge(S["fo_done"], FH)
            pe.wait_ge(S["qbd_ready"], 2 * NPAIR + 1)
            for p in range(NPAIR):
                last = mm(bk[0][0:NS, p * 64:(p + 1) * 64], fkT[:, p, SEQ:NT], qbd[:, p], start=True, stop=True)
            last.then_inc(S["sn_psum"], 1)
            pe.wait_ge(S["sn_done"], 2 * DEC_B)

            def past_scores(b, g):
                n = b * NPG + g
                if b >= 2 and g == 0:
                    pe.wait_ge(S["ss_done"], b - 1)
                pe.wait_ge(S[f"k_in{n % PRING}"], 16 * (n // PRING + 1))
                for p in range(NPAIR):
                    c = g * 64 + p * 8
                    last = mm(bk[b % 2][:, c:c + 8], kpg[:, n % PRING, p * P:(p + 1) * P], qbd[:, p, b, :], start=True, stop=True)
                last.then_inc(S["kpg_used"], 1)

            def stats(b):
                pe.wait_ge(S["m1_ready"], b + 1)
                nc.tensor.transpose(bk[2][0:64, 0:P], m1[:], ident).then_inc(S["m1_psum"], 1)
                pe.wait_ge(S["dg_ready"], b + 1)
                mm(bk[2][:, 0:64], ones[0:64, :], dg[:], start=True, stop=True).then_inc(S["mb_psum"], 1)

            def sums(b):
                pe.wait_ge(S["ss_exp"], 2 * b + 2)
                if b:
                    pe.wait_ge(S["so_done"], 2 * b)
                for g in range(NPG):
                    mm(bk[3][:, 0:64], ones[:], ssb[:, b % 2, g, :], start=g == 0, stop=False)
                mm(bk[3][:, 0:64], ones[0:NS, :], sn[:, b], start=False, stop=True).then_inc(S["l_psum"], 1)

            def past_values(b, g):
                n = b * NPG + g
                pe.wait_ge(S[f"v_in{n % PRING}"], 16 * (n // PRING + 1))
                for p in range(NPAIR):
                    last = mm(bk[3][:, 64 + p * 8:72 + p * 8], vpg[:, n % PRING, p * P:(p + 1) * P], ssb[:, b % 2, g, p * 8:p * 8 + 8],
                              start=g == 0 and p == 0, stop=False, skip_group_check=True)
                last.then_inc(S["vpg_used"], 1)

            def new_values(b):
                for p in range(NPAIR):
                    last = mm(bk[3][:, 64 + p * 8:72 + p * 8], fvs[:, p * P:(p + 1) * P], sn[:, b, p],
                              start=False, stop=True, skip_group_check=True)
                last.then_inc(S["so_psum"], 1)

            for g in range(NPG):
                past_scores(0, g)
            for b in range(DEC_B):
                stats(b)
                sums(b)
                for g in range(NPG):
                    if b + 1 < DEC_B:
                        past_scores(b + 1, g)
                    past_values(b, g)
                new_values(b)

            pe.wait_ge(S["fo_ready"], NPAIR)
            from_h(NPAIR)
            norm(4)
            feed_forward(1)

        @block.scalar
        def _(act):
            chain = [0]

            def fn(out, in_, f, **kw):
                return nc.scalar.activation(out, in_, f, **kw)

            def root():
                c = chain[0]
                act.wait_ge(S["var_ready"], c + 1)
                fn(rstd[:], var[:], ACT.Ln).then_inc(S["ln_done"], 1)
                act.wait_ge(S["ln_done"], c + 1)
                fn(rstd[:], rstd[:], ACT.Exp, scale=-0.5).then_inc(S["r_exp"], 1)
                chain[0] += 1

            def norm(z, shift):
                for k in range(DT):
                    if z:
                        act.wait_ge(S["x_done"], x_done_before[z] + k + 1)
                    else:
                        act.wait_ge(S["x_in"], 16)
                    if k >= 2:
                        act.wait_ge(S["osq_used"], osq_before[z] + k - 1)
                    elif z:
                        act.wait_ge(S["ms_ready"], chain[0])
                    fn(xs[:, k % 2, :], x[:, k, :], ACT.Square).then_inc(S["sq_ready"], 1)
                root()
                act.wait_ge(S["gains"], z + 1)
                for k in range(DT):
                    act.wait_ge(S["scaled"], z * DT + k + 1)
                    if z * DT + k >= 2:
                        act.wait_ge(S["h_ready"], z * DT + k - 1)
                    fn(hf[:, k % 2, 0:SEQ], xs[:, k % 2, 0:SEQ], ACT.Identity, scale=gain[:, k, 0:1],
                       bias=mod[:, shift + k, 0:1]).then_inc(S["hmod"], 1)
                    act.wait_ge(S["hmod"], z * DT + k + 1)
                    act.wait_ge(S["hsample"], z * DT + k + 1)
                    fn(h_hi[:, k, :], hf[:, k % 2, :], ACT.Copy).then_inc(S["hi_ready"], 1)

            x_done_before = [0, 8 * RH - 8, 8 * (RH + 2) - 8, 8 * (RH + 2) - 8, 8 * (RH + 3) - 8]
            osq_before = [0, 7 + 3 * RH, 14 + 3 * RH, 21 + 3 * RH, 28 + 3 * RH]

            def free(n, ins):
                ins.then_inc(pair_free(n), 1)

            act.wait_ge(S["c_in"], 16)
            fn(ctmp[:], cact[:], ACT.Exp, scale=-1.0).then_inc(S["c_exp"], 1)
            norm(0, 0)

            def values_out(h):
                for f in range(4):
                    wait_tile(act, ret_proj_slab(h) * SLAB + (5 + f) * SLAB)
                    if h and f == 0:
                        act.wait_ge(S["tr_ready"], 8 * h)
                    free(ret_proj_tile(h) + 4 + f, fn(two(vT[:, f, :]), pj[f % 2][:, :, 0:HALF], ACT.Copy))
                act.wait_ge(pair_free(0), (ret_proj_tile(h) + 6) // 2 + 1)
                act.wait_ge(pair_free(1), (ret_proj_tile(h) + 7) // 2 + 1)
                act.sem_inc(S["v_evac"], 1)

            def gates(h):
                for f in range(4):
                    n = 4 * h + f
                    wait_tile(act, ret_proj_slab(h) * SLAB + (9 + f) * SLAB)
                    if n >= 2:
                        act.wait_ge(S["silu_done"], n - 1)
                    fn(two(hf[:, f % 2, :]), pj[f % 2][:, :, 0:HALF], ACT.Exp, scale=-1.0).then_inc(S["silu_exp"], 1)

            act.wait_ge(S["h_ready"], DT)
            values_out(0)
            gates(0)
            act.wait_ge(S["rc_in"], 16)
            for h in range(RH):
                last_head = h == RH - 1
                for e in range(8):
                    act.wait_ge(S["tr_ready"], 8 * h + e + 1)
                    if e < 4:
                        last = fn(vtok[:, e, :], bk[e][:], ACT.Copy)
                    elif e == 4:
                        last = fn(vs[:], bk[0][0:NS, :], ACT.Copy)
                    elif e < 7:
                        for r in range(2):
                            rt = 2 * (e - 5) + r
                            last = fn(ktok[:, rt, :], bk[e - 4][:, r * DK:(r + 1) * DK], ACT.Copy,
                                      scale=rc[:, R_KP + h * RT + rt:R_KP + h * RT + rt + 1])
                    else:
                        last = fn(ks[:], bk[3][0:NS, 0:DK], ACT.Copy)
                    last.then_inc(S["tr_evac"], 1)
                for e in range(4):
                    act.wait_ge(S["o_ready"], 4 * h + e + 1)
                    if h and e == 0:
                        act.wait_ge(S["og_ready"], 4 * h)
                    fn(oT[:, e, 0:SEQ], bk[e][:], ACT.Copy).then_inc(S["o_evac"], 1)
                act.wait_ge(S["os_ready"], h + 1)
                fn(oT[:, :, SEQ:NT], bk[0][:, 0:4 * NS].rearrange("p (e n) -> p e n", e=4), ACT.Copy).then_inc(S["os_evac"], 1)
                act.wait_ge(S["silu_done"], 4 * h + 4)
                for d in range(2):
                    n = 2 * h + d
                    act.wait_ge(S["sp_ready"], n + 1)
                    if n:
                        act.wait_ge(S["sp_saved"], 16 * n)
                    fn(hf[:, 0, 0:DV], bk[3][:], ACT.Copy).then_inc(S["sp_evac"], 1)
                    act.wait_ge(S["sp_evac"], n + 1)
                    act.dma_start(A["st_p"][h, :, d, :], hf[:, 0, 0:DV]).then_inc(S["sp_saved"], 16)
                if not last_head:
                    values_out(h + 1)
                act.wait_ge(S["os_evac"], h + 1)
                for e in range(4):
                    if e >= 2:
                        act.wait_ge(S["osq_used"], 7 + 3 * h + e - 1)
                    elif True:
                        act.wait_ge(S["ms_ready"], chain[0])
                    fn(xs[:, e % 2, :], oT[:, e, :], ACT.Square).then_inc(S["osq_ready"], 1)
                root()
                for e in range(4):
                    act.wait_ge(S["gated"], 4 * h + e + 1)
                    if h and e == 0:
                        wait_tile(act, tiles_after_out(h - 1))
                    fn(og_hi[:, e, :], oT[:, e, :], ACT.Copy).then_inc(S["og_hi_ready"], 1)
                if not last_head:
                    act.wait_ge(S["sp_saved"], 16 * 2 * (h + 1))
                    gates(h + 1)

            act.wait_ge(S["sp_saved"], 16 * 2 * RH)
            states_saved(act)

            def feed_forward(layer):
                for half in range(2):
                    u = 2 * layer + half
                    base = ff_slab(layer, half) * SLAB
                    for m in range(FFT):
                        n = u * FFT + m
                        wait_tile(act, base + (2 * m + 1) * SLAB)
                        if n >= 2:
                            act.wait_ge(S["hid_full"], n - 1)
                        fn(two(sig[:, n % 2, :]), pj[(ff_tile(layer, half) + 2 * m) % 2][:, :, 0:HALF], ACT.Exp, scale=-1.0)\
                            .then_inc(S["silu_exp"], 1)
                        if m:
                            hidden_hi(n - 1, m - 1, u)
                    hidden_hi(u * FFT + FFT - 1, FFT - 1, u)

            def hidden_hi(n, m, u):
                act.wait_ge(S["hid_full"], n + 1)
                if m == 0 and u:
                    wait_tile(act, ff_done_tiles(u - 1))
                fn(hid_hi[:, m, :], hid[:, n % 2, :], ACT.Copy).then_inc(S["hid_hi_ready"], 1)

            norm(1, 3 * DT)
            feed_forward(0)
            norm(2, 12 * DT)

            def head_tile(k, tile, slab):
                wait_tile(act, (slab + 1) * SLAB)
                if k >= 2:
                    act.wait_ge(S["fk_done"], k - 1)
                fn(two(fraw[:, k % 2, :]), pj[tile % 2][:, :, 0:HALF], ACT.Copy).then_inc(S["fk_raw"], 1)
                if k % NPAIR < 2:
                    act.wait_ge(S["h_ready"], DT * (3 if k < NPAIR else 4))
                if k % NPAIR:
                    act.wait_ge(S["ms_ready"], chain_at_head(k))
                free(tile, fn(two(xs[:, k % 2, :]), pj[tile % 2][:, :, 0:HALF], ACT.Square))
                act.wait_ge(pair_free(tile), tile // 2 + 1)
                act.sem_inc(S["fk_sq"], 1)

            def chain_at_head(k):
                first = 3 + RH if k < NPAIR else 4 + RH + NPAIR
                return first + max(k % NPAIR - 1, 0)

            for p in range(NPAIR):
                head_tile(p, T_KV + p, W_KV + p)
                if p:
                    root()
            root()
            def rows_out(p):
                act.wait_ge(S["fvt_ready"], p + 1)
                fn(fv[:, :, p * P:(p + 1) * P], bk[2][:].rearrange("p (r c) -> p r c", r=RT), ACT.Copy)
                fn(fvs[:, p * P:(p + 1) * P], bk[3][0:NS, 0:P], ACT.Copy).then_inc(S["fvt_evac"], 1)

            for p in range(NPAIR):
                tile = T_KV + NPAIR + p
                wait_tile(act, (W_KV + NPAIR + p + 1) * SLAB)
                if p < 2:
                    act.wait_ge(S["fk_done"], NPAIR)
                else:
                    act.wait_ge(S["fvt_ready"], p - 1)
                    act.wait_ge(S[f"fv_saved{p % 2}"], 16 * (p // 2))
                free(tile, fn(two(fraw[:, p % 2, :]), pj[tile % 2][:, :, 0:HALF], ACT.Copy))
                act.wait_ge(pair_free(tile), tile // 2 + 1)
                act.sem_inc(S["fv_raw"], 1)
                act.dma_start(A["o_v"][:, p, :], fraw[:, p % 2, :]).then_inc(S[f"fv_saved{p % 2}"], 16)
                if p:
                    rows_out(p - 1)
            rows_out(NPAIR - 1)
            act.wait_ge(S["lf_raw"], 1)
            fn(lfa[:, 1, :], lfa[:, 1, :], ACT.Exp, scale=-1.0).then_inc(S["lf_exp"], 1)
            act.wait_ge(S["fv_saved0"], 16 * (NPAIR // 2))
            act.wait_ge(S["fv_saved1"], 16 * (NPAIR // 2))

            norm(3, 6 * DT)
            for p in range(NPAIR):
                head_tile(NPAIR + p, T_Q + p, W_Q + p)
                if p:
                    root()
            root()
            for i in range(2):
                act.wait_ge(S["R_psum"], i + 1)
                fn(Rb[:, i * DEC_B // 2:(i + 1) * DEC_B // 2].rearrange("p b g h -> p (b g h)"), bk[2 + i][:], ACT.Copy).then_inc(S["R_done"], 1)
            act.wait_ge(S["nFs_psum"], 1)
            fn(nFs[:], bk[2][0:NS, 0:FH], ACT.Copy).then_inc(S["nFs_ready"], 1)

            def bias_out(h):
                act.wait_ge(S["bias_psum"], h + 1)
                if h >= 2:
                    act.wait_ge(S["s_max"], 4 * (h - 1))
                fn(bias[:, h % 2, :], pj[1][:, 1, :], ACT.Copy).then_inc(S["bias_ready"], 1)

            def expo(t):
                n = (t % 4 + 1) * P
                act.wait_ge(S["s_max"], t + 1)
                fn(pr[:, t % 4, 0:n], pr[:, t % 4, 0:n], ACT.Exp, bias=nmx[:, t:t + 1], accum_out=rs[:, t:t + 1]).then_inc(S["p_exp"], 1)

            def turned_out(h):
                act.wait_ge(S["pT_psum"], 4 * h + 4)
                if h:
                    act.wait_ge(S["fo_psum"], h)
                for k in range(RT):
                    fn(pT[:, k, k * P:SEQ], bk[k][:, k * P:SEQ], ACT.Copy).then_inc(S["pT_ready"], 1)

            bias_out(0)
            for h in range(FH + 1):
                for qb in range(RT):
                    if h < FH:
                        expo(4 * h + qb)
                        if qb == 3 and h + 1 < FH:
                            bias_out(h + 1)
                    if qb == 1 and h:
                        turned_out(h - 1)
                    if qb == 3 and h:
                        r = ((h - 1) % 2) * HD
                        act.wait_ge(S["fo_psum"], h)
                        fn(foT[r:r + HD, (h - 1) // 2, 0:SEQ], pj[1][r:r + HD, 0, :], ACT.Copy).then_inc(S["fo_done"], 1)

            for b in range(DEC_B):
                act.wait_ge(S["ssub"], 2 * b + 2)
                fn(ssb[:, b % 2].rearrange("p g n -> p (g n)"), ssb[:, b % 2].rearrange("p g n -> p (g n)"), ACT.Exp).then_inc(S["ss_exp"], 1)
                s = sn[:, b].rearrange("p a b c -> p (a b c)")
                fn(s, s, ACT.Exp).then_inc(S["ss_exp"], 1)
            act.wait_ge(S["so_done"], 2 * DEC_B)
            for p in range(NPAIR):
                fn(h_hi[:, p, :], foT[:, p, :], ACT.Copy).then_inc(S["fo_hi_ready"], 1)
            keys_saved(act)
            norm(4, 9 * DT)
            feed_forward(1)

        @block.vector
        def _(dve):
            V = nc.vector
            links = [0]

            def link(ins):
                links[0] += 1
                ins.then_inc(S["dve_chain"], 1)
                dve.wait_ge(S["dve_chain"], links[0])

            chain = [0]

            def variance(scale):
                c = chain[0]
                dve.wait_ge(S["ms_ready"], c + 1)
                for half in range(2):
                    i = V.tensor_scalar(var[:, half * HALF:(half + 1) * HALF], bk[half][:, 0:HALF], scale, EPS, ALU.mult, ALU.add)
                i.then_inc(S["var_ready"], 1)

            def refine():
                c = chain[0]
                dve.wait_ge(S["r_exp"], c + 1)
                link(V.tensor_tensor(newt[:], rstd[:], rstd[:], ALU.mult))
                link(V.tensor_tensor(newt[:], newt[:], var[:], ALU.mult))
                link(V.tensor_scalar(newt[:], newt[:], -0.5, 1.5, ALU.mult, ALU.add))
                link(V.tensor_tensor(rstd[:], rstd[:], newt[:], ALU.mult))
                chain[0] += 1

            def sample(ap):
                return ap.rearrange("p (b t) -> p b t", b=DEC_B)

            def over_t(ap):
                return ap.unsqueeze(2).to_broadcast([P, DEC_B, DEC_T])

            def norm(z, g, shift, scale):
                link(V.tensor_scalar(gain[:], mod[:, scale:scale + DT, :], 1.0, None, ALU.add))
                V.tensor_tensor(gain[:], gain[:], vec[:, g:g + DT].unsqueeze(2).to_broadcast([P, DT, NC]), ALU.mult).then_inc(S["gains"], 1)
                dve.wait_ge(S["gains"], z + 1)
                variance(1.0 / D)
                refine()
                for k in range(DT):
                    if k >= 2:
                        dve.wait_ge(S["hmod"], z * DT + k - 1)
                    V.tensor_tensor(xs[:, k % 2, :], x[:, k, :], rstd[:], ALU.mult).then_inc(S["scaled"], 1)
                    dve.wait_ge(S["scaled"], z * DT + k + 1)
                    if z * DT + k >= 2:
                        dve.wait_ge(S["hi_ready"], z * DT + k - 1)
                        dve.wait_ge(S["h_ready"], z * DT + k - 1)
                    link(V.tensor_tensor(sample(hf[:, k % 2, SEQ:NT]), sample(xs[:, k % 2, SEQ:NT]), over_t(gain[:, k, 1:NC]), ALU.mult))
                    V.tensor_tensor(sample(hf[:, k % 2, SEQ:NT]), sample(hf[:, k % 2, SEQ:NT]), over_t(mod[:, shift + k, 1:NC]), ALU.add)\
                        .then_inc(S["hsample"], 1)
                    dve.wait_ge(S["hi_ready"], z * DT + k + 1)
                    V.tensor_tensor(h_lo[:, k, :], hf[:, k % 2, :], h_hi[:, k, :].bitcast(F32), ALU.subtract).then_inc(S["h_ready"], 1)

            def residual(tile, done, gate_at):
                for k in range(DT):
                    n = tile + k
                    wait_tile(dve, done(k))
                    ps = pj[n % 2]
                    link(V.scalar_tensor_tensor(out=x[:, k, 0:HALF], in0=ps[:, 0, 0:HALF], scalar=gain1[:, k, 0:1], in1=x[:, k, 0:HALF],
                                                op0=ALU.mult, op1=ALU.add))
                    link(V.scalar_tensor_tensor(out=x[:, k, HALF:SEQ], in0=ps[:, 1, 0:SEQ - HALF], scalar=gain1[:, k, 0:1], in1=x[:, k, HALF:SEQ],
                                                op0=ALU.mult, op1=ALU.add))
                    link(V.tensor_tensor(sample(newt[:, 0:NS]), sample(ps[:, 1, SEQ - HALF:HALF]), over_t(gain1[:, k, 1:NC]), ALU.mult))
                    V.tensor_tensor(x[:, k, SEQ:NT], x[:, k, SEQ:NT], newt[:, 0:NS], ALU.add).then_inc(S["x_done"], 1)
                    xn[0] += 1
                    dve.wait_ge(S["x_done"], xn[0])
                    dve.sem_inc(pair_free(n), 1)

            xn = [0]

            def gate_vector(g):
                link(V.tensor_scalar(gain1[:], mod[:, g:g + DT, :], 1.0, None, ALU.add))

            gain1 = ctmp

            def modulation_out(i, first, n, bank):
                dve.wait_ge(S["m_used"], first + n)
                V.tensor_tensor(mod[:, first:first + n, :], bank[:, 0:n * NC].rearrange("p (f c) -> p f c", c=NC),
                                vec[:, V_B + first:V_B + first + n].unsqueeze(2).to_broadcast([P, n, NC]), ALU.add).then_inc(S["m_done"], 1)
                dve.wait_ge(S["m_done"], i)

            dve.wait_ge(S["c_exp"], 1)
            dve.wait_ge(S["cst_in"], 32)
            link(V.tensor_scalar(ctmp[:], ctmp[:], 1.0, None, ALU.add))
            link(V.reciprocal(ctmp[:], ctmp[:]))
            V.tensor_tensor(cact[:], cact[:], ctmp[:], ALU.mult).then_inc(S["c_ready"], 1)
            modulation_out(1, 0, MOD_FIRST, bk[3])
            norm(0, V_RET, 0, DT)

            def rope(h, i, dst, scale):
                wait_tile(dve, (ret_proj_slab(h) + 2 * i + 2) * SLAB)
                n = ret_proj_tile(h) + 2 * i
                a, b = pj[0][:, :, 0:HALF], pj[1][:, :, 0:HALF]
                cos, sin = two(rc[:, R_COS:R_COS + NT]), two(rc[:, R_SIN:R_SIN + NT])
                sine = two(newt[:])

                def times(out, ps, tab):
                    return V.scalar_tensor_tensor(out=out, in0=ps, scalar=scale, in1=tab, op0=ALU.mult, op1=ALU.mult)
                link(times(two(dst[:, 0, :]), a, cos))
                link(times(sine, b, sin))
                link(V.tensor_tensor(dst[:, 0, :], dst[:, 0, :], newt[:], ALU.subtract))
                link(times(two(dst[:, 1, :]), a, sin))
                link(times(sine, b, cos))
                V.tensor_tensor(dst[:, 1, :], dst[:, 1, :], newt[:], ALU.add).then_inc(S["rope_done"], 1)
                dve.wait_ge(S["rope_done"], 2 * h + i + 1)
                dve.sem_inc(S["pair_free0"], 1)
                dve.sem_inc(S["pair_free1"], 1)

            def queries(h):
                rope(h, 0, qT, 1.0)
                rope(h, 1, kT, DK ** -0.5)

            def cross(h):
                link(V.tensor_tensor(qx[:], qT[:, :, SEQ:NT],
                                     rc[:, R_CR + h * NS:R_CR + (h + 1) * NS].unsqueeze(1).to_broadcast([P, 2, NS]), ALU.mult))

            def silu(h):
                for f in range(4):
                    n = 4 * h + f
                    e = hf[:, f % 2, :]
                    dve.wait_ge(S["silu_exp"], n + 1)
                    link(V.tensor_scalar(e, e, 1.0, None, ALU.add))
                    link(V.reciprocal(e, e))
                    V.tensor_tensor(two(gate[:, f, :]), two(e), pj[f % 2][:, :, 0:HALF], ALU.mult).then_inc(S["silu_done"], 1)
                    dve.wait_ge(S["silu_done"], n + 1)
                    dve.sem_inc(pair_free(f), 1)

            dve.wait_ge(S["rc_in"], 16)
            queries(0)
            silu(0)
            for h in range(RH):
                last_head = h == RH - 1
                if h:
                    dve.wait_ge(S["os_ready"], h)
                cross(h)
                at = 0
                for j in range(RT):
                    n = SEQ - j * P
                    dve.wait_ge(S["scores_ready"], 4 * h + j + 1)
                    dve.wait_ge(S[f"dec_in{h % 2}"], 16 * (h // 2 + 1))
                    if h and j == 0:
                        dve.wait_ge(S["o_ready"], 4 * h)
                    V.tensor_tensor(att[:, at:at + n], bk[j][:, 0:n], dec[:, h % 2, 0:n], ALU.mult).then_inc(S["decayed"], 1)
                    at += n
                V.tensor_tensor(atts[:], bk[3][0:NS, P:P + NS], rc[0:NS, R_DS + h * NS:R_DS + (h + 1) * NS], ALU.mult).then_inc(S["decayed"], 1)
                if not last_head:
                    queries(h + 1)
                dve.wait_ge(S["tr_evac"], 8 * h + 8)
                for b in range(DEC_B):
                    n = h * DEC_B + b
                    if n >= 2:
                        dve.wait_ge(S["upd_ready"], 2 * (n - 1))
                    V.tensor_scalar(kb[:, b % 2, :], ks[:], rc[0:NS, R_KS + h * DEC_B + b:R_KS + h * DEC_B + b + 1], None, ALU.mult)\
                        .then_inc(S["kb_ready"], 1)
                    for d in range(2):
                        dve.wait_ge(S["upd_ready"], 2 * n + d + 1)
                        s = st[:, n % 2, d, :]
                        V.scalar_tensor_tensor(out=s, in0=s, scalar=rc[:, R_CD + h:R_CD + h + 1], in1=bk[1 + d][:], op0=ALU.mult, op1=ALU.add)\
                            .then_inc(S["upd_done"], 1)
                variance(1.0 / DV)
                refine()
                for e in range(4):
                    link(V.tensor_tensor(oT[:, e, :], oT[:, e, :], rstd[:], ALU.mult))
                    V.tensor_tensor(oT[:, e, :], oT[:, e, :], gate[:, e, :], ALU.mult).then_inc(S["gated"], 1)
                for e in range(4):
                    dve.wait_ge(S["og_hi_ready"], 4 * h + e + 1)
                    V.tensor_tensor(og_lo[:, e, :], oT[:, e, :], og_hi[:, e, :].bitcast(F32), ALU.subtract).then_inc(S["og_ready"], 1)
                if not last_head:
                    silu(h + 1)
                m = MOD_FIRST + h * MOD_PER_HEAD
                modulation_out(2 * h + 2, m, DT, bk[3])
                if h == 0:
                    gate_vector(2 * DT)
                residual(ret_out_tile(h), lambda k: ret_out_slab(h) * SLAB + 4 * (k + 1), 2 * DT)
                modulation_out(2 * h + 3, m + DT, 2 * DT, bk[2])

            def feed_forward(layer, g):
                gate_vector(g)
                for half in range(2):
                    u = 2 * layer + half
                    base = ff_slab(layer, half) * SLAB
                    t0 = ff_tile(layer, half)
                    for m in range(FFT):
                        n = u * FFT + m
                        e = sig[:, n % 2, :]
                        dve.wait_ge(S["silu_exp"], 4 * RH + n + 1)
                        link(V.tensor_scalar(e, e, 1.0, None, ALU.add))
                        link(V.reciprocal(e, e))
                        if n >= 2:
                            dve.wait_ge(S["hid_hi_ready"], n - 1)
                        link(V.tensor_tensor(two(hid[:, n % 2, :]), two(e), pj[(t0 + 2 * m) % 2][:, :, 0:HALF], ALU.mult))
                        dve.sem_inc(pair_free(t0 + 2 * m), 1)
                        wait_tile(dve, base + (2 * m + 2) * SLAB)
                        V.tensor_tensor(two(hid[:, n % 2, :]), two(hid[:, n % 2, :]), pj[(t0 + 2 * m + 1) % 2][:, :, 0:HALF], ALU.mult)\
                            .then_inc(S["hid_full"], 1)
                        dve.wait_ge(S["hid_full"], n + 1)
                        dve.sem_inc(pair_free(t0 + 2 * m + 1), 1)
                        dve.wait_ge(S["hid_hi_ready"], n + 1)
                        V.tensor_tensor(hid_lo[:, m, :], hid[:, n % 2, :], hid_hi[:, m, :].bitcast(F32), ALU.subtract).then_inc(S["hid_ready"], 1)
                    out0 = base + 2 * FFT * SLAB
                    residual(t0 + 2 * FFT, lambda k: out0 + FFT * (k + 1), g)

            states_saved(dve)
            norm(1, V_FFN, 3 * DT, 4 * DT)
            feed_forward(0, 5 * DT)
            norm(2, V_KV, 12 * DT, 13 * DT)

            def head_rows(k, dst, g):
                variance(1.0 / HD)
                refine()
                dve.wait_ge(S["fk_raw"], k + 1)
                V.scalar_tensor_tensor(out=dst, in0=fraw[:, k % 2, :], scalar=g, in1=rstd[:], op0=ALU.mult, op1=ALU.mult).then_inc(S["fk_done"], 1)

            for p in range(NPAIR):
                head_rows(p, fkT[:, p, :], vec[:, V_KN:V_KN + 1])

            n = T_KV + 2 * NPAIR
            wait_tile(dve, (W_KV + 17) * SLAB)
            z, u, s2, acc = (lfa[:, i, :] for i in range(4))
            link(V.tensor_scalar(two(z), pj[n % 2][0:FH, :, 0:HALF], vec[0:FH, V_BF:V_BF + 1], None, ALU.add))
            dve.sem_inc(pair_free(n), 1)
            link(V.tensor_scalar(u, z, -1.0, None, ALU.mult))
            V.tensor_tensor(u, u, z, ALU.max).then_inc(S["lf_raw"], 1)
            dve.wait_ge(S["lf_exp"], 1)
            link(V.tensor_scalar(s2, u, 2.0, None, ALU.add))
            link(V.reciprocal(s2, s2))
            link(V.tensor_tensor(u, u, s2, ALU.mult))
            link(V.tensor_tensor(s2, u, u, ALU.mult))
            link(V.tensor_scalar(acc, s2, 1.0 / 17, 1.0 / 15, ALU.mult, ALU.add))
            for odd in (13, 11, 9, 7, 5, 3, 1):
                link(V.tensor_tensor(acc, acc, s2, ALU.mult))
                link(V.tensor_scalar(acc, acc, 1.0 / odd, None, ALU.add))
            link(V.tensor_tensor(acc, acc, u, ALU.mult))
            link(V.tensor_scalar(z, z, 0.0, None, ALU.min))
            V.scalar_tensor_tensor(out=lf[:], in0=acc, scalar=-2.0, in1=z, op0=ALU.mult, op1=ALU.add).then_inc(S["lf_done"], 1)
            dve.wait_ge(S["lf_done"], 1)
            link(V.memset(lfa[:, 0, 0:SEQ], 1.0))
            link(V.tensor_tensor_scan(lfa[:, 1, 0:SEQ], lfa[:, 0, 0:SEQ], lf[:, 0:SEQ], 0.0, ALU.mult, ALU.add))
            link(V.tensor_copy(lfa[:, 1, SEQ:NT], lf[:, SEQ:NT]))
            run = lfa[:, 1, SEQ:NT].rearrange("p (b t) -> p b t", b=DEC_B)
            for t in range(1, DEC_T):
                link(V.tensor_tensor(run[:, :, t:t + 1], run[:, :, t:t + 1], run[:, :, t - 1:t], ALU.add))
            V.tensor_scalar(negF[:], lfa[:, 1, :], -1.0, None, ALU.mult).then_inc(S["nF_ready"], 1)
            dve.wait_ge(S["nF_ready"], 1)
            norm(3, V_ATT, 6 * DT, 7 * DT)
            for p in range(NPAIR):
                if p == 0:
                    link(V.tensor_scalar(m0[:], vec[:, V_QN:V_QN + 1], HD ** -0.5, None, ALU.mult))
                head_rows(NPAIR + p, fqT[:, p, :], m0[:])
            dve.wait_ge(S["plf_in"], 16 * DEC_B * NPG)
            link(V.memset(suf[:, :, NPG - 1, :], 0.0))
            for g in range(NPG - 2, -1, -1):
                link(V.tensor_tensor(suf[:, :, g, :], suf[:, :, g + 1, :], plf[:, :, g + 1, :], ALU.add))
            dve.sem_inc(S["suf_ready"], 1)
            V.tensor_copy(idb[:], ident).then_inc(S["idb_ready"], 1)
            V.tensor_copy(cmb[:], cst[:, C_CM:C_CM + P]).then_inc(S["idb_ready"], 1)

            def top(t):
                n = (t % 4 + 1) * P
                dve.wait_ge(S["s_psum"], t + 1)
                dve.wait_ge(S["bias_ready"], t // 4 + 1)
                if t >= 4:
                    dve.wait_ge(S["pT_psum"], t - 3)
                link(V.tensor_tensor_reduce(out=pr[:, t % 4, 0:n], in0=s_psum(t)[:, 0:n], in1=bias[:, (t // 4) % 2, 0:n], scale=1.0, scalar=-3e38,
                                            op0=ALU.add, op1=ALU.max, accum_out=mx[:, t:t + 1]))
                V.tensor_scalar(nmx[:, t:t + 1], mx[:, t:t + 1], -1.0, None, ALU.mult).then_inc(S["s_max"], 1)

            def s_psum(t):
                return pj[0][:, t % 2, :]

            def unit_sum(t):
                n = (t % 4 + 1) * P
                dve.wait_ge(S["p_exp"], t + 1)
                link(V.reciprocal(rsi[:, t:t + 1], rs[:, t:t + 1]))
                V.tensor_scalar(pr[:, t % 4, 0:n], pr[:, t % 4, 0:n], rsi[:, t:t + 1], None, ALU.mult).then_inc(S["p_done"], 1)

            for t in range(4 * FH):
                top(t)
                if t:
                    unit_sum(t - 1)
            unit_sum(4 * FH - 1)

            dve.wait_ge(S["fo_done"], FH)
            V.memset(qbd[:], 0.0).then_inc(S["qbd_ready"], 1)
            dve.wait_ge(S["qbd_ready"], 1)
            for p in range(NPAIR):
                for j in range(2):
                    r = slice(j * HD, (j + 1) * HD)
                    V.tensor_copy(qbd[r, p, :, j * DEC_T:(j + 1) * DEC_T], sample(fqT[r, p, SEQ:NT])).then_inc(S["qbd_ready"], 1)
            dve.wait_ge(S["sn_psum"], 1)
            new = bk[0][0:NS, :].rearrange("p (a b c t) -> p b a c t", a=NPAIR, b=DEC_B, c=2)
            nf = nFs[:].rearrange("p (a c) -> p a c", c=2).unsqueeze(3).to_broadcast([NS, NPAIR, 2, DEC_T])
            for b in range(DEC_B):
                V.tensor_tensor(sn[:, b], new[:, b], nf, ALU.add).then_inc(S["sn_done"], 1)
                dve.wait_ge(S["sn_done"], 2 * b + 1)
                V.tensor_tensor(sn[:, b].rearrange("p a c t -> p (a c) t"), sn[:, b].rearrange("p a c t -> p (a c) t"),
                                cst[0:NS, C_NM + b * DEC_T:C_NM + (b + 1) * DEC_T].unsqueeze(1).to_broadcast([NS, FH, DEC_T]), ALU.add)\
                    .then_inc(S["sn_done"], 1)
            dve.wait_ge(S["sn_done"], 2 * DEC_B)

            def scores_out(b):
                dve.wait_ge(S["kpg_used"], NPG * (b + 1))
                if b >= 2:
                    dve.wait_ge(S["so_psum"], b - 1)
                V.tensor_tensor(ssb[:, b % 2].rearrange("p g (h t) -> p g h t", t=DEC_T),
                                bk[b % 2][:].rearrange("p (g h t) -> p g h t", g=NPG, t=DEC_T),
                                Rb[:, b].unsqueeze(3).to_broadcast([P, NPG, FH, DEC_T]), ALU.add).then_inc(S["ss_done"], 1)
                dve.wait_ge(S["ss_done"], b + 1)
                if b:
                    dve.wait_ge(S["m1_psum"], b)
                link(V.tensor_reduce(m1[:], ssb[:, b % 2].rearrange("p g n -> p n g"), AX.X, ALU.max))
                V.tensor_tensor(m1[0:NS, :], m1[0:NS, :], sn[:, b].rearrange("p a c t -> p (a c t)"), ALU.max).then_inc(S["m1_ready"], 1)
                dve.wait_ge(S["m1_psum"], b + 1)
                if b:
                    dve.wait_ge(S["mb_psum"], b)
                link(V.tensor_reduce(m2[:], bk[2][0:64, 0:P], AX.X, ALU.max))
                V.tensor_scalar(dg[:], cst[0:64, C_ID:C_ID + 64], m2[:], None, ALU.mult).then_inc(S["dg_ready"], 1)
                dve.wait_ge(S["mb_psum"], b + 1)
                V.tensor_tensor(ssb[:, b % 2], ssb[:, b % 2], bk[2][:, 0:64].unsqueeze(1).to_broadcast([P, NPG, 64]), ALU.subtract)\
                    .then_inc(S["ssub"], 1)
                s = sn[:, b].rearrange("p a c t -> p (a c t)")
                V.tensor_tensor(s, s, bk[2][0:NS, 0:64], ALU.subtract).then_inc(S["ssub"], 1)
                dve.wait_ge(S["ssub"], 2 * b + 2)

            def heads_out(b):
                dve.wait_ge(S["l_psum"], b + 1)
                dve.wait_ge(S["so_psum"], b + 1)
                link(V.reciprocal(li[:], bk[3][:, 0:64]))
                for j in range(2):
                    r = slice(j * HD, (j + 1) * HD)
                    o = bk[3][r, 64:128].rearrange("p (a c t) -> p a c t", c=2, t=DEC_T)[:, :, j, :]
                    l = li[r, :].rearrange("p (a c t) -> p a c t", c=2, t=DEC_T)[:, :, j, :]
                    V.tensor_tensor(foT[r, :, SEQ + b * DEC_T:SEQ + (b + 1) * DEC_T], o, l, ALU.mult).then_inc(S["so_done"], 1)

            for b in range(DEC_B):
                scores_out(b)
                heads_out(b)
            for p in range(NPAIR):
                dve.wait_ge(S["fo_hi_ready"], p + 1)
                V.tensor_tensor(h_lo[:, p, :], foT[:, p, :], h_hi[:, p, :].bitcast(F32), ALU.subtract).then_inc(S["fo_ready"], 1)
            gate_vector(8 * DT)
            residual(T_O, lambda k: (W_O + k + 1) * SLAB, 8 * DT)
            keys_saved(dve)
            norm(4, V_FFN + DT, 9 * DT, 10 * DT)
            feed_forward(1, 11 * DT)


def weight_tiles(w):
    k, n = w.shape
    return w.reshape(k // P, P, n // P, P).transpose(2, 0, 1, 3).reshape(-1, P, P)


def slabs(tiles):
    t = np.concatenate(tiles, axis=0)
    return np.ascontiguousarray(t.reshape(-1, SLAB, P, P).transpose(0, 2, 1, 3)).reshape(-1, P, SLAB * P)


def columns(v):
    return v.reshape(-1, P).T


def feature_major(a):
    return a.T.reshape(-1, P, a.shape[0]).transpose(1, 0, 2)


def token_major(a, lo, hi):
    return a[:, :, lo:hi].transpose(2, 1, 0).reshape(hi - lo, -1)


def kernel(x_prompt, x_sample, cache_k, cache_v, cache_logf, state_ret, page_table, c_prompt, c_sample, w_mod, b_mod,
           ret_norm_g, w_ret_in, w_ret_out, attn_norm_g, w_q, q_norm_g, w_o, ffn_norm_g, w_ffn_in, w_ffn_out,
           kv_norm_g, w_kvmod, b_kvmod, w_kvf, b_f, k_norm_g):
    import concourse.bacc as bacc
    from concourse.bass_utils import run_bass_kernel_spmd

    a = {k: np.asarray(v) for k, v in dict(locals()).items() if k not in ("bacc", "run_bass_kernel_spmd")}
    win, wout = a["w_ret_in"][0], a["w_ret_out"][0]

    def head_in(h):
        cols = [win[:, h * DK:(h + 1) * DK], win[:, D + h * DK:D + (h + 1) * DK],
                win[:, 2 * D + h * DV:2 * D + (h + 1) * DV], win[:, 4 * D + h * DV:4 * D + (h + 1) * DV]]
        return weight_tiles(np.concatenate(cols, axis=1))

    def head_out(h):
        return weight_tiles(wout[h * DV:(h + 1) * DV])

    def ffn(l):
        w, wo, out = a["w_ffn_in"][l], a["w_ffn_out"][l], []
        for half in range(2):
            for m in range(half * FFT, (half + 1) * FFT):
                out.append(weight_tiles(w[:, m * P:(m + 1) * P]))
                out.append(weight_tiles(w[:, FF + m * P:FF + (m + 1) * P]))
            out.append(weight_tiles(wo[half * FFT * P:(half + 1) * FFT * P]))
        return out

    kvf = np.concatenate([a["w_kvf"], np.zeros((D, P - FH), np.float32)], axis=1)
    stream = [head_in(0)]
    for h in range(RH):
        if h < RH - 1:
            stream.append(head_in(h + 1))
        stream.append(head_out(h))
    stream += ffn(0) + [weight_tiles(kvf), weight_tiles(a["w_q"][0]), weight_tiles(a["w_o"][0])] + ffn(1)
    n_pool = a["cache_k"].shape[0]
    cst, rc, dec = constants()
    pad = np.concatenate([a["b_f"], np.zeros(P - FH, np.float32)])
    vec = np.concatenate([columns(v) for v in (
        a["b_mod"][0], a["b_mod"][1], a["b_kvmod"], a["ret_norm_g"][0], a["attn_norm_g"][0], a["ffn_norm_g"][0], a["ffn_norm_g"][1],
        a["kv_norm_g"], np.concatenate([a["q_norm_g"][0]] * 2), np.concatenate([a["k_norm_g"]] * 2), pad)], axis=1)
    ins = {
        "xT": feature_major(np.concatenate([a["x_prompt"][0], a["x_sample"].reshape(NS, D)], axis=0)),
        "cT": feature_major(np.concatenate([a["c_prompt"], a["c_sample"]], axis=0)),
        "w": slabs(stream),
        "wm": slabs([weight_tiles(a["w_mod"][0]), weight_tiles(a["w_mod"][1]), weight_tiles(a["w_kvmod"])]),
        "vec": vec, "cst": cst, "rc": rc, "dec": dec,
        "state": a["state_ret"][0].reshape(DEC_B, RH, 2, P, DV).transpose(1, 0, 3, 2, 4),
        "kc": a["cache_k"].reshape(n_pool, PAGE, NPAIR, P).transpose(0, 3, 2, 1).reshape(n_pool, P, D),
        "vc": a["cache_v"].reshape(n_pool, PAGE, D),
        "lf": a["cache_logf"],
        "table": a["page_table"].reshape(1, -1),
    }
    outs = {"o_x": (P, DT, NT), "o_k": (P, NPAIR, NT), "o_v": (P, NPAIR, NT), "o_lf": (FH, NT),
            "st_p": (RH, P, 2, DV), "st_s": (RH, DEC_B, P, 2, DV)}
    nc = bacc.Bacc("TRN2", target_bir_lowering=False, num_devices=1)
    A, arrays = {}, {}
    for name, v in ins.items():
        v = np.ascontiguousarray(v)
        arrays[f"in_{name}"] = v
        A[name] = nc.dram_tensor(f"in_{name}", v.shape, mybir.dt.from_np(v.dtype), kind="ExternalInput").ap()
    for name, shape in outs.items():
        A[name] = nc.dram_tensor(f"out_{name}", shape, F32, kind="ExternalOutput").ap()
    program(nc, A)
    r = run_bass_kernel_spmd(nc, [arrays], core_ids=[0]).results[0]
    y, k, v, lf = (r[f"out_{n}"] for n in ("o_x", "o_k", "o_v", "o_lf"))
    sp = np.ascontiguousarray(r["out_st_p"].transpose(0, 2, 1, 3)).reshape(1, 1, RH, DK, DV)
    ss = np.ascontiguousarray(r["out_st_s"].transpose(1, 0, 3, 2, 4)).reshape(1, DEC_B, RH, DK, DV)
    return (token_major(y, 0, SEQ).reshape(1, SEQ, D), token_major(y, SEQ, NT).reshape(DEC_B, DEC_T, D), sp, ss,
            token_major(k, 0, SEQ).reshape(1, SEQ, FH, HD), token_major(v, 0, SEQ).reshape(1, SEQ, FH, HD),
            np.ascontiguousarray(lf[:, 0:SEQ].T).reshape(1, SEQ, FH),
            token_major(k, SEQ, NT).reshape(DEC_B, DEC_T, FH, HD), token_major(v, SEQ, NT).reshape(DEC_B, DEC_T, FH, HD),
            np.ascontiguousarray(lf[:, SEQ:NT].T).reshape(DEC_B, DEC_T, FH))
```

```python
from contextlib import ExitStack

import numpy as np
import concourse.bass as bass
from concourse import mybir

F32 = mybir.dt.float32
F32R = mybir.dt.float32r
BF16 = mybir.dt.bfloat16
I32 = mybir.dt.int32
ALU = mybir.AluOpType
ACT = mybir.ActivationFunctionType
AX = mybir.AxisListType

P = 128
D = 1024
DT = D // P
SEQ = 512
DEC_B, DEC_T = 8, 4
NS = DEC_B * DEC_T
NT = SEQ + NS
HALF = NT // 2
RT = SEQ // P
NC = 1 + DEC_B
RH = 4
DK, DV = 256, 512
FH, HD = 16, 64
NPAIR = FH // 2
FF = 2816
FFT = FF // P // 2
PAST, PAGE = 1024, 128
NPG = PAST // PAGE
EPS = 1e-6
SLAB = 8
RAW, SPL = 4, 2
VR = 3
VLAG = 12
UNITS = DEC_B * NPG
MRING = 2
NMOD = 14 * DT
MOD_FIRST = 2 * DT
MOD_PER_HEAD = (NMOD - MOD_FIRST) // RH
BIG = 1e30

V_B = 0
V_RET = NMOD
V_ATT = V_RET + DT
V_FFN = V_ATT + DT
V_KV = V_FFN + 2 * DT
V_QN = V_KV + DT
V_KN = V_QN + 1
V_BF = V_KN + 1
NV = V_BF + 1

C_ID = 0
C_BD = C_ID + P
C_US = C_BD + P
C_CM = C_US + P
C_NM = C_CM + P
C_FO = C_NM + NS
C_END = C_FO + 64
R_COS = 0
R_SIN = NT
R_CR = 2 * NT
R_KP = R_CR + RH * NS
R_KS = R_KP + RH * RT
R_DS = R_KS + RH * DEC_B
R_CD = R_DS + RH * NS
R_END = R_CD + RH


def constants():
    f = np.float32
    c = np.zeros((P, C_END), f)
    i = np.arange(P)
    c[:, C_ID:C_ID + P] = np.eye(P)
    c[:, C_BD:C_BD + P] = (i[:, None] // HD) == (i[None, :] // HD)
    c[:, C_US:C_US + P] = i[:, None] > i[None, :]
    c[:, C_CM:C_CM + P] = np.where(i[None, :] <= i[:, None], 0, -BIG)
    j, q = np.arange(NS)[:, None], np.arange(NS)[None, :]
    same = (j // DEC_T == q // DEC_T) & (j % DEC_T <= q % DEC_T)
    c[:NS, C_NM:C_NM + NS] = np.where(same, 0, -BIG)
    c[:, C_FO:C_FO + 64] = (i[:, None] % 64) == np.arange(64)[None, :]

    r = np.zeros((P, R_END), f)
    dec = np.zeros((RH, P, SEQ), f)
    half = DK // 2
    freqs = f(10000.0) ** (-np.arange(half, dtype=f) / f(half))
    pos = np.concatenate([np.arange(SEQ), np.tile(PAST + np.arange(DEC_T), DEC_B)]).astype(f)
    ang = (freqs[:, None] * pos[None, :]).astype(f)
    r[:, R_COS:R_COS + NT] = np.cos(ang)
    r[:, R_SIN:R_SIN + NT] = np.sin(ang)
    log_g = np.log1p(-np.exp2(-5.0 - np.arange(RH)))
    t = np.arange(NS) % DEC_T
    b = np.arange(NS) // DEC_T
    for h in range(RH):
        r[:, R_CR + h * NS:R_CR + (h + 1) * NS] = np.exp(log_g[h] * (t + 1))[None, :]
        for rt in range(RT):
            r[:, R_KP + h * RT + rt] = np.exp(log_g[h] * (SEQ - 1 - rt * P - i))
        for bb in range(DEC_B):
            r[:NS, R_KS + h * DEC_B + bb] = np.where(b == bb, np.exp(log_g[h] * (DEC_T - 1 - t)), 0)
        r[:NS, R_DS + h * NS:R_DS + (h + 1) * NS] = np.where(same, np.exp(log_g[h] * np.maximum(q - j, 0)), 0)
        off = np.arange(SEQ)[None, :] - i[:, None]
        dec[h] = np.where(off >= 0, np.exp(log_g[h] * np.maximum(off, 0)), 0)
        r[:, R_CD + h] = np.exp(log_g[h] * DEC_T)
    return c, r, dec


def program(nc, A):
    ctx = ExitStack()

    def sb(name, shape, dt=F32, where=None):
        return (where or ctx).enter_context(nc.sbuf_tensor(name, shape, dt))

    def sem(name):
        return ctx.enter_context(nc.semaphore(name))

    with ctx:
        x = sb("x", [P, DT, NT])
        place = ExitStack()
        h_hi = sb("h_hi", [P, DT, NT], F32R, where=place)
        h_lo = sb("h_lo", [P, DT, NT], F32R, where=place)
        place.close()
        vraw = sb("fox_vraw", [P, VR, D], where=place)
        v_hi = sb("fox_v_hi", [P, 2, D], F32R, where=place)
        v_lo = sb("fox_v_lo", [P, 2, D], F32R, where=place)
        ss0 = sb("fox_ss0", [64, PAST + NS], where=place)
        place.close()
        sb("h_place", [P, 2 * DT * NT])
        raw = sb("raw", [P, RAW, SLAB * P])
        w_hi = sb("w_hi", [P, SPL, SLAB * P], F32R)
        w_lo = sb("w_lo", [P, SPL, SLAB * P], F32R)
        mplace = ExitStack()
        mraw = sb("mraw", [P, MRING, SLAB * P], where=mplace)
        mplace.close()
        sT = sb("fox_sT", [P, 2, NPG, P], F32R, where=mplace)
        mplace.close()
        sb("m_place", [P, MRING * SLAB * P])
        mod = sb("mod", [P, NMOD, NC])
        gain = sb("gain", [P, DT, NC])
        vec = sb("vec", [P, NV])
        cst = sb("cst", [P, C_END])
        ones = sb("ones", [P, P])
        cact = sb("cact", [P, DT, NC])
        ctmp = sb("ctmp", [P, DT, NC])
        var = sb("var", [P, NT])
        rstd = sb("rstd", [P, NT])
        newt = sb("newt", [P, NT])
        xplace = ExitStack()
        xs = sb("xs", [P, 2, NT], where=xplace)
        xplace.close()
        bias = sb("fox_bias", [P, 2, SEQ], where=xplace)
        xplace.close()
        sb("x_place", [P, 2 * NT])
        hplace = ExitStack()
        hf = sb("hf", [P, 2, NT], where=hplace)
        hplace.close()
        ss1 = sb("fox_ss1", [64, PAST + NS], where=hplace)
        hplace.close()
        sb("hf_place", [P, 2 * NT])
        m0 = sb("q_gain", [P, 1])
        tabs = sb("tabs", [1, DEC_B * NPG], I32)
        ident = cst[:, C_ID:C_ID + P]
        ss = (ss0, ss1)

        pj = [ctx.enter_context(nc.psum_tensor(f"proj{i}", [P, 2, 512], F32)) for i in range(2)]
        bk = [ctx.enter_context(nc.psum_tensor(f"bank{i}", [P, 512], F32)) for i in range(4)]

        ret = ExitStack()
        rc = sb("rc", [P, R_END], where=ret)
        dec = sb("ret_dec", [P, 2, SEQ], where=ret)
        qT = sb("ret_q", [P, 2, NT], where=ret)
        kT = sb("ret_k", [P, 2, NT], where=ret)
        qx = sb("ret_qx", [P, 2, NS], where=ret)
        vT = sb("ret_vT", [P, 4, NT], where=ret)
        vtok = sb("ret_vtok", [P, RT, DV], where=ret)
        vs = sb("ret_vs", [NS, DV], where=ret)
        ktok = sb("ret_ktok", [P, RT, DK], where=ret)
        ks = sb("ret_ks", [NS, DK], where=ret)
        kb = sb("ret_kb", [NS, 2, DK], where=ret)
        att = sb("ret_att", [P, 1280], where=ret)
        atts = sb("ret_atts", [NS, NS], where=ret)
        gate = sb("ret_gate", [P, 4, NT], where=ret)
        oT = sb("ret_o", [P, 4, NT], where=ret)
        og_hi = sb("ret_og_hi", [P, 4, NT], F32R, where=ret)
        og_lo = sb("ret_og_lo", [P, 4, NT], F32R, where=ret)
        st = sb("ret_state", [P, 2, 2, DV], where=ret)
        ret.close()

        ff = ExitStack()
        hid_hi = sb("hid_hi", [P, FFT, NT], F32R, where=ff)
        hid_lo = sb("hid_lo", [P, FFT, NT], F32R, where=ff)
        hid = sb("hid", [P, 2, NT], where=ff)
        sig = sb("sig", [P, 2, NT], where=ff)
        ff.close()

        fx = ExitStack()
        fkT = sb("fox_kT", [P, NPAIR, NT], where=fx)
        fqT = sb("fox_qT", [P, NPAIR, NT], where=fx)
        fv = sb("fox_v", [P, RT, D], where=fx)
        fvs = sb("fox_vs", [NS, D], where=fx)
        lf = sb("fox_logf", [FH, NT], where=fx)
        negF = sb("fox_negF", [FH, NT], where=fx)
        nFs = sb("fox_nFs", [NS, FH], where=fx)
        Rb = sb("fox_R", [P, DEC_B, NPG, FH], where=fx)
        cmb = sb("fox_cmb", [P, P], BF16, where=fx)
        idb = sb("fox_idb", [P, P], BF16, where=fx)
        fxe = ExitStack()
        lfa = sb("fox_lfa", [FH, 4, NT], where=fxe)
        fraw = sb("fox_raw", [P, 2, NT], where=fxe)
        plf = sb("fox_plf", [P, DEC_B, NPG, FH], where=fxe)
        suf = sb("fox_suf", [P, DEC_B, NPG, FH], where=fxe)
        fxe.close()
        fxp = ExitStack()
        pr = sb("fox_p", [P, 4, SEQ], where=fxp)
        pT = sb("fox_pT", [P, 2, SEQ], where=fxp)
        mx = sb("fox_mx", [P, 64], where=fxp)
        nmx = sb("fox_nmx", [P, 64], where=fxp)
        rs = sb("fox_rs", [P, 64], where=fxp)
        rsi = sb("fox_rsi", [P, 64], where=fxp)
        fxs = ExitStack()
        sn = sb("fox_sn", [NS, DEC_B, NPAIR, 2, DEC_T], where=fxs)
        qbd = sb("fox_qbd", [P, NPAIR, DEC_B, 2 * DEC_T], where=fxs)
        qd_hi = sb("fox_qd_hi", [P, NPAIR * (P + 8)], F32R, where=fxs)
        qd_lo = sb("fox_qd_lo", [P, NPAIR * (P + 8)], F32R, where=fxs)
        so = sb("fox_so", [P, SEQ], where=fxs)
        Rx = sb("fox_Rx", [P, 2, 2, 64], where=fxs)
        pn = sb("fox_pn", [NS, 2, 64], where=fxs)
        nm = sb("fox_nm", [64, DEC_B], where=fxs)
        ls = sb("fox_ls", [64, DEC_B], where=fxs)
        li = sb("fox_li", [64, DEC_B], where=fxs)
        dg = sb("fox_dg", [64, 64], where=fxs)
        fxs.close()
        fxp.close()
        fx.close()

        foT = fqT

        S = {}
        for n in """x_in cst_in rc_in dec_in0 dec_in1 c_in tab_in m_used m_psum m_done c_exp c_ready hi_split w_split w_tiles
                 sq_ready ms_ready var_ready ln_done r_exp r_ready scaled hmod hsample hi_ready h_ready x_done gains
                 dve_chain rope_done v_evac v_tr tr_ready tr_evac scores_ready decayed
                 o_ready o_evac os_ready os_evac upd_ready kb_ready upd_done st_saved0 st_saved1 st_in0 st_in1 sp_ready sp_evac sp_saved
                 osq_ready osq_used gated og_hi_ready og_ready silu_exp silu_done
                 hid_full hid_hi_ready hid_ready
                 fk_raw fk_sq fk_done fv_raw fv_saved0 fv_saved1 fvt_ready fvt_evac lf_raw lf_exp lf_done
                 nF_ready nFs_ready nFs_psum plf_in suf_ready R_psum R_done
                 bias_in0 bias_in1 s_psum s_max p_exp p_done pT_psum pT_ready fo_psum fo_done idb_ready
                 fo_hi_ready fo_ready
                 k_in0 k_in1 k_in2 k_in3 v_in0 v_in1 v_in2 v_hi_ready v_lo_ready v_used qbd_ready qd_zero qd_hi_ready qd_ready sn_psum sn_done Rx_ready ks_out
                 snT_psum snT_out sm_ready s_exp dg_ready sT_psum sT_hi sT_ready pn_psum pn_ready so_out back_psum so_done
                 y_out nF_out k_out lf_out pair_free0 pair_free1 raw_in0 raw_in1 raw_in2 raw_in3 m_in0 m_in1""".split():
            S[n] = sem(n)
        block = ctx.enter_context(nc.Block())

        def two(ap):
            return ap.rearrange("p (h n) -> p h n", h=2)

        W_RET = RH * 16
        W_FF0 = W_RET
        W_KV = W_FF0 + 66
        W_Q = W_KV + 17
        W_PAST = W_Q + 8
        W_O = W_PAST + UNITS
        W_FF1 = W_O + 8
        W_ALL = W_FF1 + 66

        def ret_proj_slab(h):
            return 0 if h == 0 else 16 * h - 4

        def ret_out_slab(h):
            return 16 * h + 24 if h < RH - 1 else 16 * h + 12

        def ff_slab(layer, half):
            return (W_FF0 if layer == 0 else W_FF1) + 33 * half

        def ret_proj_tile(h):
            return 0 if h == 0 else 20 * h - 8

        def ret_out_tile(h):
            return 20 * h + 24 if h < RH - 1 else 20 * h + 12

        TQ = FH * RT
        STEPS = UNITS + VLAG + 1
        T_FF0 = RH * 20
        FFN_T = 2 * FFT + DT
        T_KV = T_FF0 + 2 * FFN_T
        T_Q = T_KV + 17
        T_O = T_Q + 8
        T_FF1 = T_O + 8

        def ff_done_tiles(u):
            return (ff_slab(u // 2, u % 2) + 33) * SLAB

        def tiles_after_out(h):
            return (ret_out_slab(h) + 4) * SLAB

        def ff_tile(layer, half):
            return (T_FF0 if layer == 0 else T_FF1) + FFN_T * half

        def pair_free(n):
            return S[f"pair_free{n % 2}"]

        def states_saved(eng):
            eng.wait_ge(S["st_saved0"], 16 * RH * DEC_B // 2)
            eng.wait_ge(S["st_saved1"], 16 * RH * DEC_B // 2)

        def keys_saved(eng):
            eng.wait_ge(S["k_out"], 16)
            eng.wait_ge(S["lf_out"], 16)

        def wait_tile(eng, tiles):
            eng.wait_ge(S["w_tiles"], tiles)

        def page_of(n):
            return nc.sync.value_load(tabs[0:1, n:n + 1], min_val=0, max_val=A["lf"].shape[0] - 1)

        @block.sync
        def _(sp):
            slab = [0]
            mslab = [0]

            def weights(n):
                for _ in range(n):
                    s = slab[0]
                    if s >= RAW:
                        sp.wait_ge(S["w_split"], s - RAW + 1)
                    row = s if s < W_PAST else s - UNITS
                    sp.dma_start(raw[:, s % RAW, :], A["w"][row]).then_inc(S[f"raw_in{s % RAW}"], 16)
                    slab[0] += 1

            def mods(n):
                for _ in range(n):
                    m = mslab[0]
                    if m >= MRING:
                        sp.wait_ge(S["m_used"], m - MRING + 1)
                    sp.dma_start(mraw[:, m % MRING, :], A["wm"][m]).then_inc(S[f"m_in{m % MRING}"], 16)
                    mslab[0] += 1

            def load_state(n):
                if n >= 2:
                    sp.wait_ge(S[f"st_saved{n % 2}"], 16 * (n // 2))
                sp.dma_start(st[:, n % 2], A["state"][n // DEC_B, n % DEC_B]).then_inc(S[f"st_in{n % 2}"], 16)

            def save_state(n):
                sp.wait_ge(S["upd_done"], 2 * n + 2)
                sp.dma_start(A["st_s"][n // DEC_B, n % DEC_B], st[:, n % 2]).then_inc(S[f"st_saved{n % 2}"], 16)

            sp.dma_start(cact[:], A["cT"]).then_inc(S["c_in"], 16)
            sp.dma_start(vec[:], A["vec"]).then_inc(S["cst_in"], 16)
            sp.dma_start(cst[:], A["cst"]).then_inc(S["cst_in"], 16)
            sp.dma_start(x[:], A["xT"]).then_inc(S["x_in"], 16)
            sp.dma_start(tabs[:], A["table"]).then_inc(S["tab_in"], 16)
            mods(MOD_FIRST)
            sp.dma_start(rc[:], A["rc"]).then_inc(S["rc_in"], 16)
            weights(12 + RAW)
            load_state(0)
            load_state(1)
            for h in range(RH):
                last = h == RH - 1
                if h >= 2:
                    sp.wait_ge(S["decayed"], 5 * (h - 1))
                sp.dma_start(dec[:, h % 2, :], A["dec"][h]).then_inc(S[f"dec_in{h % 2}"], 16)
                for n in range(h * DEC_B, (h + 1) * DEC_B):
                    if n:
                        save_state(n - 1)
                        if n + 1 < RH * DEC_B:
                            load_state(n + 1)
                    if not last:
                        weights(1)
                for _ in range(4):
                    if not last:
                        weights(1)
                    mods(2)
                for _ in range(4):
                    mods(2)
                    weights(1)
                    mods(2)
            save_state(RH * DEC_B - 1)
            weights(66 - RAW + 17 + 8)
            sp.wait_ge(S["tab_in"], 16)
            sp.wait_ge(S["h_ready"], DT * 3)
            with nc.sync.Fori(0, DEC_B) as b:
                for g in range(NPG):
                    pg = nc.sync.value_load(tabs[0:1, bass.ds(b * NPG + g, 1)], min_val=0, max_val=A["lf"].shape[0] - 1)
                    sp.dma_start(plf[:, bass.ds(b, 1), g, :], A["lf"][bass.ds(pg, 1)].rearrange("a p h -> p a h")).then_inc(S["plf_in"], 16)
            sp.wait_ge(S["fk_done"], NPAIR)
            sp.wait_ge(S["lf_done"], 1)
            sp.dma_start(A["o_k"], fkT[:]).then_inc(S["k_out"], 16)
            sp.dma_start(A["o_lf"], lf[:]).then_inc(S["lf_out"], 16)

            sp.wait_ge(S["nF_ready"], 1)
            sp.dma_start(A["nF"], negF[:, 0:SEQ]).then_inc(S["nF_out"], 16)

            def keys(n):
                s, b, c, ph = slab[0], n // NPG, n % NPG // 2, n % 2
                sp.wait_ge(S["w_split"], s - RAW + 1)
                for i in range(2):
                    pg = page_of(b * NPG + 2 * c + i)
                    sp.dma_start(raw[:, s % RAW, i * SEQ:(i + 1) * SEQ].unsqueeze(1),
                                 A["kc"][bass.ds(pg, 1)][:, :, ph * SEQ:(ph + 1) * SEQ].rearrange("a p n -> p a n"))\
                        .then_inc(S[f"k_in{s % RAW}"], 16)
                slab[0] += 1

            def values(v):
                b, half, q = v // NPG, v % NPG // 4, v % 4
                if v >= VR:
                    sp.wait_ge(S["v_lo_ready"], v - VR + 1)
                for i in range(2):
                    pg = page_of(b * NPG + 2 * q + i)
                    sp.dma_start(vraw[:, v % VR, i * SEQ:(i + 1) * SEQ].unsqueeze(1),
                                 A["vc"][bass.ds(pg, 1)][:, :, half * SEQ:(half + 1) * SEQ].rearrange("a p n -> p a n"))\
                        .then_inc(S[f"v_in{v % VR}"], 16)

            for t in range(UNITS + VLAG + 1):
                if t < UNITS:
                    keys(t)
                if t == VLAG + 1:
                    wait_tile(sp, (W_Q + 8) * SLAB)
                if t >= VLAG + 1:
                    values(t - VLAG - 1)
            weights(8)
            weights(66)
            sp.wait_ge(S["x_done"], 8 * (RH + 2 + 1 + 2))
            sp.dma_start(A["o_x"], x[:]).then_inc(S["y_out"], 16)
            sp.wait_ge(S["y_out"], 16)
            sp.wait_ge(S["nF_out"], 16)
            sp.wait_ge(S["k_out"], 16)
            sp.wait_ge(S["lf_out"], 16)
            sp.wait_ge(S["st_saved0"], 16 * RH * DEC_B // 2)
            sp.wait_ge(S["st_saved1"], 16 * RH * DEC_B // 2)
            sp.wait_ge(S["sp_saved"], 16 * 2 * RH)
            sp.wait_ge(S["fv_saved0"], 16 * NPAIR // 2)
            sp.wait_ge(S["fv_saved1"], 16 * NPAIR // 2)

        @block.gpsimd
        def _(g):
            nc.gpsimd.memset(ones[:], 1.0).then_inc(S["hi_split"], 1)
            g.wait_ge(S["hi_split"], 1)
            unit = ones[:, 0:1].to_broadcast([P, SLAB * P])

            def split(s, slot, ring):
                nc.gpsimd.tensor_tensor(w_hi[:, slot, :], raw[:, ring, :], unit, ALU.mult).then_inc(S["hi_split"], 1)
                g.wait_ge(S["hi_split"], s + 2)
                nc.gpsimd.tensor_tensor(w_lo[:, slot, :], raw[:, ring, :], w_hi[:, slot, :].bitcast(F32),
                                        ALU.subtract).then_inc(S["w_split"], 1)

            def weight(s, ring, uses):
                g.wait_ge(S[f"raw_in{ring}"], 16 * uses)
                split(s, ring % SPL, ring)

            for s in range(RAW):
                if s >= SPL:
                    g.wait_ge(S["w_tiles"], SLAB * (s - SPL + 1))
                weight(s, s, 1)
            with nc.gpsimd.Fori(1, W_PAST // RAW) as i:
                for r in range(RAW):
                    g.wait_ge(S["w_tiles"], (i * RAW + r - SPL + 1) * SLAB)
                    weight(i * RAW + r, r, i + 1)
            for s in range(W_PAST // RAW * RAW, W_PAST):
                g.wait_ge(S["w_tiles"], SLAB * (s - SPL + 1))
                weight(s, s % RAW, s // RAW + 1)
            with nc.gpsimd.Fori(0, UNITS // RAW) as i:
                for r in range(RAW):
                    s = i * RAW + (W_PAST + r)
                    ring = (W_PAST + r) % RAW
                    g.wait_ge(S["w_tiles"], (s - SPL + 1) * SLAB)
                    g.wait_ge(S[f"k_in{ring}"], 32 * (i + 1))
                    split(s, ring % SPL, ring)
            for s in range(W_O, W_ALL):
                g.wait_ge(S["w_tiles"], SLAB * (s - SPL + 1))
                weight(s, s % RAW, (s - UNITS) // RAW + 1)

        @block.tensor
        def _(pe):
            mm = nc.tensor.matmul
            tiles = [0]
            tile_no = [0]
            chain = [0]
            msq = [0]

            def project(n, ktiles, hi, lo, ready=None):
                for i in range(n):
                    f = tile_no[0]
                    if f >= 2:
                        pe.wait_ge(pair_free(f), f // 2)
                    for k in range(ktiles):
                        t = tiles[0]
                        s = t // SLAB
                        if k == 0 or t % SLAB == 0:
                            pe.wait_ge(S["w_split"], s + 1)
                        if ready and i == 0:
                            pe.wait_ge(S[ready[0]], ready[1] + k + 1)
                        c = (t % SLAB) * P
                        for half in range(2):
                            cols = slice(half * HALF, (half + 1) * HALF)
                            for j, (w, a) in enumerate(((w_lo, hi), (w_hi, lo), (w_hi, hi))):
                                last = mm(pj[f % 2][:, half, 0:HALF], w[:, s % SPL, c:c + P], a(k)[:, cols],
                                          start=k == 0 and j == 0, stop=k == ktiles - 1 and j == 2)
                        tiles[0] += 1
                        last.then_inc(S["w_tiles"], 1)
                    tile_no[0] += 1

            def from_h(n, ready=None):
                project(n, DT, lambda k: h_hi[:, k, :], lambda k: h_lo[:, k, :], ready)

            def modulation(first, n, bank, at=0):
                for m in range(first, first + n):
                    pe.wait_ge(S[f"m_in{m % MRING}"], 16 * (m // MRING + 1))
                    for k in range(DT):
                        last = mm(bank[:, (m - first + at) * NC:(m - first + at + 1) * NC], mraw[:, m % MRING, k * P:(k + 1) * P],
                                  cact[:, k, :], start=k == 0, stop=k == DT - 1)
                    last.then_inc(S["m_used"], 1)

            def sum_squares(src, n, wait_each, lhs=None):
                for k in range(n):
                    wait_each(k)
                    for half in range(2):
                        last = mm(bk[half][:, 0:HALF], lhs if lhs is not None else ones[:], src(k)[:, half * HALF:(half + 1) * HALF],
                                  start=k == 0, stop=k == n - 1)
                    if k < n - 1:
                        last.then_inc(S["osq_used"], 1)
                last.then_inc(S["ms_ready"], 1)

            def norm(z):
                def w(k):
                    pe.wait_ge(S["sq_ready"], z * DT + k + 1)
                sum_squares(lambda k: xs[:, k % 2, :], DT, w)

            def from_norm(z, n=1):
                from_h(1, ("h_ready", DT * z))
                from_h(n - 1)

            pe.wait_ge(S["cst_in"], 32)
            pe.wait_ge(S["hi_split"], 1)
            pe.wait_ge(S["c_ready"], 1)
            norm(0)
            modulation(0, MOD_FIRST, bk[3])
            from_norm(0, 12)

            for h in range(RH):
                last_head = h == RH - 1
                pe.wait_ge(S["v_evac"], h + 1)
                pe.wait_ge(S["rope_done"], 2 * h + 2)
                if h:
                    pe.wait_ge(S["sp_evac"], 2 * h)
                    pe.wait_ge(S["os_evac"], h)
                    pe.wait_ge(S["m_done"], 2 * h + 1)
                    pe.wait_ge(S["og_ready"], 4 * h)
                    pe.wait_ge(S["upd_done"], 16 * h)
                for e in range(8):
                    if e >= 4:
                        pe.wait_ge(S["tr_evac"], 8 * h + e - 3)
                    if e < 4:
                        for f in range(4):
                            last = nc.tensor.transpose(bk[e][:, f * P:(f + 1) * P], vT[:, f, e * P:(e + 1) * P], ident)
                    elif e == 4:
                        for f in range(4):
                            last = nc.tensor.transpose(bk[0][0:NS, f * P:(f + 1) * P], vT[:, f, SEQ:NT], ident)
                    elif e < 7:
                        for r in range(2):
                            rt = 2 * (e - 5) + r
                            for d in range(2):
                                c = r * DK + d * P
                                last = nc.tensor.transpose(bk[e - 4][:, c:c + P], kT[:, d, rt * P:(rt + 1) * P], ident)
                    else:
                        for d in range(2):
                            last = nc.tensor.transpose(bk[3][0:NS, d * P:(d + 1) * P], kT[:, d, SEQ:NT], ident)
                    last.then_inc(S["tr_ready"], 1)
                for j in range(RT):
                    pe.wait_ge(S["tr_evac"], 8 * h + 5 + j)
                    n = SEQ - j * P
                    for d in range(2):
                        last = mm(bk[j][:, 0:n], kT[:, d, j * P:(j + 1) * P], qT[:, d, j * P:SEQ], start=d == 0, stop=d == 1)
                    if j == RT - 1:
                        for d in range(2):
                            last = mm(bk[3][0:NS, P:P + NS], kT[:, d, SEQ:NT], qT[:, d, SEQ:NT], start=d == 0, stop=d == 1)
                    last.then_inc(S["scores_ready"], 1)
                pe.wait_ge(S["decayed"], 5 * h + 5)
                for i in range(DEC_B):
                    if not last_head:
                        from_h(1)
                    if i == 0:
                        for e in range(4):
                            mm(bk[0][:, e * NS:(e + 1) * NS], vs[:, e * P:(e + 1) * P], atts[:], start=e == 0, stop=False, skip_group_check=True)
                    n = h * DEC_B + i
                    pe.wait_ge(S[f"st_in{n % 2}"], 16 * (n // 2 + 1))
                    for e in range(4):
                        for d in range(2):
                            last = mm(bk[0][:, e * NS + i * DEC_T:e * NS + (i + 1) * DEC_T], st[:, n % 2, d, e * P:(e + 1) * P],
                                      qx[:, d, i * DEC_T:(i + 1) * DEC_T], start=False, stop=i == DEC_B - 1 and d == 1, skip_group_check=True)
                    if i == DEC_B - 1:
                        last.then_inc(S["os_ready"], 1)
                    pe.wait_ge(S["kb_ready"], n + 1)
                    for d in range(2):
                        if i:
                            pe.wait_ge(S["upd_done"], 2 * n + d - 1)
                        mm(bk[1 + d][:], kb[:, i % 2, d * P:(d + 1) * P], vs[:], start=True, stop=True).then_inc(S["upd_ready"], 1)
                    if 1 <= i <= 4:
                        e, at = i - 1, 0
                        if e:
                            pe.wait_ge(S["o_evac"], 4 * h + e)
                        for j in range(RT):
                            n = SEQ - j * P
                            last = mm(bk[3][:, j * P:SEQ], vtok[:, j, e * P:(e + 1) * P], att[:, at:at + n], start=j == 0, stop=j == RT - 1)
                            at += n
                        last.then_inc(S["o_ready"], 1)
                    if 5 <= i <= 6:
                        d = i - 5
                        pe.wait_ge(S["o_evac"], 4 * h + 4)
                        if d:
                            pe.wait_ge(S["sp_evac"], 2 * h + 1)
                        for rt in range(RT):
                            last = mm(bk[3][:], ktok[:, rt, d * P:(d + 1) * P], vtok[:, rt, :], start=rt == 0, stop=rt == RT - 1)
                        last.then_inc(S["sp_ready"], 1)
                pe.wait_ge(S["os_evac"], h + 1)
                pe.wait_ge(S["upd_done"], 16 * h + 16)

                def w(k):
                    pe.wait_ge(S["osq_ready"], 4 * h + k + 1)
                sum_squares(lambda k: xs[:, k % 2, :], 4, w)
                pe.wait_ge(S["sp_evac"], 2 * h + 2)
                m = MOD_FIRST + h * MOD_PER_HEAD
                pe.wait_ge(S["m_done"], 2 * h + 1)
                for i in range(4):
                    if not last_head:
                        from_h(1)
                    modulation(m + 2 * i, 2, bk[3], 2 * i)
                for i in range(DT):
                    project(1, 4, lambda k: og_hi[:, k, :], lambda k: og_lo[:, k, :], ("og_ready", 4 * h) if i == 0 else None)
                    modulation(m + DT + 2 * i, 2, bk[2], 2 * i)

            def feed_forward(layer):
                for half in range(2):
                    u = 2 * layer + half
                    if half:
                        from_h(2 * FFT)
                    else:
                        from_norm(1 if layer == 0 else 4, 2 * FFT)
                    project(1, FFT, lambda k: hid_hi[:, k, :], lambda k: hid_lo[:, k, :], ("hid_ready", FFT * u))
                    project(DT - 1, FFT, lambda k: hid_hi[:, k, :], lambda k: hid_lo[:, k, :])

            norm(1)
            feed_forward(0)

            BD = cst[:, C_BD:C_BD + P]
            norm(2)

            def head_norm(k):
                pe.wait_ge(S["fk_sq"], k + 1)
                for half in range(2):
                    last = mm(bk[half][:, 0:HALF], BD, xs[:, k % 2, half * HALF:(half + 1) * HALF], start=True, stop=True)
                last.then_inc(S["ms_ready"], 1)

            for p in range(NPAIR):
                if p:
                    from_h(1)
                else:
                    from_norm(2)
                if p:
                    pe.wait_ge(S["var_ready"], 3 + RH + p - 1)
                    head_norm(p - 1)
            pe.wait_ge(S["var_ready"], 3 + RH + NPAIR - 1)
            head_norm(NPAIR - 1)

            def v_rows(p):
                pe.wait_ge(S["fv_raw"], p + 1)
                if p:
                    pe.wait_ge(S["fvt_evac"], p)
                for rt in range(RT):
                    nc.tensor.transpose(bk[2][:, rt * P:(rt + 1) * P], fraw[:, p % 2, rt * P:(rt + 1) * P], ident)
                nc.tensor.transpose(bk[3][0:NS, 0:P], fraw[:, p % 2, SEQ:NT], ident).then_inc(S["fvt_ready"], 1)

            for p in range(NPAIR):
                from_h(1)
                if p:
                    v_rows(p - 1)
            from_h(1)
            v_rows(NPAIR - 1)

            norm(3)
            for p in range(NPAIR):
                if p:
                    from_h(1)
                else:
                    from_norm(3)
                if p:
                    pe.wait_ge(S["var_ready"], 4 + RH + NPAIR + p - 1)
                    head_norm(NPAIR + p - 1)
            pe.wait_ge(S["var_ready"], 4 + RH + 2 * NPAIR - 1)
            head_norm(2 * NPAIR - 1)

            pe.wait_ge(S["suf_ready"], 1)
            pe.wait_ge(S["fvt_evac"], NPAIR)
            half_b = DEC_B // 2
            for i in range(2):
                o = bk[2 + i][:].rearrange("p (b g h) -> p b g h", b=half_b, g=NPG)
                mm(o, cst[:, C_US:C_US + P], plf[:, i * half_b:(i + 1) * half_b], start=True, stop=False)
                mm(o, ones[:], suf[:, i * half_b:(i + 1) * half_b], start=False, stop=True).then_inc(S["R_psum"], 1)
            pe.wait_ge(S["R_done"], 2)
            pe.wait_ge(S["nF_ready"], 1)
            nc.tensor.transpose(bk[2][0:NS, 0:FH], negF[:, SEQ:NT], cst[0:FH, C_ID:C_ID + FH]).then_inc(S["nFs_psum"], 1)

            pe.wait_ge(S["fk_done"], 2 * NPAIR)
            pe.wait_ge(S["idb_ready"], 2)
            pe.wait_ge(S["nFs_ready"], 1)
            pe.wait_ge(S["qbd_ready"], 2 * NPAIR + 1)
            for p in range(NPAIR):
                last = mm(bk[3][0:NS, p * 64:(p + 1) * 64], fkT[:, p, SEQ:NT], qbd[:, p], start=True, stop=True)
            last.then_inc(S["sn_psum"], 1)

            def score(t):
                h, qb = t // RT, t % RT
                r = (h % 2) * HD
                if t >= 2:
                    pe.wait_ge(S["s_max"], t - 1)
                n = (qb + 1) * P
                mm(pj[0][:, t % 2, 0:n], fqT[r:r + HD, h // 2, qb * P:n], fkT[r:r + HD, h // 2, 0:n], start=True, stop=False)
                mm(pj[0][:, t % 2, qb * P:n], idb[:], cmb[:], start=False, stop=True).then_inc(S["s_psum"], 1)

            def turn(t):
                pe.wait_ge(S["p_done"], t + 1)
                if t >= 2:
                    pe.wait_ge(S["pT_ready"], t - 1)
                for k in range(t % RT + 1):
                    last = nc.tensor.transpose(pj[1][:, t % 2, k * P:(k + 1) * P], pr[:, t % 4, k * P:(k + 1) * P], ident)
                last.then_inc(S["pT_psum"], 1)

            def weigh(t):
                h, qb = t // RT, t % RT
                r = (h % 2) * HD
                pe.wait_ge(S["pT_ready"], t + 1)
                if qb == 0 and h:
                    pe.wait_ge(S["fo_done"], h)
                for k in range(qb + 1):
                    last = mm(bk[0][r:r + HD, qb * P:(qb + 1) * P], fv[:, k, h * HD:(h + 1) * HD], pT[:, t % 2, k * P:(k + 1) * P],
                              start=k == 0, stop=k == qb)
                last.then_inc(S["fo_psum"], 1)

            def past_scores(n):
                b, c, ph = n // NPG, n % NPG // 2, n % 2
                s = tiles[0] // SLAB
                chunk = n // 2
                if n % NPG == 0:
                    pe.wait_ge(S["qd_ready"], b + 1)
                if ph == 0 and chunk:
                    pe.wait_ge(S["ks_out"], chunk)
                pe.wait_ge(S["w_split"], s + 1)
                if ph:
                    pe.wait_ge(S["Rx_ready"], chunk + 1)
                    for i in range(2):
                        mm(bk[1][0:64, i * P:(i + 1) * P], Rx[:, chunk % 2, i, :], ident, start=False, stop=False)
                for i in range(NPAIR // 2):
                    p = ph * NPAIR // 2 + i
                    for j, (q, w) in enumerate(((qd_lo, w_hi), (qd_hi, w_lo), (qd_hi, w_hi))):
                        keys = w[:, s % SPL, :].rearrange("p (g a n) -> p g a n", g=2, a=NPAIR // 2)[:, :, i, :]
                        last = mm(bk[1][:, 0:256], q[:, p * P:(p + 1) * P], keys, start=p == 0 and j == 0, stop=p == NPAIR - 1 and j == 2)
                    last.then_inc(S["w_tiles"], 2)
                    tiles[0] += 2

            def new_scores(b):
                if b >= 1:
                    pe.wait_ge(S["pn_ready"], b)
                if b >= 2:
                    pe.wait_ge(S["so_done"], 4 * (b - 1))
                if b == 0:
                    pe.wait_ge(S["sn_done"], 2 * DEC_B)
                nc.tensor.transpose(bk[2][0:64, 0:NS], sn[:, b].rearrange("p a c t -> p (a c t)"),
                                    cst[0:NS, C_ID:C_ID + NS]).then_inc(S["snT_psum"], 1)

            def turn_weights(b):
                pe.wait_ge(S["dg_ready"], b + 1)
                pe.wait_ge(S["snT_out"], b + 1)
                if b >= 2:
                    pe.wait_ge(S["so_done"], 4 * (b - 2) + 2)
                for k in range(NPG):
                    last = mm(bk[2][:, k * 64:(k + 1) * 64], ss[b % 2][:, k * P:(k + 1) * P], dg[:], start=True, stop=True)
                last.then_inc(S["sT_psum"], 1)

            def turn_new(b):
                pe.wait_ge(S["sT_ready"], b + 1)
                mm(bk[2][0:NS, 0:64], ss[b % 2][:, PAST:PAST + NS], dg[:], start=True, stop=True).then_inc(S["pn_psum"], 1)

            def past_values(v):
                b, half, q = v // NPG, v % NPG // 4, v % 4
                if q == 0:
                    pe.wait_ge(S["sT_ready"], b + 1)
                    if v:
                        pe.wait_ge(S["so_out"], v // 4)
                pe.wait_ge(S["v_lo_ready"], v + 1)
                if q == 3:
                    pe.wait_ge(S["pn_ready"], b + 1)
                    mm(bk[3][0:64, :], pn[:, b % 2, :], fvs[:, half * SEQ:(half + 1) * SEQ], start=False, stop=False)
                for i in range(2):
                    for j, w in enumerate((v_lo, v_hi)):
                        last = mm(bk[3][:], sT[:, b % 2, 2 * q + i, :], w[:, v % 2, i * SEQ:(i + 1) * SEQ],
                                  start=q == 0 and i == 0 and j == 0, stop=q == 3 and i == 1 and j == 1)
                last.then_inc(S["v_used"], 1)

            def features_out(n):
                b, half = n // 2, n % 2
                pe.wait_ge(S["so_out"], n + 1)
                pe.wait_ge(S["pn_ready"], min(b + 1 + half, DEC_B))
                pe.wait_ge(S["snT_out"], min(b + 2, DEC_B))
                if n:
                    pe.wait_ge(S["so_done"], 2 * n)
                for i in range(NPAIR // 2):
                    p = half * NPAIR // 2 + i
                    last = mm(bk[2][:, i * 8:i * 8 + 8], so[:, i * P:(i + 1) * P], cst[:, C_FO + p * 8:C_FO + p * 8 + 8],
                              start=True, stop=True)
                last.then_inc(S["back_psum"], 1)

            for t in range(STEPS):
                b, g = t // NPG, t % NPG
                if t < TQ:
                    score(t)
                if 0 <= t - 2 < TQ:
                    turn(t - 2)
                if 0 <= t - 4 < TQ:
                    weigh(t - 4)
                if t < UNITS:
                    past_scores(t)
                    if g == 6:
                        new_scores(b)
                if 1 <= b <= DEC_B:
                    if g == 2:
                        turn_weights(b - 1)
                    if g == 3:
                        turn_new(b - 1)
                if 0 <= t - VLAG < UNITS:
                    past_values(t - VLAG)
                if t > VLAG and (t - VLAG) % 4 == 0:
                    features_out((t - VLAG) // 4 - 1)

            from_h(1, ("fo_ready", 0))
            from_h(NPAIR - 1)
            norm(4)
            feed_forward(1)

        @block.scalar
        def _(act):
            chain = [0]

            def fn(out, in_, f, **kw):
                return nc.scalar.activation(out, in_, f, **kw)

            def root():
                c = chain[0]
                act.wait_ge(S["var_ready"], c + 1)
                fn(rstd[:], var[:], ACT.Ln).then_inc(S["ln_done"], 1)
                act.wait_ge(S["ln_done"], c + 1)
                fn(rstd[:], rstd[:], ACT.Exp, scale=-0.5).then_inc(S["r_exp"], 1)
                chain[0] += 1

            def norm(z, shift):
                for k in range(DT):
                    if z:
                        act.wait_ge(S["x_done"], x_done_before[z] + k + 1)
                    else:
                        act.wait_ge(S["x_in"], 16)
                    if k >= 2:
                        act.wait_ge(S["osq_used"], osq_before[z] + k - 1)
                    elif z:
                        act.wait_ge(S["ms_ready"], chain[0])
                    fn(xs[:, k % 2, :], x[:, k, :], ACT.Square).then_inc(S["sq_ready"], 1)
                root()
                act.wait_ge(S["gains"], z + 1)
                for k in range(DT):
                    act.wait_ge(S["scaled"], z * DT + k + 1)
                    if z * DT + k >= 2:
                        act.wait_ge(S["h_ready"], z * DT + k - 1)
                    fn(hf[:, k % 2, 0:SEQ], xs[:, k % 2, 0:SEQ], ACT.Identity, scale=gain[:, k, 0:1],
                       bias=mod[:, shift + k, 0:1]).then_inc(S["hmod"], 1)
                    act.wait_ge(S["hmod"], z * DT + k + 1)
                    act.wait_ge(S["hsample"], z * DT + k + 1)
                    fn(h_hi[:, k, :], hf[:, k % 2, :], ACT.Copy).then_inc(S["hi_ready"], 1)

            x_done_before = [0, 8 * RH - 8, 8 * (RH + 2) - 8, 8 * (RH + 2) - 8, 8 * (RH + 3) - 8]
            osq_before = [0, 7 + 3 * RH, 14 + 3 * RH, 21 + 3 * RH, 28 + 3 * RH]

            def free(n, ins):
                ins.then_inc(pair_free(n), 1)

            act.wait_ge(S["c_in"], 16)
            fn(ctmp[:], cact[:], ACT.Exp, scale=-1.0).then_inc(S["c_exp"], 1)
            norm(0, 0)

            def value_out(h, f):
                wait_tile(act, (ret_proj_slab(h) + 5 + f) * SLAB)
                if h and f == 0:
                    act.wait_ge(S["tr_ready"], 8 * h)
                n = ret_proj_tile(h) + 4 + f
                free(n, fn(two(vT[:, f, :]), pj[f % 2][:, :, 0:HALF], ACT.Copy))
                if f == 3:
                    act.wait_ge(pair_free(0), (n - 1) // 2 + 1)
                    act.wait_ge(pair_free(1), n // 2 + 1)
                    act.sem_inc(S["v_evac"], 1)

            def gates(h):
                for f in range(4):
                    n = 4 * h + f
                    wait_tile(act, ret_proj_slab(h) * SLAB + (9 + f) * SLAB)
                    if n >= 2:
                        act.wait_ge(S["silu_done"], n - 1)
                    fn(two(hf[:, f % 2, :]), pj[f % 2][:, :, 0:HALF], ACT.Exp, scale=-1.0).then_inc(S["silu_exp"], 1)

            act.wait_ge(S["h_ready"], DT)
            for f in range(4):
                value_out(0, f)
            gates(0)
            act.wait_ge(S["rc_in"], 16)
            for h in range(RH):
                last_head = h == RH - 1
                for e in range(8):
                    act.wait_ge(S["tr_ready"], 8 * h + e + 1)
                    if e < 4:
                        last = fn(vtok[:, e, :], bk[e][:], ACT.Copy)
                    elif e == 4:
                        last = fn(vs[:], bk[0][0:NS, :], ACT.Copy)
                    elif e < 7:
                        for r in range(2):
                            rt = 2 * (e - 5) + r
                            last = fn(ktok[:, rt, :], bk[e - 4][:, r * DK:(r + 1) * DK], ACT.Copy,
                                      scale=rc[:, R_KP + h * RT + rt:R_KP + h * RT + rt + 1])
                    else:
                        last = fn(ks[:], bk[3][0:NS, 0:DK], ACT.Copy)
                    last.then_inc(S["tr_evac"], 1)
                def o_out(e):
                    act.wait_ge(S["o_ready"], 4 * h + e + 1)
                    if h and e == 0:
                        act.wait_ge(S["og_ready"], 4 * h)
                    fn(oT[:, e, 0:SEQ], bk[3][:], ACT.Copy).then_inc(S["o_evac"], 1)

                def state_out(d):
                    n = 2 * h + d
                    act.wait_ge(S["silu_done"], 4 * h + 4)
                    act.wait_ge(S["sp_ready"], n + 1)
                    if n:
                        act.wait_ge(S["sp_saved"], 16 * n)
                    fn(hf[:, 0, 0:DV], bk[3][:], ACT.Copy).then_inc(S["sp_evac"], 1)
                    act.wait_ge(S["sp_evac"], n + 1)
                    act.dma_start(A["st_p"][h, :, d, :], hf[:, 0, 0:DV]).then_inc(S["sp_saved"], 16)

                for e in range(3):
                    o_out(e)
                for f in range(4):
                    if not last_head:
                        value_out(h + 1, f)
                    if f == 0:
                        o_out(3)
                    if f in (1, 2):
                        state_out(f - 1)
                act.wait_ge(S["os_ready"], h + 1)
                fn(oT[:, :, SEQ:NT], bk[0][:, 0:4 * NS].rearrange("p (e n) -> p e n", e=4), ACT.Copy).then_inc(S["os_evac"], 1)
                act.wait_ge(S["os_evac"], h + 1)
                for e in range(4):
                    if e >= 2:
                        act.wait_ge(S["osq_used"], 7 + 3 * h + e - 1)
                    elif True:
                        act.wait_ge(S["ms_ready"], chain[0])
                    fn(xs[:, e % 2, :], oT[:, e, :], ACT.Square).then_inc(S["osq_ready"], 1)
                root()
                for e in range(4):
                    act.wait_ge(S["gated"], 4 * h + e + 1)
                    if h and e == 0:
                        wait_tile(act, tiles_after_out(h - 1))
                    fn(og_hi[:, e, :], oT[:, e, :], ACT.Copy).then_inc(S["og_hi_ready"], 1)
                if not last_head:
                    act.wait_ge(S["sp_saved"], 16 * 2 * (h + 1))
                    gates(h + 1)

            act.wait_ge(S["sp_saved"], 16 * 2 * RH)
            states_saved(act)

            def feed_forward(layer):
                for half in range(2):
                    u = 2 * layer + half
                    base = ff_slab(layer, half) * SLAB
                    for m in range(FFT):
                        n = u * FFT + m
                        wait_tile(act, base + (2 * m + 1) * SLAB)
                        if n >= 2:
                            act.wait_ge(S["hid_full"], n - 1)
                        fn(two(sig[:, n % 2, :]), pj[(ff_tile(layer, half) + 2 * m) % 2][:, :, 0:HALF], ACT.Exp, scale=-1.0)\
                            .then_inc(S["silu_exp"], 1)
                        if m:
                            hidden_hi(n - 1, m - 1, u)
                    hidden_hi(u * FFT + FFT - 1, FFT - 1, u)

            def hidden_hi(n, m, u):
                act.wait_ge(S["hid_full"], n + 1)
                if m == 0 and u:
                    wait_tile(act, ff_done_tiles(u - 1))
                fn(hid_hi[:, m, :], hid[:, n % 2, :], ACT.Copy).then_inc(S["hid_hi_ready"], 1)

            norm(1, 3 * DT)
            feed_forward(0)
            norm(2, 12 * DT)

            def head_tile(k, tile, slab):
                wait_tile(act, (slab + 1) * SLAB)
                if k >= 2:
                    act.wait_ge(S["fk_done"], k - 1)
                fn(two(fraw[:, k % 2, :]), pj[tile % 2][:, :, 0:HALF], ACT.Copy).then_inc(S["fk_raw"], 1)
                if k % NPAIR < 2:
                    act.wait_ge(S["h_ready"], DT * (3 if k < NPAIR else 4))
                if k % NPAIR:
                    act.wait_ge(S["ms_ready"], chain_at_head(k))
                free(tile, fn(two(xs[:, k % 2, :]), pj[tile % 2][:, :, 0:HALF], ACT.Square))
                act.wait_ge(pair_free(tile), tile // 2 + 1)
                act.sem_inc(S["fk_sq"], 1)

            def chain_at_head(k):
                first = 3 + RH if k < NPAIR else 4 + RH + NPAIR
                return first + max(k % NPAIR - 1, 0)

            for p in range(NPAIR):
                head_tile(p, T_KV + p, W_KV + p)
                if p:
                    root()
            root()
            def rows_out(p):
                act.wait_ge(S["fvt_ready"], p + 1)
                fn(fv[:, :, p * P:(p + 1) * P], bk[2][:].rearrange("p (r c) -> p r c", r=RT), ACT.Copy)
                fn(fvs[:, p * P:(p + 1) * P], bk[3][0:NS, 0:P], ACT.Copy).then_inc(S["fvt_evac"], 1)

            for p in range(NPAIR):
                tile = T_KV + NPAIR + p
                wait_tile(act, (W_KV + NPAIR + p + 1) * SLAB)
                if p < 2:
                    act.wait_ge(S["fk_done"], NPAIR)
                else:
                    act.wait_ge(S["fvt_ready"], p - 1)
                    act.wait_ge(S[f"fv_saved{p % 2}"], 16 * (p // 2))
                free(tile, fn(two(fraw[:, p % 2, :]), pj[tile % 2][:, :, 0:HALF], ACT.Copy))
                act.wait_ge(pair_free(tile), tile // 2 + 1)
                act.sem_inc(S["fv_raw"], 1)
                act.dma_start(A["o_v"][:, p, :], fraw[:, p % 2, :]).then_inc(S[f"fv_saved{p % 2}"], 16)
                if p:
                    rows_out(p - 1)
            rows_out(NPAIR - 1)
            act.wait_ge(S["lf_raw"], 1)
            fn(lfa[:, 1, :], lfa[:, 1, :], ACT.Exp, scale=-1.0).then_inc(S["lf_exp"], 1)
            act.wait_ge(S["fv_saved0"], 16 * (NPAIR // 2))
            act.wait_ge(S["fv_saved1"], 16 * (NPAIR // 2))

            norm(3, 6 * DT)
            for p in range(NPAIR):
                head_tile(NPAIR + p, T_Q + p, W_Q + p)
                if p:
                    root()
            root()
            for i in range(2):
                act.wait_ge(S["R_psum"], i + 1)
                fn(Rb[:, i * DEC_B // 2:(i + 1) * DEC_B // 2].rearrange("p b g h -> p (b g h)"), bk[2 + i][:], ACT.Copy).then_inc(S["R_done"], 1)
            act.wait_ge(S["nFs_psum"], 1)
            fn(nFs[:], bk[2][0:NS, 0:FH], ACT.Copy).then_inc(S["nFs_ready"], 1)

            def bias_in(h):
                if h >= 2:
                    act.wait_ge(S["s_max"], RT * (h - 1))
                act.dma_start(bias[:, h % 2, :], A["nF"][h:h + 1, :].to_broadcast([P, SEQ])).then_inc(S[f"bias_in{h % 2}"], 16)

            def expo(t):
                n = (t % 4 + 1) * P
                act.wait_ge(S["s_max"], t + 1)
                fn(pr[:, t % 4, 0:n], pr[:, t % 4, 0:n], ACT.Exp, bias=nmx[:, t:t + 1], accum_out=rs[:, t:t + 1]).then_inc(S["p_exp"], 1)

            def turned_out(t):
                n = (t % RT + 1) * P
                act.wait_ge(S["pT_psum"], t + 1)
                if t >= 2:
                    act.wait_ge(S["fo_psum"], t - 1)
                fn(pT[:, t % 2, 0:n], pj[1][:, t % 2, 0:n], ACT.Copy).then_inc(S["pT_ready"], 1)

            def head_out(h):
                r = (h % 2) * HD
                act.wait_ge(S["fo_psum"], RT * h + RT)
                fn(foT[r:r + HD, h // 2, 0:SEQ], bk[0][r:r + HD, :], ACT.Copy).then_inc(S["fo_done"], 1)

            def diag(ap):
                return ap.rearrange("p (a n) -> p a n", n=P + 8)[:, :, 0:8]

            def queries_hi(b):
                if b:
                    wait_tile(act, (W_PAST + NPG * b) * SLAB)
                fn(diag(qd_hi[:]), qbd[:, :, b, :], ACT.Copy).then_inc(S["qd_hi_ready"], 1)

            def values_hi(v):
                act.wait_ge(S[f"v_in{v % VR}"], 32 * (v // VR + 1))
                if v >= 2:
                    act.wait_ge(S["v_used"], v - 1)
                fn(v_hi[:, v % 2, :], vraw[:, v % VR, :], ACT.Copy).then_inc(S["v_hi_ready"], 1)

            def sample_exp(b):
                act.wait_ge(S["sm_ready"], b + 1)
                w = ss[b % 2]
                fn(w[:], w[:], ACT.Exp, bias=nm[:, b:b + 1], accum_out=ls[:, b:b + 1]).then_inc(S["s_exp"], 1)

            def weights_hi(b):
                act.wait_ge(S["sT_psum"], b + 1)
                if b >= 2:
                    act.wait_ge(S["v_used"], NPG * (b - 1))
                fn(sT[:, b % 2, :, 0:64], bk[2][:].rearrange("p (k n) -> p k n", n=64), ACT.Copy).then_inc(S["sT_hi"], 1)

            def new_weights(b):
                act.wait_ge(S["pn_psum"], b + 1)
                fn(pn[:, b % 2, :], bk[2][0:NS, 0:64], ACT.Copy).then_inc(S["pn_ready"], 1)

            def sums_out(n):
                act.wait_ge(S["v_used"], 4 * (n + 1))
                if n:
                    act.wait_ge(S["back_psum"], n)
                fn(so[:], bk[3][:], ACT.Copy).then_inc(S["so_out"], 1)

            act.wait_ge(S["nF_out"], 16)
            act.wait_ge(S["fk_done"], 2 * NPAIR)
            bias_in(0)
            bias_in(1)
            act.wait_ge(S["qd_zero"], 2)
            act.wait_ge(S["qbd_ready"], 2 * NPAIR + 1)
            for t in range(STEPS):
                b, g = t // NPG, t % NPG
                if g == 0 and b < DEC_B:
                    queries_hi(b)
                if t < TQ:
                    expo(t)
                if 0 <= t - 2 < TQ:
                    turned_out(t - 2)
                if t >= 7 and (t - 7) % RT == 0 and (t - 7) // RT < FH:
                    head_out((t - 7) // RT)
                if t % RT == RT - 1 and t // RT + 2 < FH:
                    bias_in(t // RT + 2)
                if 1 <= b <= DEC_B:
                    if g == 0:
                        sample_exp(b - 1)
                    if g == 2:
                        weights_hi(b - 1)
                    if g == 3:
                        new_weights(b - 1)
                if 0 <= t - VLAG + 1 < UNITS:
                    values_hi(t - VLAG + 1)
                if t >= VLAG and (t - VLAG) % 4 == 3:
                    sums_out((t - VLAG) // 4)
            act.wait_ge(S["so_done"], 4 * DEC_B)
            for p in range(NPAIR):
                fn(h_hi[:, p, :], foT[:, p, :], ACT.Copy).then_inc(S["fo_hi_ready"], 1)
            keys_saved(act)
            norm(4, 9 * DT)
            feed_forward(1)

        @block.vector
        def _(dve):
            V = nc.vector
            links = [0]

            def link(ins):
                links[0] += 1
                ins.then_inc(S["dve_chain"], 1)
                dve.wait_ge(S["dve_chain"], links[0])

            chain = [0]

            def variance(scale):
                c = chain[0]
                dve.wait_ge(S["ms_ready"], c + 1)
                for half in range(2):
                    i = V.tensor_scalar(var[:, half * HALF:(half + 1) * HALF], bk[half][:, 0:HALF], scale, EPS, ALU.mult, ALU.add)
                i.then_inc(S["var_ready"], 1)

            def refine():
                c = chain[0]
                dve.wait_ge(S["r_exp"], c + 1)
                link(V.tensor_tensor(newt[:], rstd[:], rstd[:], ALU.mult))
                link(V.tensor_tensor(newt[:], newt[:], var[:], ALU.mult))
                link(V.tensor_scalar(newt[:], newt[:], -0.5, 1.5, ALU.mult, ALU.add))
                link(V.tensor_tensor(rstd[:], rstd[:], newt[:], ALU.mult))
                chain[0] += 1

            def sample(ap):
                return ap.rearrange("p (b t) -> p b t", b=DEC_B)

            def over_t(ap):
                return ap.unsqueeze(2).to_broadcast([P, DEC_B, DEC_T])

            def norm(z, g, shift, scale):
                link(V.tensor_scalar(gain[:], mod[:, scale:scale + DT, :], 1.0, None, ALU.add))
                V.tensor_tensor(gain[:], gain[:], vec[:, g:g + DT].unsqueeze(2).to_broadcast([P, DT, NC]), ALU.mult).then_inc(S["gains"], 1)
                dve.wait_ge(S["gains"], z + 1)
                if z:
                    variance(1.0 / D)
                    refine()
                for k in range(DT + 1):
                    if k < DT:
                        if k >= 2:
                            dve.wait_ge(S["hmod"], z * DT + k - 1)
                        V.tensor_tensor(xs[:, k % 2, :], x[:, k, :], rstd[:], ALU.mult).then_inc(S["scaled"], 1)
                        dve.wait_ge(S["scaled"], z * DT + k + 1)
                        if z * DT + k >= 2:
                            dve.wait_ge(S["hi_ready"], z * DT + k - 1)
                            dve.wait_ge(S["h_ready"], z * DT + k - 1)
                        link(V.tensor_tensor(sample(hf[:, k % 2, SEQ:NT]), sample(xs[:, k % 2, SEQ:NT]), over_t(gain[:, k, 1:NC]), ALU.mult))
                        V.tensor_tensor(sample(hf[:, k % 2, SEQ:NT]), sample(hf[:, k % 2, SEQ:NT]), over_t(mod[:, shift + k, 1:NC]), ALU.add)\
                            .then_inc(S["hsample"], 1)
                    if k:
                        dve.wait_ge(S["hi_ready"], z * DT + k)
                        V.tensor_tensor(h_lo[:, k - 1, :], hf[:, (k - 1) % 2, :], h_hi[:, k - 1, :].bitcast(F32), ALU.subtract)\
                            .then_inc(S["h_ready"], 1)

            def residual(tile, done, gate_at):
                for k in range(DT):
                    n = tile + k
                    wait_tile(dve, done(k))
                    ps = pj[n % 2]
                    link(V.scalar_tensor_tensor(out=x[:, k, 0:HALF], in0=ps[:, 0, 0:HALF], scalar=gain1[:, k, 0:1], in1=x[:, k, 0:HALF],
                                                op0=ALU.mult, op1=ALU.add))
                    link(V.scalar_tensor_tensor(out=x[:, k, HALF:SEQ], in0=ps[:, 1, 0:SEQ - HALF], scalar=gain1[:, k, 0:1], in1=x[:, k, HALF:SEQ],
                                                op0=ALU.mult, op1=ALU.add))
                    link(V.tensor_tensor(sample(newt[:, 0:NS]), sample(ps[:, 1, SEQ - HALF:HALF]), over_t(gain1[:, k, 1:NC]), ALU.mult))
                    V.tensor_tensor(x[:, k, SEQ:NT], x[:, k, SEQ:NT], newt[:, 0:NS], ALU.add).then_inc(S["x_done"], 1)
                    xn[0] += 1
                    dve.wait_ge(S["x_done"], xn[0])
                    dve.sem_inc(pair_free(n), 1)

            xn = [0]

            def gate_vector(g):
                link(V.tensor_scalar(gain1[:], mod[:, g:g + DT, :], 1.0, None, ALU.add))

            gain1 = ctmp

            def modulation_out(i, first, n, bank):
                dve.wait_ge(S["m_used"], first + n)
                V.tensor_tensor(mod[:, first:first + n, :], bank[:, 0:n * NC].rearrange("p (f c) -> p f c", c=NC),
                                vec[:, V_B + first:V_B + first + n].unsqueeze(2).to_broadcast([P, n, NC]), ALU.add).then_inc(S["m_done"], 1)
                dve.wait_ge(S["m_done"], i)

            dve.wait_ge(S["c_exp"], 1)
            dve.wait_ge(S["cst_in"], 32)
            link(V.tensor_scalar(ctmp[:], ctmp[:], 1.0, None, ALU.add))
            link(V.reciprocal(ctmp[:], ctmp[:]))
            V.tensor_tensor(cact[:], cact[:], ctmp[:], ALU.mult).then_inc(S["c_ready"], 1)
            variance(1.0 / D)
            refine()
            modulation_out(1, 0, MOD_FIRST, bk[3])
            norm(0, V_RET, 0, DT)

            def rope(h, i, dst, scale):
                wait_tile(dve, (ret_proj_slab(h) + 2 * i + 2) * SLAB)
                n = ret_proj_tile(h) + 2 * i
                a, b = pj[0][:, :, 0:HALF], pj[1][:, :, 0:HALF]
                cos, sin = two(rc[:, R_COS:R_COS + NT]), two(rc[:, R_SIN:R_SIN + NT])
                sine = two(newt[:])

                def times(out, ps, tab):
                    return V.scalar_tensor_tensor(out=out, in0=ps, scalar=scale, in1=tab, op0=ALU.mult, op1=ALU.mult)
                link(times(two(dst[:, 0, :]), a, cos))
                link(times(sine, b, sin))
                link(V.tensor_tensor(dst[:, 0, :], dst[:, 0, :], newt[:], ALU.subtract))
                link(times(two(dst[:, 1, :]), a, sin))
                link(times(sine, b, cos))
                V.tensor_tensor(dst[:, 1, :], dst[:, 1, :], newt[:], ALU.add).then_inc(S["rope_done"], 1)
                dve.wait_ge(S["rope_done"], 2 * h + i + 1)
                dve.sem_inc(S["pair_free0"], 1)
                dve.sem_inc(S["pair_free1"], 1)

            def cross(h):
                link(V.tensor_tensor(qx[:], qT[:, :, SEQ:NT],
                                     rc[:, R_CR + h * NS:R_CR + (h + 1) * NS].unsqueeze(1).to_broadcast([P, 2, NS]), ALU.mult))

            def silu(h):
                for f in range(4):
                    n = 4 * h + f
                    e = hf[:, f % 2, :]
                    dve.wait_ge(S["silu_exp"], n + 1)
                    link(V.tensor_scalar(e, e, 1.0, None, ALU.add))
                    link(V.reciprocal(e, e))
                    V.tensor_tensor(two(gate[:, f, :]), two(e), pj[f % 2][:, :, 0:HALF], ALU.mult).then_inc(S["silu_done"], 1)
                    dve.wait_ge(S["silu_done"], n + 1)
                    dve.sem_inc(pair_free(f), 1)

            dve.wait_ge(S["rc_in"], 16)
            rope(0, 0, qT, 1.0)
            rope(0, 1, kT, DK ** -0.5)
            silu(0)
            for h in range(RH):
                last_head = h == RH - 1
                if h:
                    dve.wait_ge(S["os_ready"], h)
                cross(h)
                at = 0
                for j in range(RT):
                    n = SEQ - j * P
                    dve.wait_ge(S["scores_ready"], 4 * h + j + 1)
                    dve.wait_ge(S[f"dec_in{h % 2}"], 16 * (h // 2 + 1))
                    if h and j == 0:
                        dve.wait_ge(S["o_ready"], 4 * h)
                    V.tensor_tensor(att[:, at:at + n], bk[j][:, 0:n], dec[:, h % 2, 0:n], ALU.mult).then_inc(S["decayed"], 1)
                    at += n
                V.tensor_tensor(atts[:], bk[3][0:NS, P:P + NS], rc[0:NS, R_DS + h * NS:R_DS + (h + 1) * NS], ALU.mult).then_inc(S["decayed"], 1)
                dve.wait_ge(S["tr_evac"], 8 * h + 8)
                for b in range(DEC_B):
                    n = h * DEC_B + b
                    if b == 1 and not last_head:
                        rope(h + 1, 0, qT, 1.0)
                    if b == 3 and not last_head:
                        rope(h + 1, 1, kT, DK ** -0.5)
                    if n >= 2:
                        dve.wait_ge(S["upd_ready"], 2 * (n - 1))
                    V.tensor_scalar(kb[:, b % 2, :], ks[:], rc[0:NS, R_KS + h * DEC_B + b:R_KS + h * DEC_B + b + 1], None, ALU.mult)\
                        .then_inc(S["kb_ready"], 1)
                    for d in range(2):
                        dve.wait_ge(S["upd_ready"], 2 * n + d + 1)
                        s = st[:, n % 2, d, :]
                        V.scalar_tensor_tensor(out=s, in0=s, scalar=rc[:, R_CD + h:R_CD + h + 1], in1=bk[1 + d][:], op0=ALU.mult, op1=ALU.add)\
                            .then_inc(S["upd_done"], 1)
                variance(1.0 / DV)
                refine()
                for e in range(4):
                    link(V.tensor_tensor(oT[:, e, :], oT[:, e, :], rstd[:], ALU.mult))
                    V.tensor_tensor(oT[:, e, :], oT[:, e, :], gate[:, e, :], ALU.mult).then_inc(S["gated"], 1)
                for e in range(4):
                    dve.wait_ge(S["og_hi_ready"], 4 * h + e + 1)
                    V.tensor_tensor(og_lo[:, e, :], oT[:, e, :], og_hi[:, e, :].bitcast(F32), ALU.subtract).then_inc(S["og_ready"], 1)
                if not last_head:
                    silu(h + 1)
                m = MOD_FIRST + h * MOD_PER_HEAD
                modulation_out(2 * h + 2, m, DT, bk[3])
                if h == 0:
                    gate_vector(2 * DT)
                residual(ret_out_tile(h), lambda k: ret_out_slab(h) * SLAB + 4 * (k + 1), 2 * DT)
                modulation_out(2 * h + 3, m + DT, 2 * DT, bk[2])

            def feed_forward(layer, g):
                gate_vector(g)
                for half in range(2):
                    u = 2 * layer + half
                    base = ff_slab(layer, half) * SLAB
                    t0 = ff_tile(layer, half)
                    for m in range(FFT):
                        n = u * FFT + m
                        e = sig[:, n % 2, :]
                        dve.wait_ge(S["silu_exp"], 4 * RH + n + 1)
                        link(V.tensor_scalar(e, e, 1.0, None, ALU.add))
                        link(V.reciprocal(e, e))
                        if n >= 2:
                            dve.wait_ge(S["hid_hi_ready"], n - 1)
                        link(V.tensor_tensor(two(hid[:, n % 2, :]), two(e), pj[(t0 + 2 * m) % 2][:, :, 0:HALF], ALU.mult))
                        dve.sem_inc(pair_free(t0 + 2 * m), 1)
                        wait_tile(dve, base + (2 * m + 2) * SLAB)
                        V.tensor_tensor(two(hid[:, n % 2, :]), two(hid[:, n % 2, :]), pj[(t0 + 2 * m + 1) % 2][:, :, 0:HALF], ALU.mult)\
                            .then_inc(S["hid_full"], 1)
                        dve.wait_ge(S["hid_full"], n + 1)
                        dve.sem_inc(pair_free(t0 + 2 * m + 1), 1)
                        dve.wait_ge(S["hid_hi_ready"], n + 1)
                        V.tensor_tensor(hid_lo[:, m, :], hid[:, n % 2, :], hid_hi[:, m, :].bitcast(F32), ALU.subtract).then_inc(S["hid_ready"], 1)
                    out0 = base + 2 * FFT * SLAB
                    residual(t0 + 2 * FFT, lambda k: out0 + FFT * (k + 1), g)

            states_saved(dve)
            norm(1, V_FFN, 3 * DT, 4 * DT)
            feed_forward(0, 5 * DT)
            norm(2, V_KV, 12 * DT, 13 * DT)

            def head_rows(k, dst, g):
                variance(1.0 / HD)
                refine()
                dve.wait_ge(S["fk_raw"], k + 1)
                V.scalar_tensor_tensor(out=dst, in0=fraw[:, k % 2, :], scalar=g, in1=rstd[:], op0=ALU.mult, op1=ALU.mult).then_inc(S["fk_done"], 1)

            for p in range(NPAIR):
                head_rows(p, fkT[:, p, :], vec[:, V_KN:V_KN + 1])

            n = T_KV + 2 * NPAIR
            wait_tile(dve, (W_KV + 17) * SLAB)
            z, u, s2, acc = (lfa[:, i, :] for i in range(4))
            link(V.tensor_scalar(two(z), pj[n % 2][0:FH, :, 0:HALF], vec[0:FH, V_BF:V_BF + 1], None, ALU.add))
            dve.sem_inc(pair_free(n), 1)
            link(V.tensor_scalar(u, z, -1.0, None, ALU.mult))
            V.tensor_tensor(u, u, z, ALU.max).then_inc(S["lf_raw"], 1)
            dve.wait_ge(S["lf_exp"], 1)
            link(V.tensor_scalar(s2, u, 2.0, None, ALU.add))
            link(V.reciprocal(s2, s2))
            link(V.tensor_tensor(u, u, s2, ALU.mult))
            link(V.tensor_tensor(s2, u, u, ALU.mult))
            link(V.tensor_scalar(acc, s2, 1.0 / 17, 1.0 / 15, ALU.mult, ALU.add))
            for odd in (13, 11, 9, 7, 5, 3, 1):
                link(V.tensor_tensor(acc, acc, s2, ALU.mult))
                link(V.tensor_scalar(acc, acc, 1.0 / odd, None, ALU.add))
            link(V.tensor_tensor(acc, acc, u, ALU.mult))
            link(V.tensor_scalar(z, z, 0.0, None, ALU.min))
            V.scalar_tensor_tensor(out=lf[:], in0=acc, scalar=-2.0, in1=z, op0=ALU.mult, op1=ALU.add).then_inc(S["lf_done"], 1)
            dve.wait_ge(S["lf_done"], 1)
            link(V.memset(lfa[:, 0, 0:SEQ], 1.0))
            link(V.tensor_tensor_scan(lfa[:, 1, 0:SEQ], lfa[:, 0, 0:SEQ], lf[:, 0:SEQ], 0.0, ALU.mult, ALU.add))
            link(V.tensor_copy(lfa[:, 1, SEQ:NT], lf[:, SEQ:NT]))
            run = lfa[:, 1, SEQ:NT].rearrange("p (b t) -> p b t", b=DEC_B)
            for t in range(1, DEC_T):
                link(V.tensor_tensor(run[:, :, t:t + 1], run[:, :, t:t + 1], run[:, :, t - 1:t], ALU.add))
            V.tensor_scalar(negF[:], lfa[:, 1, :], -1.0, None, ALU.mult).then_inc(S["nF_ready"], 1)
            dve.wait_ge(S["nF_ready"], 1)
            norm(3, V_ATT, 6 * DT, 7 * DT)
            for p in range(NPAIR):
                if p == 0:
                    link(V.tensor_scalar(m0[:], vec[:, V_QN:V_QN + 1], HD ** -0.5, None, ALU.mult))
                head_rows(NPAIR + p, fqT[:, p, :], m0[:])
            dve.wait_ge(S["plf_in"], 16 * DEC_B * NPG)
            link(V.memset(suf[:, :, NPG - 1, :], 0.0))
            for g in range(NPG - 2, -1, -1):
                link(V.tensor_tensor(suf[:, :, g, :], suf[:, :, g + 1, :], plf[:, :, g + 1, :], ALU.add))
            dve.sem_inc(S["suf_ready"], 1)
            V.tensor_copy(idb[:], ident).then_inc(S["idb_ready"], 1)
            V.tensor_copy(cmb[:], cst[:, C_CM:C_CM + P]).then_inc(S["idb_ready"], 1)

            dve.wait_ge(S["R_psum"], 2)
            V.tensor_scalar(qd_hi[:], ones[:, 0:1].to_broadcast([P, NPAIR * (P + 8)]), 0.0, None, ALU.mult).then_inc(S["qd_zero"], 1)
            V.tensor_scalar(qd_lo[:], ones[:, 0:1].to_broadcast([P, NPAIR * (P + 8)]), 0.0, None, ALU.mult).then_inc(S["qd_zero"], 1)
            V.memset(qbd[:], 0.0).then_inc(S["qbd_ready"], 1)
            dve.wait_ge(S["qbd_ready"], 1)
            for p in range(NPAIR):
                for j in range(2):
                    r = slice(j * HD, (j + 1) * HD)
                    V.tensor_copy(qbd[r, p, :, j * DEC_T:(j + 1) * DEC_T], sample(fqT[r, p, SEQ:NT])).then_inc(S["qbd_ready"], 1)

            def top(t):
                n = (t % 4 + 1) * P
                dve.wait_ge(S["s_psum"], t + 1)
                h = t // RT
                dve.wait_ge(S[f"bias_in{h % 2}"], 16 * (h // 2 + 1))
                if t >= 4:
                    dve.wait_ge(S["pT_psum"], t - 3)
                link(V.tensor_tensor_reduce(out=pr[:, t % 4, 0:n], in0=s_psum(t)[:, 0:n], in1=bias[:, (t // 4) % 2, 0:n], scale=1.0, scalar=-3e38,
                                            op0=ALU.add, op1=ALU.max, accum_out=mx[:, t:t + 1]))
                V.tensor_scalar(nmx[:, t:t + 1], mx[:, t:t + 1], -1.0, None, ALU.mult).then_inc(S["s_max"], 1)

            def s_psum(t):
                return pj[0][:, t % 2, :]

            def unit_sum(t):
                n = (t % 4 + 1) * P
                dve.wait_ge(S["p_exp"], t + 1)
                link(V.reciprocal(rsi[:, t:t + 1], rs[:, t:t + 1]))
                V.tensor_scalar(pr[:, t % 4, 0:n], pr[:, t % 4, 0:n], rsi[:, t:t + 1], None, ALU.mult).then_inc(S["p_done"], 1)

            dve.wait_ge(S["sn_psum"], 1)
            new = bk[3][0:NS, :].rearrange("p (a b c t) -> p b a c t", a=NPAIR, b=DEC_B, c=2)
            nf = nFs[:].rearrange("p (a c) -> p a c", c=2).unsqueeze(3).to_broadcast([NS, NPAIR, 2, DEC_T])
            for b in range(DEC_B):
                V.tensor_tensor(sn[:, b], new[:, b], nf, ALU.add).then_inc(S["sn_done"], 1)
                dve.wait_ge(S["sn_done"], 2 * b + 1)
                V.tensor_tensor(sn[:, b].rearrange("p a c t -> p (a c) t"), sn[:, b].rearrange("p a c t -> p (a c) t"),
                                cst[0:NS, C_NM + b * DEC_T:C_NM + (b + 1) * DEC_T].unsqueeze(1).to_broadcast([NS, FH, DEC_T]), ALU.add)\
                    .then_inc(S["sn_done"], 1)
            dve.wait_ge(S["sn_done"], 2 * DEC_B)

            def diag(ap):
                return ap.rearrange("p (a n) -> p a n", n=P + 8)[:, :, 0:8]

            def queries_lo(b):
                dve.wait_ge(S["qd_hi_ready"], b + 1)
                V.tensor_tensor(diag(qd_lo[:]), qbd[:, :, b, :], diag(qd_hi[:].bitcast(F32)), ALU.subtract).then_inc(S["qd_ready"], 1)

            def spread_sums(n):
                if n >= 2:
                    wait_tile(dve, (W_PAST + 2 * (n - 1)) * SLAB)
                V.tensor_copy(Rx[:, n % 2].rearrange("p g (h t) -> p g h t", t=DEC_T),
                              Rb[:, n // 4, 2 * (n % 4):2 * (n % 4) + 2, :].unsqueeze(3).to_broadcast([P, 2, FH, DEC_T])).then_inc(S["Rx_ready"], 1)

            def scores_out(n):
                c = n % 4
                wait_tile(dve, (W_PAST + 2 * (n + 1)) * SLAB)
                V.tensor_copy(ss[n // 4 % 2][:, c * 256:(c + 1) * 256], bk[1][0:64, 0:256]).then_inc(S["ks_out"], 1)

            def new_out(b):
                dve.wait_ge(S["snT_psum"], b + 1)
                V.tensor_copy(ss[b % 2][:, PAST:PAST + NS], bk[2][0:64, 0:NS]).then_inc(S["snT_out"], 1)

            def row_max(b):
                dve.wait_ge(S["snT_out"], b + 1)
                dve.wait_ge(S["ks_out"], 4 * b + 4)
                link(V.tensor_reduce(nm[:, b:b + 1], ss[b % 2][:], AX.X, ALU.max))
                V.tensor_scalar(nm[:, b:b + 1], nm[:, b:b + 1], -1.0, None, ALU.mult).then_inc(S["sm_ready"], 1)

            def row_sum(b):
                dve.wait_ge(S["s_exp"], b + 1)
                link(V.reciprocal(li[:, b:b + 1], ls[:, b:b + 1]))
                V.tensor_scalar(dg[:], cst[0:64, C_ID:C_ID + 64], li[:, b:b + 1], None, ALU.mult).then_inc(S["dg_ready"], 1)

            def weights_lo(b):
                dve.wait_ge(S["sT_hi"], b + 1)
                V.tensor_tensor(sT[:, b % 2, :, 64:128], bk[2][:].rearrange("p (k n) -> p k n", n=64),
                                sT[:, b % 2, :, 0:64].bitcast(F32), ALU.subtract).then_inc(S["sT_ready"], 1)

            def values_lo(v):
                dve.wait_ge(S["v_hi_ready"], v + 1)
                V.tensor_tensor(v_lo[:, v % 2, :], vraw[:, v % VR, :], v_hi[:, v % 2, :].bitcast(F32), ALU.subtract).then_inc(S["v_lo_ready"], 1)

            def heads_out(n):
                b, half = n // 2, n % 2
                dve.wait_ge(S["back_psum"], n + 1)
                for j in range(2):
                    r = slice(j * HD, (j + 1) * HD)
                    o = bk[2][r, 0:32].rearrange("p (a c t) -> p a c t", c=2, t=DEC_T)[:, :, j, :]
                    V.tensor_copy(foT[r, 4 * half:4 * half + 4, SEQ + b * DEC_T:SEQ + (b + 1) * DEC_T], o).then_inc(S["so_done"], 1)

            for t in range(STEPS + 1):
                b, g = t // NPG, t % NPG
                if g == 0 and b < DEC_B:
                    queries_lo(b)
                if 0 < t <= UNITS and t % 2 == 0:
                    scores_out(t // 2 - 1)
                if t < UNITS and t % 2 == 0:
                    spread_sums(t // 2)
                if t > VLAG + 1 and (t - VLAG - 1) % 4 == 0:
                    heads_out((t - VLAG - 1) // 4 - 1)
                if t < TQ:
                    top(t)
                if 0 <= t - 1 < TQ:
                    unit_sum(t - 1)
                if 1 <= b <= DEC_B:
                    if g == 0:
                        row_max(b - 1)
                    if g == 1:
                        row_sum(b - 1)
                    if g == 2:
                        weights_lo(b - 1)
                if b < DEC_B and g == 7:
                    new_out(b)
                if 0 <= t - VLAG + 1 < UNITS:
                    values_lo(t - VLAG + 1)
            dve.wait_ge(S["so_done"], 4 * DEC_B)
            for p in range(NPAIR):
                dve.wait_ge(S["fo_hi_ready"], p + 1)
                V.tensor_tensor(h_lo[:, p, :], foT[:, p, :], h_hi[:, p, :].bitcast(F32), ALU.subtract).then_inc(S["fo_ready"], 1)
            gate_vector(8 * DT)
            residual(T_O, lambda k: (W_O + k + 1) * SLAB, 8 * DT)
            keys_saved(dve)
            norm(4, V_FFN + DT, 9 * DT, 10 * DT)
            feed_forward(1, 11 * DT)


def weight_tiles(w):
    k, n = w.shape
    return w.reshape(k // P, P, n // P, P).transpose(2, 0, 1, 3).reshape(-1, P, P)


def slabs(tiles):
    t = np.concatenate(tiles, axis=0)
    return np.ascontiguousarray(t.reshape(-1, SLAB, P, P).transpose(0, 2, 1, 3)).reshape(-1, P, SLAB * P)


def columns(v):
    return v.reshape(-1, P).T


def feature_major(a):
    return a.T.reshape(-1, P, a.shape[0]).transpose(1, 0, 2)


def token_major(a, lo, hi):
    return a[:, :, lo:hi].transpose(2, 1, 0).reshape(hi - lo, -1)


def kernel(x_prompt, x_sample, cache_k, cache_v, cache_logf, state_ret, page_table, c_prompt, c_sample, w_mod, b_mod,
           ret_norm_g, w_ret_in, w_ret_out, attn_norm_g, w_q, q_norm_g, w_o, ffn_norm_g, w_ffn_in, w_ffn_out,
           kv_norm_g, w_kvmod, b_kvmod, w_kvf, b_f, k_norm_g):
    import concourse.bacc as bacc
    from concourse.bass_utils import run_bass_kernel_spmd

    a = {k: np.asarray(v) for k, v in dict(locals()).items() if k not in ("bacc", "run_bass_kernel_spmd")}
    win, wout = a["w_ret_in"][0], a["w_ret_out"][0]

    def head_in(h):
        cols = [win[:, h * DK:(h + 1) * DK], win[:, D + h * DK:D + (h + 1) * DK],
                win[:, 2 * D + h * DV:2 * D + (h + 1) * DV], win[:, 4 * D + h * DV:4 * D + (h + 1) * DV]]
        return weight_tiles(np.concatenate(cols, axis=1))

    def head_out(h):
        return weight_tiles(wout[h * DV:(h + 1) * DV])

    def ffn(l):
        w, wo, out = a["w_ffn_in"][l], a["w_ffn_out"][l], []
        for half in range(2):
            for m in range(half * FFT, (half + 1) * FFT):
                out.append(weight_tiles(w[:, m * P:(m + 1) * P]))
                out.append(weight_tiles(w[:, FF + m * P:FF + (m + 1) * P]))
            out.append(weight_tiles(wo[half * FFT * P:(half + 1) * FFT * P]))
        return out

    kvf = np.concatenate([a["w_kvf"], np.zeros((D, P - FH), np.float32)], axis=1)
    stream = [head_in(0)]
    for h in range(RH):
        if h < RH - 1:
            stream.append(head_in(h + 1))
        stream.append(head_out(h))
    stream += ffn(0) + [weight_tiles(kvf), weight_tiles(a["w_q"][0]), weight_tiles(a["w_o"][0])] + ffn(1)
    n_pool = a["cache_k"].shape[0]
    cst, rc, dec = constants()
    pad = np.concatenate([a["b_f"], np.zeros(P - FH, np.float32)])
    vec = np.concatenate([columns(v) for v in (
        a["b_mod"][0], a["b_mod"][1], a["b_kvmod"], a["ret_norm_g"][0], a["attn_norm_g"][0], a["ffn_norm_g"][0], a["ffn_norm_g"][1],
        a["kv_norm_g"], np.concatenate([a["q_norm_g"][0]] * 2), np.concatenate([a["k_norm_g"]] * 2), pad)], axis=1)
    ins = {
        "xT": feature_major(np.concatenate([a["x_prompt"][0], a["x_sample"].reshape(NS, D)], axis=0)),
        "cT": feature_major(np.concatenate([a["c_prompt"], a["c_sample"]], axis=0)),
        "w": slabs(stream),
        "wm": slabs([weight_tiles(a["w_mod"][0]), weight_tiles(a["w_mod"][1]), weight_tiles(a["w_kvmod"])]),
        "vec": vec, "cst": cst, "rc": rc, "dec": dec,
        "state": a["state_ret"][0].reshape(DEC_B, RH, 2, P, DV).transpose(1, 0, 3, 2, 4),
        "kc": a["cache_k"].reshape(n_pool, PAGE, NPAIR, P).transpose(0, 3, 2, 1).reshape(n_pool, P, D),
        "vc": a["cache_v"].reshape(n_pool, PAGE, D),
        "lf": a["cache_logf"],
        "table": a["page_table"].reshape(1, -1),
    }
    outs = {"o_x": (P, DT, NT), "o_k": (P, NPAIR, NT), "o_v": (P, NPAIR, NT), "o_lf": (FH, NT),
            "st_p": (RH, P, 2, DV), "st_s": (RH, DEC_B, P, 2, DV)}
    nc = bacc.Bacc("TRN2", target_bir_lowering=False, num_devices=1)
    A, arrays = {}, {}
    for name, v in ins.items():
        v = np.ascontiguousarray(v)
        arrays[f"in_{name}"] = v
        A[name] = nc.dram_tensor(f"in_{name}", v.shape, mybir.dt.from_np(v.dtype), kind="ExternalInput").ap()
    for name, shape in outs.items():
        A[name] = nc.dram_tensor(f"out_{name}", shape, F32, kind="ExternalOutput").ap()
    A["nF"] = nc.dram_tensor("neg_running_sums", (FH, SEQ), F32, kind="Internal").ap()
    program(nc, A)
    r = run_bass_kernel_spmd(nc, [arrays], core_ids=[0]).results[0]
    y, k, v, lf = (r[f"out_{n}"] for n in ("o_x", "o_k", "o_v", "o_lf"))
    sp = np.ascontiguousarray(r["out_st_p"].transpose(0, 2, 1, 3)).reshape(1, 1, RH, DK, DV)
    ss = np.ascontiguousarray(r["out_st_s"].transpose(1, 0, 3, 2, 4)).reshape(1, DEC_B, RH, DK, DV)
    return (token_major(y, 0, SEQ).reshape(1, SEQ, D), token_major(y, SEQ, NT).reshape(DEC_B, DEC_T, D), sp, ss,
            token_major(k, 0, SEQ).reshape(1, SEQ, FH, HD), token_major(v, 0, SEQ).reshape(1, SEQ, FH, HD),
            np.ascontiguousarray(lf[:, 0:SEQ].T).reshape(1, SEQ, FH),
            token_major(k, SEQ, NT).reshape(DEC_B, DEC_T, FH, HD), token_major(v, SEQ, NT).reshape(DEC_B, DEC_T, FH, HD),
            np.ascontiguousarray(lf[:, SEQ:NT].T).reshape(DEC_B, DEC_T, FH))
```

```python
from contextlib import ExitStack

import numpy as np
import concourse.bass as bass
from concourse import mybir

F32 = mybir.dt.float32
F32R = mybir.dt.float32r
BF16 = mybir.dt.bfloat16
I32 = mybir.dt.int32
ALU = mybir.AluOpType
ACT = mybir.ActivationFunctionType
AX = mybir.AxisListType

P = 128
D = 1024
DT = D // P
SEQ = 512
DEC_B, DEC_T = 8, 4
NS = DEC_B * DEC_T
NT = SEQ + NS
HALF = NT // 2
RT = SEQ // P
NC = 1 + DEC_B
RH = 4
DK, DV = 256, 512
FH, HD = 16, 64
NPAIR = FH // 2
FF = 2816
FFT = FF // P // 2
PAST, PAGE = 1024, 128
NPG = PAST // PAGE
EPS = 1e-6
SLAB = 8
RING = 3
VR = 3
VLAG = 12
UNITS = DEC_B * NPG
MBLK = 4
NMOD = 14 * DT
MOD_FIRST = 2 * DT
MOD_AT = (0, 1, 2, 3, 5, 6, 7, 8)
FIRST = MOD_FIRST + 2
BIG = 1e30

V_B = 0
V_RET = NMOD
V_ATT = V_RET + DT
V_FFN = V_ATT + DT
V_KV = V_FFN + 2 * DT
V_QN = V_KV + DT
V_KN = V_QN + 1
V_BF = V_KN + 1
NV = V_BF + 1

C_ID = 0
C_BD = C_ID + P
C_US = C_BD + P
C_CM = C_US + P
C_NM = C_CM + P
C_FO = C_NM + NS
C_FM = C_FO + 64
C_END = C_FM + NC
R_COS = 0
R_SIN = NT
R_CR = 2 * NT
R_KP = R_CR + RH * NS
R_KS = R_KP + RH * RT
R_DS = R_KS + RH * DEC_B
R_CD = R_DS + RH * NS
R_END = R_CD + RH


def constants():
    f = np.float32
    c = np.zeros((P, C_END), f)
    i = np.arange(P)
    c[:, C_ID:C_ID + P] = np.eye(P)
    c[:, C_BD:C_BD + P] = (i[:, None] // HD) == (i[None, :] // HD)
    c[:, C_US:C_US + P] = i[:, None] > i[None, :]
    c[:, C_CM:C_CM + P] = np.where(i[None, :] <= i[:, None], 0, -BIG)
    j, q = np.arange(NS)[:, None], np.arange(NS)[None, :]
    same = (j // DEC_T == q // DEC_T) & (j % DEC_T <= q % DEC_T)
    c[:NS, C_NM:C_NM + NS] = np.where(same, 0, -BIG)
    c[:2 * NC, C_FM:C_FM + NC] = (i[:2 * NC, None] % NC) == np.arange(NC)[None, :]
    c[:, C_FO:C_FO + 64] = (i[:, None] % 64) == np.arange(64)[None, :]

    r = np.zeros((P, R_END), f)
    dec = np.zeros((RH, P, SEQ), f)
    half = DK // 2
    freqs = f(10000.0) ** (-np.arange(half, dtype=f) / f(half))
    pos = np.concatenate([np.arange(SEQ), np.tile(PAST + np.arange(DEC_T), DEC_B)]).astype(f)
    ang = (freqs[:, None] * pos[None, :]).astype(f)
    r[:, R_COS:R_COS + NT] = np.cos(ang)
    r[:, R_SIN:R_SIN + NT] = np.sin(ang)
    log_g = np.log1p(-np.exp2(-5.0 - np.arange(RH)))
    t = np.arange(NS) % DEC_T
    b = np.arange(NS) // DEC_T
    for h in range(RH):
        r[:, R_CR + h * NS:R_CR + (h + 1) * NS] = np.exp(log_g[h] * (t + 1))[None, :]
        for rt in range(RT):
            r[:, R_KP + h * RT + rt] = np.exp(log_g[h] * (SEQ - 1 - rt * P - i))
        for bb in range(DEC_B):
            r[:NS, R_KS + h * DEC_B + bb] = np.where(b == bb, np.exp(log_g[h] * (DEC_T - 1 - t)), 0)
        r[:NS, R_DS + h * NS:R_DS + (h + 1) * NS] = np.where(same, np.exp(log_g[h] * np.maximum(q - j, 0)), 0)
        off = np.arange(SEQ)[None, :] - i[:, None]
        dec[h] = np.where(off >= 0, np.exp(log_g[h] * np.maximum(off, 0)), 0)
        r[:, R_CD + h] = np.exp(log_g[h] * DEC_T)
    return c, r, dec


def slab_order():
    m = [("m", 0, 0)]
    order = m * MOD_FIRST + [("p", 0, i) for i in range(12)]
    for h in range(RH):
        following = h < RH - 1
        for i in range(12):
            order += [("p", h + 1, i)] * following + m * (2 if i < DEC_B else 0)
        for j in range(4):
            order += [("o", h, j)] + m
    for u in range(4):
        if u == 2:
            order += [("k", 0, i) for i in range(17)] + [("q", 0, i) for i in range(8)]
            order += [("past", 0, n) for n in range(UNITS)] + [("a", 0, i) for i in range(8)]
        for t in range(FFT):
            order += [("f", u, 2 * t), ("f", u, 2 * t + 1)] + m * (u < 2 and t in MOD_AT)
        order += [("g", u, i) for i in range(FFT)]
    return order


def program(nc, A):
    ctx = ExitStack()

    def sb(name, shape, dt=F32, where=None):
        return (where or ctx).enter_context(nc.sbuf_tensor(name, shape, dt))

    def sem(name):
        return ctx.enter_context(nc.semaphore(name))

    with ctx:
        x = sb("x", [P, DT, NT])
        place = ExitStack()
        h_hi = sb("h_hi", [P, DT, NT], F32R, where=place)
        h_lo = sb("h_lo", [P, DT, NT], F32R, where=place)
        place.close()
        vraw = sb("fox_vraw", [P, VR, D], where=place)
        v_hi = sb("fox_v_hi", [P, 2, D], F32R, where=place)
        v_lo = sb("fox_v_lo", [P, 2, D], F32R, where=place)
        ss0 = sb("fox_ss0", [64, PAST + NS], where=place)
        place.close()
        sb("h_place", [P, 2 * DT * NT])
        raw = sb("raw", [P, RING, SLAB * P])
        w_hi = sb("w_hi", [P, RING, SLAB * P], F32R)
        w_lo = sb("w_lo", [P, RING, SLAB * P], F32R)
        mod = sb("mod", [P, NMOD, NC])
        gain = sb("gain", [P, DT, NC])
        vec = sb("vec", [P, NV])
        cst = sb("cst", [P, C_END])
        ones = sb("ones", [P, P])
        cact = sb("cact", [P, DT, NC])
        ctmp = sb("ctmp", [P, DT, NC])
        nplace = ExitStack()
        var = sb("var", [P, NT], where=nplace)
        rstd = sb("rstd", [P, NT], where=nplace)
        newt = sb("newt", [P, NT], where=nplace)
        nplace.close()
        pT = sb("fox_pT", [P, 2, SEQ], where=nplace)
        so = sb("fox_so", [P, SEQ], where=nplace)
        nplace.close()
        sb("norm_place", [P, 3 * NT])
        xplace = ExitStack()
        xs = sb("xs", [P, 2, NT], where=xplace)
        xplace.close()
        bias = sb("fox_bias", [P, 2, SEQ], where=xplace)
        xplace.close()
        sb("x_place", [P, 2 * NT])
        hplace = ExitStack()
        hf = sb("hf", [P, 2, NT], where=hplace)
        hplace.close()
        ss1 = sb("fox_ss1", [64, PAST + NS], where=hplace)
        hplace.close()
        sb("hf_place", [P, 2 * NT])
        m0 = sb("q_gain", [P, 1])
        tabs = sb("tabs", [1, DEC_B * NPG], I32)
        ident = cst[:, C_ID:C_ID + P]
        ss = (ss0, ss1)

        pj = [ctx.enter_context(nc.psum_tensor(f"proj{i}", [P, 2, 512], F32)) for i in range(2)]
        bk = [ctx.enter_context(nc.psum_tensor(f"bank{i}", [P, 512], F32)) for i in range(4)]

        start = ExitStack()
        first_raw = sb("first_raw", [P, MOD_FIRST, SLAB * P], where=start)
        start.close()

        ret = ExitStack()
        rc = sb("rc", [P, R_END], where=ret)
        dec = sb("ret_dec", [P, 2, SEQ], where=ret)
        qT = sb("ret_q", [P, 2, NT], where=ret)
        kT = sb("ret_k", [P, 2, NT], where=ret)
        qx = sb("ret_qx", [P, 2, NS], where=ret)
        vT = sb("ret_vT", [P, 4, NT], where=ret)
        vtok = sb("ret_vtok", [P, RT, DV], where=ret)
        vs = sb("ret_vs", [NS, DV], where=ret)
        ktok = sb("ret_ktok", [P, RT, DK], where=ret)
        ks = sb("ret_ks", [NS, DK], where=ret)
        kb = sb("ret_kb", [NS, 2, DK], where=ret)
        att = sb("ret_att", [P, 1280], where=ret)
        atts = sb("ret_atts", [NS, NS], where=ret)
        gate = sb("ret_gate", [P, 4, NT], where=ret)
        oT = sb("ret_o", [P, 4, NT], where=ret)
        og_hi = sb("ret_og_hi", [P, 4, NT], F32R, where=ret)
        og_lo = sb("ret_og_lo", [P, 4, NT], F32R, where=ret)
        st = sb("ret_state", [P, 2, 2, DV], where=ret)
        cs = sb("c_parts", [P, DT, P], F32R, where=ret)
        mev = sb("mod_rows", [2 * NC, SEQ], where=ret)
        ret.close()

        ff = ExitStack()
        hid_hi = sb("hid_hi", [P, FFT, NT], F32R, where=ff)
        hid_lo = sb("hid_lo", [P, FFT, NT], F32R, where=ff)
        hid = sb("hid", [P, 2, NT], where=ff)
        sig = sb("sig", [P, 2, NT], where=ff)
        ff.close()

        fx = ExitStack()
        fkT = sb("fox_kT", [P, NPAIR, NT], where=fx)
        fqT = sb("fox_qT", [P, NPAIR, NT], where=fx)
        fv = sb("fox_v", [P, RT, D], where=fx)
        fvs = sb("fox_vs", [NS, D], where=fx)
        lf = sb("fox_logf", [FH, NT], where=fx)
        negF = sb("fox_negF", [FH, NT], where=fx)
        nFs = sb("fox_nFs", [NS, FH], where=fx)
        Rb = sb("fox_R", [P, DEC_B, NPG, FH], where=fx)
        cmb = sb("fox_cmb", [P, P], BF16, where=fx)
        idb = sb("fox_idb", [P, P], BF16, where=fx)
        fxe = ExitStack()
        lfa = sb("fox_lfa", [FH, 4, NT], where=fxe)
        fraw = sb("fox_raw", [P, 2, NT], where=fxe)
        plf = sb("fox_plf", [P, DEC_B, NPG, FH], where=fxe)
        suf = sb("fox_suf", [P, DEC_B, NPG, FH], where=fxe)
        fxe.close()
        fxp = ExitStack()
        pr = sb("fox_p", [P, 4, SEQ], where=fxp)
        mx = sb("fox_mx", [P, 64], where=fxp)
        nmx = sb("fox_nmx", [P, 64], where=fxp)
        rs = sb("fox_rs", [P, 64], where=fxp)
        rsi = sb("fox_rsi", [P, 64], where=fxp)
        fxs = ExitStack()
        sn = sb("fox_sn", [NS, DEC_B, NPAIR, 2, DEC_T], where=fxs)
        qbd = sb("fox_qbd", [P, NPAIR, DEC_B, 2 * DEC_T], where=fxs)
        qd_hi = sb("fox_qd_hi", [P, NPAIR * (P + 8)], F32R, where=fxs)
        qd_lo = sb("fox_qd_lo", [P, NPAIR * (P + 8)], F32R, where=fxs)
        Rx = sb("fox_Rx", [P, 2, 2, 64], where=fxs)
        pn = sb("fox_pn", [NS, 2, 64], where=fxs)
        nm = sb("fox_nm", [64, DEC_B], where=fxs)
        ls = sb("fox_ls", [64, DEC_B], where=fxs)
        li = sb("fox_li", [64, DEC_B], where=fxs)
        dg = sb("fox_dg", [64, 64], where=fxs)
        sT = sb("fox_sT", [P, 2, NPG, P], F32R, where=fxs)
        fxs.close()
        fxp.close()
        fx.close()

        foT = fqT

        S = {}
        for n in """x_in cst_in rc_in dec_in0 dec_in1 c_in tab_in first_in0 first_in1 first_in2 first_in3 mod_hi cs_hi_ready cs_ready mod_rows mod_turned m_done c_exp c_ready hi_split first_split w_split w_tiles
                 sq_ready ms_ready var_ready r_root scaled hs_full hs_hi hi_ready h_ready x_done gains
                 dve_chain rope_done v_evac tr_ready tr_evac scores_ready decayed
                 o_ready o_evac os_ready os_evac upd_ready kb_ready upd_done st_saved0 st_saved1 st_in0 st_in1 sp_ready sp_evac sp_saved
                 osq_ready osq_used gated og_hi_ready og_ready silu_exp silu_done
                 hid_full hid_hi_ready hid_ready
                 fk_raw fk_sq fk_done fv_raw fv_saved0 fv_saved1 fvt_ready fvt_evac lf_raw lf_exp lf_done
                 nF_ready nFs_ready nFs_psum plf_in suf_ready R_psum R_done
                 bias_in0 bias_in1 s_psum s_max p_exp p_done pT_psum pT_ready fo_psum fo_done idb_ready
                 fo_hi_ready fo_ready
                 k_in0 k_in1 k_in2 v_in0 v_in1 v_in2 v_hi_ready v_lo_ready v_used qbd_ready qd_zero qd_hi_ready qd_ready sn_psum sn_done Rx_ready ks_out
                 snT_psum snT_out sm_ready s_exp dg_ready sT_psum sT_hi sT_ready pn_psum pn_ready so_out back_psum so_done
                 y_out nF_out k_out lf_out pair_free0 pair_free1 raw_in0 raw_in1 raw_in2""".split():
            S[n] = sem(n)
        block = ctx.enter_context(nc.Block())

        def two(ap):
            return ap.rearrange("p (h n) -> p h n", h=2)

        order = slab_order()
        mod_slabs_at = [s for s, what in enumerate(order) if what[0] == "m"]
        assert len(mod_slabs_at) == NMOD and FIRST % RING == 0
        place_of = {what: s for s, what in enumerate(order) if what[0] != "m"}
        W_KV, W_Q = place_of["k", 0, 0], place_of["q", 0, 0]
        W_PAST, W_O = place_of["past", 0, 0], place_of["a", 0, 0]
        W_ALL = len(order)

        FIRST_BLOCKS = MOD_FIRST // MBLK

        def block_bank(b):
            return bk[2 + b % 2] if b < FIRST_BLOCKS else bk[2]

        def proj_done(h, i):
            return (place_of["p", h, i] + 1) * SLAB

        def out_done(h, k):
            return place_of["o", h, k // 2] * SLAB + 4 * (k % 2 + 1)

        def block_done(m):
            return (mod_slabs_at[MBLK * m + MBLK - 1] + 1) * SLAB

        def ret_proj_tile(h):
            return 0 if h == 0 else 20 * h - 8

        def ret_out_tile(h):
            return 20 * h + 24 if h < RH - 1 else 20 * h + 12

        TQ = FH * RT
        STEPS = UNITS + VLAG + 1
        T_FF0 = RH * 20
        FFN_T = 2 * FFT + DT
        T_KV = T_FF0 + 2 * FFN_T
        T_Q = T_KV + 17
        T_O = T_Q + 8
        T_FF1 = T_O + 8

        def ff_done_tiles(u):
            return (place_of["g", u, FFT - 1] + 1) * SLAB

        def hidden_done(u, j):
            return (place_of["f", u, j] + 1) * SLAB

        def tiles_after_out(h):
            return out_done(h, DT - 1)

        def ff_tile(layer, half):
            return (T_FF0 if layer == 0 else T_FF1) + FFN_T * half

        def pair_free(n):
            return S[f"pair_free{n % 2}"]

        def states_saved(eng):
            eng.wait_ge(S["st_saved0"], 16 * RH * DEC_B // 2)
            eng.wait_ge(S["st_saved1"], 16 * RH * DEC_B // 2)

        def keys_saved(eng):
            eng.wait_ge(S["k_out"], 16)
            eng.wait_ge(S["lf_out"], 16)

        def first_slab(s):
            return first_raw[:, s, :] if s < MOD_FIRST else raw[:, s % RING, :]

        def uses(s):
            return sum(1 for before in range(MOD_FIRST, s + 1) if before % RING == s % RING and order[before][0] != "past")

        def wait_split(eng, n):
            if n <= FIRST:
                eng.wait_ge(S["first_split"], n)
            else:
                eng.wait_ge(S["w_split"], n - FIRST)

        def wait_tile(eng, tiles):
            eng.wait_ge(S["w_tiles"], tiles)

        def page_of(n):
            return nc.sync.value_load(tabs[0:1, n:n + 1], min_val=0, max_val=A["lf"].shape[0] - 1)

        @block.sync
        def _(sp):
            slab = [0]

            def weights(n):
                for _ in range(n):
                    s = slab[0]
                    if s >= MOD_FIRST + RING:
                        wait_split(sp, s - RING + 1)
                    row = s if s < W_PAST else s - UNITS
                    sp.dma_start(raw[:, s % RING, :], A["w"][row]).then_inc(S[f"raw_in{s % RING}"], 16)
                    slab[0] += 1

            def load_state(n):
                if n >= 2:
                    sp.wait_ge(S[f"st_saved{n % 2}"], 16 * (n // 2))
                sp.dma_start(st[:, n % 2], A["state"][n // DEC_B, n % DEC_B]).then_inc(S[f"st_in{n % 2}"], 16)

            def save_state(n):
                sp.wait_ge(S["upd_done"], 2 * n + 2)
                sp.dma_start(A["st_s"][n // DEC_B, n % DEC_B], st[:, n % 2]).then_inc(S[f"st_saved{n % 2}"], 16)

            sp.dma_start(cact[:], A["cT"]).then_inc(S["c_in"], 16)
            sp.dma_start(vec[:], A["vec"]).then_inc(S["cst_in"], 16)
            sp.dma_start(cst[:], A["cst"]).then_inc(S["cst_in"], 16)
            def first_slabs(b):
                sp.dma_start(first_raw[:, b * MBLK:(b + 1) * MBLK, :], A["w"][b * MBLK:(b + 1) * MBLK].rearrange("s p n -> p s n"))\
                    .then_inc(S[f"first_in{b}"], 16)
                slab[0] += MBLK

            first_slabs(0)
            sp.dma_start(x[:], A["xT"]).then_inc(S["x_in"], 16)
            sp.dma_start(tabs[:], A["table"]).then_inc(S["tab_in"], 16)
            for b in range(1, FIRST_BLOCKS):
                first_slabs(b)
            weights(RING)
            sp.wait_ge(S["first_split"], MOD_FIRST)
            sp.dma_start(rc[:], A["rc"]).then_inc(S["rc_in"], 16)
            weights(12)
            load_state(0)
            load_state(1)
            for h in range(RH):
                last = h == RH - 1
                if h >= 2:
                    sp.wait_ge(S["decayed"], 5 * (h - 1))
                sp.dma_start(dec[:, h % 2, :], A["dec"][h]).then_inc(S[f"dec_in{h % 2}"], 16)
                for n in range(h * DEC_B, (h + 1) * DEC_B):
                    if n:
                        save_state(n - 1)
                        if n + 1 < RH * DEC_B:
                            load_state(n + 1)
                    weights(2 if last else 3)
                for _ in range(4):
                    weights(0 if last else 1)
                for _ in range(4):
                    weights(2)
            save_state(RH * DEC_B - 1)
            weights(W_KV + RING - slab[0])
            sp.wait_ge(S["tab_in"], 16)
            sp.wait_ge(S["h_ready"], DT * 3)
            for n in range(UNITS):
                if n % 3 == 0 and slab[0] < W_PAST:
                    weights(1)
                sp.dma_start(plf[:, n // NPG, n % NPG, :].unsqueeze(1), A["lf"][bass.ds(page_of(n), 1)].rearrange("a p h -> p a h"))\
                    .then_inc(S["plf_in"], 16)
            weights(W_PAST - slab[0])
            sp.wait_ge(S["fk_done"], NPAIR)
            sp.wait_ge(S["lf_done"], 1)
            sp.dma_start(A["o_k"], fkT[:]).then_inc(S["k_out"], 16)
            sp.dma_start(A["o_lf"], lf[:]).then_inc(S["lf_out"], 16)

            sp.wait_ge(S["nF_ready"], 1)
            sp.dma_start(A["nF"], negF[:, 0:SEQ]).then_inc(S["nF_out"], 16)

            def keys(n):
                s, b, c, ph = slab[0], n // NPG, n % NPG // 2, n % 2
                wait_split(sp, s - RING + 1)
                for i in range(2):
                    pg = page_of(b * NPG + 2 * c + i)
                    sp.dma_start(raw[:, s % RING, i * SEQ:(i + 1) * SEQ].unsqueeze(1),
                                 A["kc"][bass.ds(pg, 1)][:, :, ph * SEQ:(ph + 1) * SEQ].rearrange("a p n -> p a n"))\
                        .then_inc(S[f"k_in{s % RING}"], 16)
                slab[0] += 1

            def values(v):
                b, half, q = v // NPG, v % NPG // 4, v % 4
                if v >= VR:
                    sp.wait_ge(S["v_lo_ready"], v - VR + 1)
                for i in range(2):
                    pg = page_of(b * NPG + 2 * q + i)
                    sp.dma_start(vraw[:, v % VR, i * SEQ:(i + 1) * SEQ].unsqueeze(1),
                                 A["vc"][bass.ds(pg, 1)][:, :, half * SEQ:(half + 1) * SEQ].rearrange("a p n -> p a n"))\
                        .then_inc(S[f"v_in{v % VR}"], 16)

            for t in range(UNITS + VLAG + 1):
                if t < UNITS:
                    keys(t)
                if t == VLAG + 1:
                    wait_tile(sp, (W_Q + 8) * SLAB)
                if t >= VLAG + 1:
                    values(t - VLAG - 1)
            weights(8)
            weights(66)
            sp.wait_ge(S["x_done"], 8 * (RH + 2 + 1 + 2))
            sp.dma_start(A["o_x"], x[:]).then_inc(S["y_out"], 16)
            sp.wait_ge(S["y_out"], 16)
            sp.wait_ge(S["nF_out"], 16)
            sp.wait_ge(S["k_out"], 16)
            sp.wait_ge(S["lf_out"], 16)
            sp.wait_ge(S["st_saved0"], 16 * RH * DEC_B // 2)
            sp.wait_ge(S["st_saved1"], 16 * RH * DEC_B // 2)
            sp.wait_ge(S["sp_saved"], 16 * 2 * RH)
            sp.wait_ge(S["fv_saved0"], 16 * NPAIR // 2)
            sp.wait_ge(S["fv_saved1"], 16 * NPAIR // 2)

        @block.gpsimd
        def _(g):
            nc.gpsimd.memset(ones[:], 1.0).then_inc(S["hi_split"], 1)
            g.wait_ge(S["hi_split"], 1)
            unit = ones[:, 0:1].to_broadcast([P, SLAB * P])

            def split(s, slot, ring):
                nc.gpsimd.tensor_tensor(w_hi[:, slot, :], raw[:, ring, :], unit, ALU.mult).then_inc(S["hi_split"], 1)
                g.wait_ge(S["hi_split"], s - FIRST + 2)
                nc.gpsimd.tensor_tensor(w_lo[:, slot, :], raw[:, ring, :], w_hi[:, slot, :].bitcast(F32),
                                        ALU.subtract).then_inc(S["w_split"], 1)

            def weight(s, ring, held):
                g.wait_ge(S[f"raw_in{ring}"], 16 * held)
                split(s, ring % RING, ring)

            with nc.gpsimd.Fori(FIRST // RING, W_PAST // RING) as i:
                for r in range(RING):
                    g.wait_ge(S["w_tiles"], (i * RING + r - RING + 1) * SLAB)
                    weight(i * RING + r, r, i - (FIRST // RING - uses(FIRST + r)))
            for s in range(W_PAST // RING * RING, W_PAST):
                g.wait_ge(S["w_tiles"], SLAB * (s - RING + 1))
                weight(s, s % RING, uses(s))
            with nc.gpsimd.Fori(0, UNITS // RING) as i:
                for r in range(RING):
                    s = i * RING + (W_PAST + r)
                    ring = (W_PAST + r) % RING
                    g.wait_ge(S["w_tiles"], (s - RING + 1) * SLAB)
                    g.wait_ge(S[f"k_in{ring}"], 32 * (i + 1))
                    split(s, ring, ring)
            for s in range(W_PAST + UNITS // RING * RING, W_O):
                g.wait_ge(S["w_tiles"], SLAB * (s - RING + 1))
                g.wait_ge(S[f"k_in{s % RING}"], 32 * (UNITS // RING + 1))
                split(s, s % RING, s % RING)
            for s in range(W_O, W_ALL):
                g.wait_ge(S["w_tiles"], SLAB * (s - RING + 1))
                weight(s, s % RING, uses(s))

        @block.tensor
        def _(pe):
            mm = nc.tensor.matmul
            tiles = [0]
            tile_no = [0]
            chain = [0]

            def project(n, ktiles, hi, lo, ready=None):
                for i in range(n):
                    f = tile_no[0]
                    if f >= 2:
                        pe.wait_ge(pair_free(f), f // 2)
                    for k in range(ktiles):
                        t = tiles[0]
                        s = t // SLAB
                        if k == 0 or t % SLAB == 0:
                            wait_split(pe, s + 1)
                        if ready and i == 0:
                            pe.wait_ge(S[ready[0]], ready[1] + k + 1)
                        c = (t % SLAB) * P
                        for half in range(2):
                            cols = slice(half * HALF, (half + 1) * HALF)
                            for j, (w, a) in enumerate(((w_lo, hi), (w_hi, lo), (w_hi, hi))):
                                last = mm(pj[f % 2][:, half, 0:HALF], w[:, s % RING, c:c + P], a(k)[:, cols],
                                          start=k == 0 and j == 0, stop=k == ktiles - 1 and j == 2)
                        tiles[0] += 1
                        last.then_inc(S["w_tiles"], 1)
                    tile_no[0] += 1

            def from_h(n, ready=None):
                project(n, DT, lambda k: h_hi[:, k, :], lambda k: h_lo[:, k, :], ready)

            mslabs = [0]
            turned = [0]

            def modulate(n=1):
                for _ in range(n):
                    m, s = mslabs[0], tiles[0] // SLAB
                    wait_split(pe, s + 1)
                    b = m // MBLK
                    if m % MBLK == 0 and b > 1:
                        pe.wait_ge(S["m_done"], b - 1 if b < FIRST_BLOCKS else b)
                    for kk in range(2):
                        k = 2 * (m % MBLK) + kk
                        for j, w in enumerate((w_lo, w_hi)):
                            last = mm(block_bank(b)[:], cs[:, k, :], w[:, s % RING, kk * SEQ:(kk + 1) * SEQ], start=k == 0 and j == 0, stop=k == DT - 1 and j == 1)
                        last.then_inc(S["w_tiles"], SLAB // 2)
                    tiles[0] += SLAB
                    mslabs[0] += 1

            def turn_block():
                b = turned[0]
                turned[0] += 1
                pe.wait_ge(S["mod_rows"], b + 1)
                for i in range(MBLK):
                    last = mm(block_bank(b)[:, i * NC:(i + 1) * NC], mev[:, i * P:(i + 1) * P], cst[0:2 * NC, C_FM:C_FM + NC], start=True, stop=True)
                last.then_inc(S["mod_turned"], 1)

            def sum_squares(src, n, wait_each, lhs=None):
                for k in range(n):
                    wait_each(k)
                    for half in range(2):
                        last = mm(bk[half][:, 0:HALF], lhs if lhs is not None else ones[:], src(k)[:, half * HALF:(half + 1) * HALF],
                                  start=k == 0, stop=k == n - 1)
                    if k < n - 1:
                        last.then_inc(S["osq_used"], 1)
                last.then_inc(S["ms_ready"], 1)

            def norm(z):
                def w(k):
                    pe.wait_ge(S["sq_ready"], (z - (z > 3)) * DT + k + 1)
                sum_squares(lambda k: xs[:, k % 2, :], DT, w)

            def from_new(sem, first):
                f, s = tile_no[0], tiles[0] // SLAB
                pe.wait_ge(pair_free(f), f // 2) if f >= 2 else None
                pe.wait_ge(pair_free(f + 1), (f + 1) // 2) if f >= 2 else None
                wait_split(pe, s + 2)
                for k in range(DT):
                    pe.wait_ge(S[sem], first + k + 1)
                    for i in range(2):
                        for half in range(2):
                            cols = slice(half * HALF, (half + 1) * HALF)
                            for j, (w, a) in enumerate(((w_lo, h_hi), (w_hi, h_lo), (w_hi, h_hi))):
                                last = mm(pj[(f + i) % 2][:, half, 0:HALF], w[:, (s + i) % RING, k * P:(k + 1) * P], a[:, k, cols],
                                          start=k == 0 and j == 0, stop=k == DT - 1 and j == 2)
                        if i == 0:
                            last.then_inc(S["w_tiles"], 1)
                last.then_inc(S["w_tiles"], SLAB)
                tiles[0] += 2 * SLAB
                tile_no[0] += 2

            def from_norm(z, n=2):
                from_new("h_ready", DT * z)
                from_h(n - 2)

            pe.wait_ge(S["cst_in"], 32)
            pe.wait_ge(S["hi_split"], 1)
            pe.wait_ge(S["c_ready"], 1)
            pe.wait_ge(S["cs_ready"], 1)
            modulate(MBLK)
            norm(0)
            for b in range(1, FIRST_BLOCKS):
                modulate(2)
                turn_block()
                modulate(2)
            turn_block()
            from_norm(0, 12)

            for h in range(RH):
                last_head = h == RH - 1
                pe.wait_ge(S["v_evac"], h + 1)
                pe.wait_ge(S["rope_done"], 2 * h + 2)
                if h:
                    pe.wait_ge(S["sp_evac"], 2 * h)
                    pe.wait_ge(S["os_evac"], h)
                    pe.wait_ge(S["m_done"], (MOD_FIRST + 20 * h) // MBLK)
                    pe.wait_ge(S["og_ready"], 4 * h)
                    pe.wait_ge(S["upd_done"], 16 * h)
                for e in range(8):
                    if e >= 4:
                        pe.wait_ge(S["tr_evac"], 8 * h + e - 3)
                    if e < 4:
                        for f in range(4):
                            last = nc.tensor.transpose(bk[e][:, f * P:(f + 1) * P], vT[:, f, e * P:(e + 1) * P], ident)
                    elif e == 4:
                        for f in range(4):
                            last = nc.tensor.transpose(bk[0][0:NS, f * P:(f + 1) * P], vT[:, f, SEQ:NT], ident)
                    elif e < 7:
                        for r in range(2):
                            rt = 2 * (e - 5) + r
                            for d in range(2):
                                c = r * DK + d * P
                                last = nc.tensor.transpose(bk[e - 4][:, c:c + P], kT[:, d, rt * P:(rt + 1) * P], ident)
                    else:
                        for d in range(2):
                            last = nc.tensor.transpose(bk[3][0:NS, d * P:(d + 1) * P], kT[:, d, SEQ:NT], ident)
                    last.then_inc(S["tr_ready"], 1)
                for j in range(RT):
                    pe.wait_ge(S["tr_evac"], 8 * h + 5 + j)
                    n = SEQ - j * P
                    for d in range(2):
                        last = mm(bk[j][:, 0:n], kT[:, d, j * P:(j + 1) * P], qT[:, d, j * P:SEQ], start=d == 0, stop=d == 1)
                    if j == RT - 1:
                        for d in range(2):
                            last = mm(bk[3][0:NS, P:P + NS], kT[:, d, SEQ:NT], qT[:, d, SEQ:NT], start=d == 0, stop=d == 1)
                    last.then_inc(S["scores_ready"], 1)
                pe.wait_ge(S["decayed"], 5 * h + 5)
                for i in range(DEC_B):
                    if i in (2, 4, 6):
                        turn_block()
                    if not last_head:
                        from_h(1)
                    modulate()
                    if i == 0:
                        for e in range(4):
                            mm(bk[0][:, e * NS:(e + 1) * NS], vs[:, e * P:(e + 1) * P], atts[:], start=e == 0, stop=False, skip_group_check=True)
                    n = h * DEC_B + i
                    pe.wait_ge(S[f"st_in{n % 2}"], 16 * (n // 2 + 1))
                    pe.wait_ge(S["kb_ready"], n + 1)
                    for d in range(2):
                        for e in range(4):
                            last = mm(bk[0][:, e * NS + i * DEC_T:e * NS + (i + 1) * DEC_T], st[:, n % 2, d, e * P:(e + 1) * P],
                                      qx[:, d, i * DEC_T:(i + 1) * DEC_T], start=False, stop=i == DEC_B - 1 and d == 1, skip_group_check=True)
                        if i == DEC_B - 1 and d == 1:
                            last.then_inc(S["os_ready"], 1)
                        if n or d:
                            pe.wait_ge(S["upd_done"], 2 * n + d)
                        mm(bk[1][:], kb[:, i % 2, d * P:(d + 1) * P], vs[:], start=True, stop=True).then_inc(S["upd_ready"], 1)
                    modulate()
                    if 1 <= i <= 4:
                        e, at = i - 1, 0
                        if e:
                            pe.wait_ge(S["o_evac"], 4 * h + e)
                        for j in range(RT):
                            n = SEQ - j * P
                            last = mm(bk[3][:, j * P:SEQ], vtok[:, j, e * P:(e + 1) * P], att[:, at:at + n], start=j == 0, stop=j == RT - 1)
                            at += n
                        last.then_inc(S["o_ready"], 1)
                    if 5 <= i <= 6:
                        d = i - 5
                        pe.wait_ge(S["o_evac"], 4 * h + 4)
                        if d:
                            pe.wait_ge(S["sp_evac"], 2 * h + 1)
                        for rt in range(RT):
                            last = mm(bk[3][:], ktok[:, rt, d * P:(d + 1) * P], vtok[:, rt, :], start=rt == 0, stop=rt == RT - 1)
                        last.then_inc(S["sp_ready"], 1)
                turn_block()
                pe.wait_ge(S["os_evac"], h + 1)
                pe.wait_ge(S["upd_done"], 16 * h + 16)

                def w(k):
                    pe.wait_ge(S["osq_ready"], 4 * h + k + 1)
                sum_squares(lambda k: xs[:, k % 2, :], 4, w)
                pe.wait_ge(S["sp_evac"], 2 * h + 2)
                for i in range(4):
                    if not last_head:
                        from_h(1)
                for i in range(DT):
                    project(1, 4, lambda k: og_hi[:, k, :], lambda k: og_lo[:, k, :], ("og_ready", 4 * h) if i == 0 else None)
                    if i % 2:
                        modulate()
                turn_block()

            def feed_forward(layer):
                for half in range(2):
                    u = 2 * layer + half
                    for m in range(FFT):
                        if m in (5, 10) and layer == 0:
                            turn_block()
                        if half or m:
                            from_h(2)
                        else:
                            from_norm(1 if layer == 0 else 4, 2)
                        if m in MOD_AT and layer == 0:
                            modulate()
                    project(1, FFT, lambda k: hid_hi[:, k, :], lambda k: hid_lo[:, k, :], ("hid_ready", FFT * u))
                    project(DT - 1, FFT, lambda k: hid_hi[:, k, :], lambda k: hid_lo[:, k, :])

            norm(1)
            feed_forward(0)

            BD = cst[:, C_BD:C_BD + P]
            norm(2)

            def head_norm(k):
                pe.wait_ge(S["fk_sq"], k + 1)
                for half in range(2):
                    last = mm(bk[half][:, 0:HALF], BD, xs[:, k % 2, half * HALF:(half + 1) * HALF], start=True, stop=True)
                last.then_inc(S["ms_ready"], 1)

            for p in range(NPAIR):
                if p == 0:
                    from_norm(2)
                elif p > 1:
                    from_h(1)
                if p:
                    pe.wait_ge(S["var_ready"], 3 + RH + p - 1)
                    head_norm(p - 1)
            pe.wait_ge(S["var_ready"], 3 + RH + NPAIR - 1)
            head_norm(NPAIR - 1)

            def v_rows(p):
                pe.wait_ge(S["fv_raw"], p + 1)
                if p:
                    pe.wait_ge(S["fvt_evac"], p)
                for rt in range(RT):
                    nc.tensor.transpose(bk[2][:, rt * P:(rt + 1) * P], fraw[:, p % 2, rt * P:(rt + 1) * P], ident)
                nc.tensor.transpose(bk[3][0:NS, 0:P], fraw[:, p % 2, SEQ:NT], ident).then_inc(S["fvt_ready"], 1)

            for p in range(NPAIR):
                from_h(1)
                if p:
                    v_rows(p - 1)
            from_h(1)
            v_rows(NPAIR - 1)

            for p in range(NPAIR):
                if p == 0:
                    from_norm(3)
                elif p > 1:
                    from_h(1)
                if p:
                    pe.wait_ge(S["var_ready"], 3 + RH + NPAIR + p - 1)
                    head_norm(NPAIR + p - 1)
            pe.wait_ge(S["var_ready"], 3 + RH + 2 * NPAIR - 1)
            head_norm(2 * NPAIR - 1)

            pe.wait_ge(S["suf_ready"], 1)
            pe.wait_ge(S["fvt_evac"], NPAIR)
            half_b = DEC_B // 2
            for i in range(2):
                o = bk[2 + i][:].rearrange("p (b g h) -> p b g h", b=half_b, g=NPG)
                mm(o, cst[:, C_US:C_US + P], plf[:, i * half_b:(i + 1) * half_b], start=True, stop=False)
                mm(o, ones[:], suf[:, i * half_b:(i + 1) * half_b], start=False, stop=True).then_inc(S["R_psum"], 1)
            pe.wait_ge(S["R_done"], 2)
            pe.wait_ge(S["nF_ready"], 1)
            nc.tensor.transpose(bk[2][0:NS, 0:FH], negF[:, SEQ:NT], cst[0:FH, C_ID:C_ID + FH]).then_inc(S["nFs_psum"], 1)

            pe.wait_ge(S["fk_done"], 2 * NPAIR)
            pe.wait_ge(S["idb_ready"], 2)
            pe.wait_ge(S["nFs_ready"], 1)
            pe.wait_ge(S["qbd_ready"], 2 * NPAIR + 1)
            for p in range(NPAIR):
                last = mm(bk[3][0:NS, p * 64:(p + 1) * 64], fkT[:, p, SEQ:NT], qbd[:, p], start=True, stop=True)
            last.then_inc(S["sn_psum"], 1)

            def score(t):
                h, qb = t // RT, t % RT
                r = (h % 2) * HD
                if t >= 2:
                    pe.wait_ge(S["s_max"], t - 1)
                n = (qb + 1) * P
                mm(pj[0][:, t % 2, 0:n], fqT[r:r + HD, h // 2, qb * P:n], fkT[r:r + HD, h // 2, 0:n], start=True, stop=False)
                mm(pj[0][:, t % 2, qb * P:n], idb[:], cmb[:], start=False, stop=True).then_inc(S["s_psum"], 1)

            def turn(t):
                pe.wait_ge(S["p_done"], t + 1)
                if t >= 2:
                    pe.wait_ge(S["pT_ready"], t - 1)
                for k in range(t % RT + 1):
                    last = nc.tensor.transpose(pj[1][:, t % 2, k * P:(k + 1) * P], pr[:, t % 4, k * P:(k + 1) * P], ident)
                last.then_inc(S["pT_psum"], 1)

            def weigh(t):
                h, qb = t // RT, t % RT
                r = (h % 2) * HD
                pe.wait_ge(S["pT_ready"], t + 1)
                if qb == 0 and h:
                    pe.wait_ge(S["fo_done"], h)
                for k in range(qb + 1):
                    last = mm(bk[0][r:r + HD, qb * P:(qb + 1) * P], fv[:, k, h * HD:(h + 1) * HD], pT[:, t % 2, k * P:(k + 1) * P],
                              start=k == 0, stop=k == qb)
                last.then_inc(S["fo_psum"], 1)

            def past_scores(n):
                b, c, ph = n // NPG, n % NPG // 2, n % 2
                s = tiles[0] // SLAB
                chunk = n // 2
                if n % NPG == 0:
                    pe.wait_ge(S["qd_ready"], b + 1)
                if ph == 0 and chunk:
                    pe.wait_ge(S["ks_out"], chunk)
                wait_split(pe, s + 1)
                if ph:
                    pe.wait_ge(S["Rx_ready"], chunk + 1)
                    for i in range(2):
                        mm(bk[1][0:64, i * P:(i + 1) * P], Rx[:, chunk % 2, i, :], ident, start=False, stop=False)
                for i in range(NPAIR // 2):
                    p = ph * NPAIR // 2 + i
                    for j, (q, w) in enumerate(((qd_lo, w_hi), (qd_hi, w_lo), (qd_hi, w_hi))):
                        keys = w[:, s % RING, :].rearrange("p (g a n) -> p g a n", g=2, a=NPAIR // 2)[:, :, i, :]
                        last = mm(bk[1][:, 0:256], q[:, p * P:(p + 1) * P], keys, start=p == 0 and j == 0, stop=p == NPAIR - 1 and j == 2)
                    last.then_inc(S["w_tiles"], 2)
                    tiles[0] += 2

            def new_scores(b):
                if b >= 1:
                    pe.wait_ge(S["pn_ready"], b)
                if b >= 2:
                    pe.wait_ge(S["so_done"], 4 * (b - 1))
                if b == 0:
                    pe.wait_ge(S["sn_done"], 2 * DEC_B)
                nc.tensor.transpose(bk[2][0:64, 0:NS], sn[:, b].rearrange("p a c t -> p (a c t)"),
                                    cst[0:NS, C_ID:C_ID + NS]).then_inc(S["snT_psum"], 1)

            def turn_weights(b):
                pe.wait_ge(S["dg_ready"], b + 1)
                pe.wait_ge(S["snT_out"], b + 1)
                if b >= 2:
                    pe.wait_ge(S["so_done"], 4 * (b - 2) + 2)
                for k in range(NPG):
                    last = mm(bk[2][:, k * 64:(k + 1) * 64], ss[b % 2][:, k * P:(k + 1) * P], dg[:], start=True, stop=True)
                last.then_inc(S["sT_psum"], 1)

            def turn_new(b):
                pe.wait_ge(S["sT_ready"], b + 1)
                mm(bk[2][0:NS, 0:64], ss[b % 2][:, PAST:PAST + NS], dg[:], start=True, stop=True).then_inc(S["pn_psum"], 1)

            def past_values(v):
                b, half, q = v // NPG, v % NPG // 4, v % 4
                if q == 0:
                    pe.wait_ge(S["sT_ready"], b + 1)
                    if v:
                        pe.wait_ge(S["so_out"], v // 4)
                pe.wait_ge(S["v_lo_ready"], v + 1)
                if q == 3:
                    pe.wait_ge(S["pn_ready"], b + 1)
                    mm(bk[3][0:64, :], pn[:, b % 2, :], fvs[:, half * SEQ:(half + 1) * SEQ], start=False, stop=False)
                for i in range(2):
                    for j, w in enumerate((v_lo, v_hi)):
                        last = mm(bk[3][:], sT[:, b % 2, 2 * q + i, :], w[:, v % 2, i * SEQ:(i + 1) * SEQ],
                                  start=q == 0 and i == 0 and j == 0, stop=q == 3 and i == 1 and j == 1)
                last.then_inc(S["v_used"], 1)

            def features_out(n):
                b, half = n // 2, n % 2
                pe.wait_ge(S["so_out"], n + 1)
                pe.wait_ge(S["pn_ready"], min(b + 1 + half, DEC_B))
                pe.wait_ge(S["snT_out"], min(b + 2, DEC_B))
                if n:
                    pe.wait_ge(S["so_done"], 2 * n)
                for i in range(NPAIR // 2):
                    p = half * NPAIR // 2 + i
                    last = mm(bk[2][:, i * 8:i * 8 + 8], so[:, i * P:(i + 1) * P], cst[:, C_FO + p * 8:C_FO + p * 8 + 8],
                              start=True, stop=True)
                last.then_inc(S["back_psum"], 1)

            for t in range(STEPS):
                b, g = t // NPG, t % NPG
                if t < TQ:
                    score(t)
                if 0 <= t - 2 < TQ:
                    turn(t - 2)
                if 0 <= t - 4 < TQ:
                    weigh(t - 4)
                if t < UNITS:
                    past_scores(t)
                    if g == 6:
                        new_scores(b)
                if 1 <= b <= DEC_B:
                    if g == 2:
                        turn_weights(b - 1)
                    if g == 3:
                        turn_new(b - 1)
                if 0 <= t - VLAG < UNITS:
                    past_values(t - VLAG)
                if t > VLAG and (t - VLAG) % 4 == 0:
                    features_out((t - VLAG) // 4 - 1)

            from_new("fo_ready", 0)
            from_h(NPAIR - 2)
            norm(4)
            feed_forward(1)

        @block.scalar
        def _(act):
            chain = [0]
            hs = hf[:, 0, 0:DT * NS].rearrange("p (k n) -> p k n", k=DT)

            def fn(out, in_, f, **kw):
                return nc.scalar.activation(out, in_, f, **kw)

            def root():
                c = chain[0]
                act.wait_ge(S["var_ready"], c + 1)
                fn(rstd[:], var[:], ACT.Abs_reciprocal_sqrt).then_inc(S["r_root"], 1)
                chain[0] += 1

            def first_slabs(lo, hi):
                for s in range(lo, hi):
                    if s < MOD_FIRST:
                        act.wait_ge(S[f"first_in{s // MBLK}"], 16)
                    else:
                        act.wait_ge(S[f"raw_in{s % RING}"], 16)
                    if s >= RING:
                        wait_tile(act, SLAB * (s - RING + 1))
                    fn(w_hi[:, s % RING, :], first_slab(s), ACT.Copy).then_inc(S["mod_hi"], 1)

            def norm(z, shift):
                if z == 0:
                    first_slabs(0, MBLK)
                for k in range(DT if z != 3 else 0):
                    if z:
                        act.wait_ge(S["x_done"], x_done_before[z] + k + 1)
                    else:
                        act.wait_ge(S["x_in"], 16)
                    if k >= 2:
                        act.wait_ge(S["osq_used"], osq_before[z] + k - 1)
                    elif z:
                        act.wait_ge(S["ms_ready"], chain[0])
                    fn(xs[:, k % 2, :], x[:, k, :], ACT.Square).then_inc(S["sq_ready"], 1)
                if z == 0:
                    first_slabs(MBLK, 3 * MBLK)
                if z != 3:
                    root()
                if z == 0:
                    first_slabs(3 * MBLK, FIRST)
                for k in range(DT):
                    act.wait_ge(S["scaled"], z * DT + k + 1)
                    fn(h_hi[:, k, 0:SEQ], xs[:, k % 2, 0:SEQ], ACT.Identity, bias=mod[:, shift + k, 0:1]).then_inc(S["hi_ready"], 1)
                    if k == 0:
                        act.wait_ge(S["hs_full"], z + 1)
                        fn(h_hi[:, :, SEQ:NT], hs, ACT.Copy).then_inc(S["hs_hi"], 1)

            x_done_before = [0, 8 * RH - 8, 8 * (RH + 2) - 8, 8 * (RH + 2) - 8, 8 * (RH + 3) - 8]
            osq_before = [0, 7 + 3 * RH, 14 + 3 * RH, 0, 21 + 3 * RH]

            def free(n, ins):
                ins.then_inc(pair_free(n), 1)

            act.wait_ge(S["c_in"], 16)
            fn(ctmp[:], cact[:], ACT.Exp, scale=-1.0).then_inc(S["c_exp"], 1)
            act.wait_ge(S["c_ready"], 2)
            fn(cs[:, :, 0:NC], cact[:], ACT.Copy).then_inc(S["cs_hi_ready"], 1)
            norm(0, 0)

            def raw_out(h, i):
                wait_tile(act, proj_done(h, i))
                if h and i == 0:
                    act.wait_ge(S["ms_ready"], chain[0])
                if i == 2:
                    act.wait_ge(S["rope_done"], 2 * h + 1)
                n = ret_proj_tile(h) + i
                free(n, fn(two(xs[:, i % 2, :]), pj[n % 2][:, :, 0:HALF], ACT.Copy))

            def value_out(h, f):
                wait_tile(act, proj_done(h, 4 + f))
                if h and f == 0:
                    act.wait_ge(S["tr_ready"], 8 * h)
                n = ret_proj_tile(h) + 4 + f
                free(n, fn(two(vT[:, f, :]), pj[f % 2][:, :, 0:HALF], ACT.Copy))
                if f == 3:
                    act.wait_ge(pair_free(0), (n - 1) // 2 + 1)
                    act.wait_ge(pair_free(1), n // 2 + 1)
                    act.sem_inc(S["v_evac"], 1)

            def gates(h):
                for f in range(4):
                    n = 4 * h + f
                    wait_tile(act, proj_done(h, 8 + f))
                    if n >= 2:
                        act.wait_ge(S["silu_done"], n - 1)
                    fn(two(hf[:, f % 2, :]), pj[f % 2][:, :, 0:HALF], ACT.Exp, scale=-1.0).then_inc(S["silu_exp"], 1)
                    free(ret_proj_tile(h) + 8 + f, fn(two(gate[:, f, :]), pj[f % 2][:, :, 0:HALF], ACT.Copy))

            act.wait_ge(S["h_ready"], DT)
            for i in range(4):
                raw_out(0, i)
            for f in range(4):
                value_out(0, f)
            gates(0)
            act.wait_ge(S["rc_in"], 16)
            for h in range(RH):
                last_head = h == RH - 1
                for e in range(8):
                    act.wait_ge(S["tr_ready"], 8 * h + e + 1)
                    if e < 4:
                        last = fn(vtok[:, e, :], bk[e][:], ACT.Copy)
                    elif e == 4:
                        last = fn(vs[:], bk[0][0:NS, :], ACT.Copy)
                    elif e < 7:
                        for r in range(2):
                            rt = 2 * (e - 5) + r
                            last = fn(ktok[:, rt, :], bk[e - 4][:, r * DK:(r + 1) * DK], ACT.Copy,
                                      scale=rc[:, R_KP + h * RT + rt:R_KP + h * RT + rt + 1])
                    else:
                        last = fn(ks[:], bk[3][0:NS, 0:DK], ACT.Copy)
                    last.then_inc(S["tr_evac"], 1)
                def o_out(e):
                    act.wait_ge(S["o_ready"], 4 * h + e + 1)
                    if h and e == 0:
                        act.wait_ge(S["og_ready"], 4 * h)
                    fn(oT[:, e, 0:SEQ], bk[3][:], ACT.Copy).then_inc(S["o_evac"], 1)

                def state_out(d):
                    n = 2 * h + d
                    act.wait_ge(S["silu_done"], 4 * h + 4)
                    act.wait_ge(S["sp_ready"], n + 1)
                    if n:
                        act.wait_ge(S["sp_saved"], 16 * n)
                    fn(hf[:, 0, 0:DV], bk[3][:], ACT.Copy).then_inc(S["sp_evac"], 1)
                    act.wait_ge(S["sp_evac"], n + 1)
                    act.dma_start(A["st_p"][h, :, d, :], hf[:, 0, 0:DV]).then_inc(S["sp_saved"], 16)

                for i in range(4):
                    if not last_head:
                        raw_out(h + 1, i)
                    if i:
                        o_out(i - 1)
                for f in range(4):
                    if not last_head:
                        value_out(h + 1, f)
                    if f == 0:
                        o_out(3)
                    if f in (1, 2):
                        state_out(f - 1)
                act.wait_ge(S["os_ready"], h + 1)
                fn(oT[:, :, SEQ:NT], bk[0][:, 0:4 * NS].rearrange("p (e n) -> p e n", e=4), ACT.Copy).then_inc(S["os_evac"], 1)
                act.wait_ge(S["os_evac"], h + 1)
                for e in range(4):
                    if e >= 2:
                        act.wait_ge(S["osq_used"], 7 + 3 * h + e - 1)
                    else:
                        act.wait_ge(S["ms_ready"], chain[0])
                    fn(xs[:, e % 2, :], oT[:, e, :], ACT.Square).then_inc(S["osq_ready"], 1)
                root()
                for e in range(4):
                    act.wait_ge(S["gated"], 4 * h + e + 1)
                    if h and e == 0:
                        wait_tile(act, tiles_after_out(h - 1))
                    fn(og_hi[:, e, :], oT[:, e, :], ACT.Copy).then_inc(S["og_hi_ready"], 1)
                if not last_head:
                    act.wait_ge(S["sp_saved"], 16 * 2 * (h + 1))
                    gates(h + 1)

            act.wait_ge(S["sp_saved"], 16 * 2 * RH)
            states_saved(act)

            def feed_forward(layer):
                for half in range(2):
                    u = 2 * layer + half
                    for m in range(FFT):
                        n = u * FFT + m
                        wait_tile(act, hidden_done(u, 2 * m))
                        if n >= 2:
                            act.wait_ge(S["hid_full"], n - 1)
                        fn(two(sig[:, n % 2, :]), pj[(ff_tile(layer, half) + 2 * m) % 2][:, :, 0:HALF], ACT.Exp, scale=-1.0)\
                            .then_inc(S["silu_exp"], 1)
                        t = ff_tile(layer, half) + 2 * m
                        free(t, fn(two(xs[:, n % 2, :]), pj[t % 2][:, :, 0:HALF], ACT.Copy))
                        if m:
                            hidden_hi(n - 1, m - 1, u)
                    hidden_hi(u * FFT + FFT - 1, FFT - 1, u)

            def hidden_hi(n, m, u):
                act.wait_ge(S["hid_full"], n + 1)
                if m == 0 and u:
                    wait_tile(act, ff_done_tiles(u - 1))
                fn(hid_hi[:, m, :], hid[:, n % 2, :], ACT.Copy).then_inc(S["hid_hi_ready"], 1)

            norm(1, 3 * DT)
            feed_forward(0)
            norm(2, 12 * DT)

            def head_tile(k, tile, slab):
                wait_tile(act, (slab + 1) * SLAB)
                if k >= 2:
                    act.wait_ge(S["fk_done"], k - 1)
                fn(two(fraw[:, k % 2, :]), pj[tile % 2][:, :, 0:HALF], ACT.Copy).then_inc(S["fk_raw"], 1)
                if k % NPAIR < 2:
                    act.wait_ge(S["h_ready"], DT * (3 if k < NPAIR else 4))
                if k % NPAIR:
                    act.wait_ge(S["ms_ready"], chain_at_head(k))
                free(tile, fn(two(xs[:, k % 2, :]), pj[tile % 2][:, :, 0:HALF], ACT.Square))
                act.wait_ge(pair_free(tile), tile // 2 + 1)
                act.sem_inc(S["fk_sq"], 1)

            def chain_at_head(k):
                first = 3 + RH if k < NPAIR else 3 + RH + NPAIR
                return first + max(k % NPAIR - 1, 0)

            for p in range(NPAIR):
                head_tile(p, T_KV + p, W_KV + p)
                if p:
                    root()
            root()
            def rows_out(p):
                act.wait_ge(S["fvt_ready"], p + 1)
                fn(fv[:, :, p * P:(p + 1) * P], bk[2][:].rearrange("p (r c) -> p r c", r=RT), ACT.Copy)
                fn(fvs[:, p * P:(p + 1) * P], bk[3][0:NS, 0:P], ACT.Copy).then_inc(S["fvt_evac"], 1)

            for p in range(NPAIR):
                tile = T_KV + NPAIR + p
                wait_tile(act, (W_KV + NPAIR + p + 1) * SLAB)
                if p < 2:
                    act.wait_ge(S["fk_done"], NPAIR)
                else:
                    act.wait_ge(S["fvt_ready"], p - 1)
                    act.wait_ge(S[f"fv_saved{p % 2}"], 16 * (p // 2))
                free(tile, fn(two(fraw[:, p % 2, :]), pj[tile % 2][:, :, 0:HALF], ACT.Copy))
                act.wait_ge(pair_free(tile), tile // 2 + 1)
                act.sem_inc(S["fv_raw"], 1)
                act.dma_start(A["o_v"][:, p, :], fraw[:, p % 2, :]).then_inc(S[f"fv_saved{p % 2}"], 16)
                if p:
                    rows_out(p - 1)
            rows_out(NPAIR - 1)
            act.wait_ge(S["lf_raw"], 1)
            fn(lfa[:, 1, :], lfa[:, 1, :], ACT.Exp, scale=-1.0).then_inc(S["lf_exp"], 1)
            act.wait_ge(S["fv_saved0"], 16 * (NPAIR // 2))
            act.wait_ge(S["fv_saved1"], 16 * (NPAIR // 2))

            norm(3, 6 * DT)
            for p in range(NPAIR):
                head_tile(NPAIR + p, T_Q + p, W_Q + p)
                if p:
                    root()
            root()
            for i in range(2):
                act.wait_ge(S["R_psum"], i + 1)
                fn(Rb[:, i * DEC_B // 2:(i + 1) * DEC_B // 2].rearrange("p b g h -> p (b g h)"), bk[2 + i][:], ACT.Copy).then_inc(S["R_done"], 1)
            act.wait_ge(S["nFs_psum"], 1)
            fn(nFs[:], bk[2][0:NS, 0:FH], ACT.Copy).then_inc(S["nFs_ready"], 1)

            def bias_in(h):
                if h >= 2:
                    act.wait_ge(S["s_max"], RT * (h - 1))
                act.dma_start(bias[:, h % 2, :], A["nF"][h:h + 1, :].to_broadcast([P, SEQ])).then_inc(S[f"bias_in{h % 2}"], 16)

            def expo(t):
                n = (t % 4 + 1) * P
                act.wait_ge(S["s_max"], t + 1)
                fn(pr[:, t % 4, 0:n], pr[:, t % 4, 0:n], ACT.Exp, bias=nmx[:, t:t + 1], accum_out=rs[:, t:t + 1]).then_inc(S["p_exp"], 1)

            def turned_out(t):
                n = (t % RT + 1) * P
                act.wait_ge(S["pT_psum"], t + 1)
                if t >= 2:
                    act.wait_ge(S["fo_psum"], t - 1)
                fn(pT[:, t % 2, 0:n], pj[1][:, t % 2, 0:n], ACT.Copy).then_inc(S["pT_ready"], 1)

            def head_out(h):
                r = (h % 2) * HD
                act.wait_ge(S["fo_psum"], RT * h + RT)
                fn(foT[r:r + HD, h // 2, 0:SEQ], bk[0][r:r + HD, :], ACT.Copy).then_inc(S["fo_done"], 1)

            def diag(ap):
                return ap.rearrange("p (a n) -> p a n", n=P + 8)[:, :, 0:8]

            def queries_hi(b):
                if b:
                    wait_tile(act, (W_PAST + NPG * b) * SLAB)
                fn(diag(qd_hi[:]), qbd[:, :, b, :], ACT.Copy).then_inc(S["qd_hi_ready"], 1)

            def values_hi(v):
                act.wait_ge(S[f"v_in{v % VR}"], 32 * (v // VR + 1))
                if v >= 2:
                    act.wait_ge(S["v_used"], v - 1)
                fn(v_hi[:, v % 2, :], vraw[:, v % VR, :], ACT.Copy).then_inc(S["v_hi_ready"], 1)

            def sample_exp(b):
                act.wait_ge(S["sm_ready"], b + 1)
                w = ss[b % 2]
                fn(w[:], w[:], ACT.Exp, bias=nm[:, b:b + 1], accum_out=ls[:, b:b + 1]).then_inc(S["s_exp"], 1)

            def weights_hi(b):
                act.wait_ge(S["sT_psum"], b + 1)
                if b >= 2:
                    act.wait_ge(S["v_used"], NPG * (b - 1))
                fn(sT[:, b % 2, :, 0:64], bk[2][:].rearrange("p (k n) -> p k n", n=64), ACT.Copy).then_inc(S["sT_hi"], 1)

            def new_weights(b):
                act.wait_ge(S["pn_psum"], b + 1)
                fn(pn[:, b % 2, :], bk[2][0:NS, 0:64], ACT.Copy).then_inc(S["pn_ready"], 1)

            def sums_out(n):
                act.wait_ge(S["v_used"], 4 * (n + 1))
                if n:
                    act.wait_ge(S["back_psum"], n)
                fn(so[:], bk[3][:], ACT.Copy).then_inc(S["so_out"], 1)

            act.wait_ge(S["nF_out"], 16)
            act.wait_ge(S["fk_done"], 2 * NPAIR)
            bias_in(0)
            bias_in(1)
            act.wait_ge(S["qd_zero"], 2)
            act.wait_ge(S["qbd_ready"], 2 * NPAIR + 1)
            for t in range(STEPS):
                b, g = t // NPG, t % NPG
                if g == 0 and b < DEC_B:
                    queries_hi(b)
                if t < TQ:
                    expo(t)
                if 0 <= t - 2 < TQ:
                    turned_out(t - 2)
                if t >= 7 and (t - 7) % RT == 0 and (t - 7) // RT < FH:
                    head_out((t - 7) // RT)
                if t % RT == RT - 1 and t // RT + 2 < FH:
                    bias_in(t // RT + 2)
                if 1 <= b <= DEC_B:
                    if g == 0:
                        sample_exp(b - 1)
                    if g == 2:
                        weights_hi(b - 1)
                    if g == 3:
                        new_weights(b - 1)
                if 0 <= t - VLAG + 1 < UNITS:
                    values_hi(t - VLAG + 1)
                if t >= VLAG and (t - VLAG) % 4 == 3:
                    sums_out((t - VLAG) // 4)
            act.wait_ge(S["so_done"], 4 * DEC_B)
            for p in range(NPAIR):
                fn(h_hi[:, p, :], foT[:, p, :], ACT.Copy).then_inc(S["fo_hi_ready"], 1)
            keys_saved(act)
            norm(4, 9 * DT)
            feed_forward(1)

        @block.vector
        def _(dve):
            V = nc.vector
            links = [0]

            def link(ins):
                links[0] += 1
                ins.then_inc(S["dve_chain"], 1)
                dve.wait_ge(S["dve_chain"], links[0])

            chain = [0]

            def variance(scale):
                c = chain[0]
                dve.wait_ge(S["ms_ready"], c + 1)
                for half in range(2):
                    i = V.tensor_scalar(var[:, half * HALF:(half + 1) * HALF], bk[half][:, 0:HALF], scale, EPS, ALU.mult, ALU.add)
                i.then_inc(S["var_ready"], 1)

            def refine():
                c = chain[0]
                dve.wait_ge(S["r_root"], c + 1)
                link(V.tensor_tensor(newt[:], rstd[:], rstd[:], ALU.mult))
                link(V.scalar_tensor_tensor(out=newt[:], in0=newt[:], scalar=-0.5, in1=var[:], op0=ALU.mult, op1=ALU.mult))
                link(V.scalar_tensor_tensor(out=rstd[:], in0=newt[:], scalar=1.5, in1=rstd[:], op0=ALU.add, op1=ALU.mult))
                chain[0] += 1

            hs = hf[:, 0, 0:DT * NS].rearrange("p (k n) -> p k n", k=DT)

            def sample(ap):
                return ap.rearrange("p (b t) -> p b t", b=DEC_B)

            def over_t(ap):
                return ap.unsqueeze(2).to_broadcast([P, DEC_B, DEC_T])

            def norm(z, g, shift, scale):
                link(V.tensor_scalar(gain[:], mod[:, scale:scale + DT, :], 1.0, None, ALU.add))
                V.tensor_tensor(gain[:], gain[:], vec[:, g:g + DT].unsqueeze(2).to_broadcast([P, DT, NC]), ALU.mult).then_inc(S["gains"], 1)
                dve.wait_ge(S["gains"], z + 1)
                by_time = [P, DT, DEC_B, DEC_T]
                rows = hs.rearrange("p k (b t) -> p k b t", b=DEC_B)
                r = rstd if z != 3 else hf[:, 1, :]
                if z:
                    link(V.tensor_tensor(rows, x[:, :, SEQ:NT].rearrange("p k (b t) -> p k b t", b=DEC_B), gain[:, :, 1:NC].unsqueeze(3).to_broadcast(by_time), ALU.mult))
                    if z != 3:
                        variance(1.0 / D)
                        refine()
                    if z == 2:
                        V.tensor_copy(hf[:, 1, :], rstd[:])
                else:
                    link(V.tensor_tensor(rows, x[:, :, SEQ:NT].rearrange("p k (b t) -> p k b t", b=DEC_B), gain[:, :, 1:NC].unsqueeze(3).to_broadcast(by_time), ALU.mult))
                for k in range(DT + 1):
                    if k < DT:
                        if k >= 2:
                            dve.wait_ge(S["h_ready"], z * DT + k - 1)
                        V.scalar_tensor_tensor(out=xs[:, k % 2, 0:SEQ], in0=x[:, k, 0:SEQ], scalar=gain[:, k, 0:1], in1=r[:, 0:SEQ],
                                               op0=ALU.mult, op1=ALU.mult).then_inc(S["scaled"], 1)
                    if k == 0:
                        link(V.tensor_tensor(hs, hs, r[:, SEQ:NT].unsqueeze(1).to_broadcast([P, DT, NS]), ALU.mult))
                        V.tensor_tensor(rows, rows, mod[:, shift:shift + DT, 1:NC].unsqueeze(3).to_broadcast(by_time), ALU.add).then_inc(S["hs_full"], 1)
                    else:
                        if k == 1:
                            dve.wait_ge(S["hs_hi"], z + 1)
                            V.tensor_tensor(h_lo[:, :, SEQ:NT], hs, h_hi[:, :, SEQ:NT].bitcast(F32), ALU.subtract)
                        dve.wait_ge(S["hi_ready"], z * DT + k)
                        V.scalar_tensor_tensor(out=h_lo[:, k - 1, 0:SEQ], in0=xs[:, (k - 1) % 2, 0:SEQ], scalar=mod[:, shift + k - 1, 0:1],
                                               in1=h_hi[:, k - 1, 0:SEQ].bitcast(F32), op0=ALU.add, op1=ALU.subtract).then_inc(S["h_ready"], 1)

            def residual(tile, done, gate_at):
                for k in range(DT):
                    n = tile + k
                    wait_tile(dve, done(k))
                    ps = pj[n % 2]
                    link(V.scalar_tensor_tensor(out=x[:, k, 0:HALF], in0=ps[:, 0, 0:HALF], scalar=gain1[:, k, 0:1], in1=x[:, k, 0:HALF],
                                                op0=ALU.mult, op1=ALU.add))
                    link(V.scalar_tensor_tensor(out=x[:, k, HALF:SEQ], in0=ps[:, 1, 0:SEQ - HALF], scalar=gain1[:, k, 0:1], in1=x[:, k, HALF:SEQ],
                                                op0=ALU.mult, op1=ALU.add))
                    link(V.tensor_tensor(sample(newt[:, 0:NS]), sample(ps[:, 1, SEQ - HALF:HALF]), over_t(gain1[:, k, 1:NC]), ALU.mult))
                    V.tensor_tensor(x[:, k, SEQ:NT], x[:, k, SEQ:NT], newt[:, 0:NS], ALU.add).then_inc(S["x_done"], 1)
                    xn[0] += 1
                    dve.wait_ge(S["x_done"], xn[0])
                    dve.sem_inc(pair_free(n), 1)

            xn = [0]

            def gate_vector(g):
                link(V.tensor_scalar(gain1[:], mod[:, g:g + DT, :], 1.0, None, ALU.add))

            gain1 = ctmp

            blocks = [0]

            def block_rows():
                b = blocks[0]
                wait_tile(dve, block_done(b))
                V.tensor_copy(mev[:], block_bank(b)[0:2 * NC, :]).then_inc(S["mod_rows"], 1)

            def block_out():
                b = blocks[0]
                dve.wait_ge(S["mod_turned"], b + 1)
                f = slice(b * MBLK, (b + 1) * MBLK)
                V.tensor_tensor(mod[:, f, :], block_bank(b)[:, 0:MBLK * NC].rearrange("p (f c) -> p f c", c=NC),
                                vec[:, V_B + b * MBLK:V_B + (b + 1) * MBLK].unsqueeze(2).to_broadcast([P, MBLK, NC]), ALU.add).then_inc(S["m_done"], 1)
                dve.wait_ge(S["m_done"], b + 1)
                blocks[0] += 1

            dve.wait_ge(S["hi_split"], 1)
            V.tensor_scalar(cs[:], ones[:, 0:1].unsqueeze(2).to_broadcast([P, DT, P]), 0.0, None, ALU.mult).then_inc(S["c_ready"], 1)
            dve.wait_ge(S["c_exp"], 1)
            dve.wait_ge(S["cst_in"], 32)
            link(V.tensor_scalar(ctmp[:], ctmp[:], 1.0, None, ALU.add))
            link(V.reciprocal(ctmp[:], ctmp[:]))
            V.tensor_tensor(cact[:], cact[:], ctmp[:], ALU.mult).then_inc(S["c_ready"], 1)
            dve.wait_ge(S["cs_hi_ready"], 1)
            V.tensor_tensor(cs[:, :, NC:2 * NC], cact[:], cs[:, :, 0:NC].bitcast(F32), ALU.subtract).then_inc(S["cs_ready"], 1)
            for s in range(FIRST):
                if s == 3 * MBLK:
                    variance(1.0 / D)
                    refine()
                dve.wait_ge(S["mod_hi"], s + 1)
                V.tensor_tensor(w_lo[:, s % RING, :], first_slab(s), w_hi[:, s % RING, :].bitcast(F32), ALU.subtract).then_inc(S["first_split"], 1)
                if s > MBLK and s % MBLK == 1:
                    block_rows()
                if s > MBLK and s % MBLK == 3:
                    block_out()
            block_out()
            norm(0, V_RET, 0, DT)

            def rope(h, i, dst, scale):
                n = ret_proj_tile(h) + 2 * i
                for t in (n, n + 1):
                    dve.wait_ge(pair_free(t), t // 2 + 1)
                a, b = xs[:, 0, :], xs[:, 1, :]
                cos, sin = rc[:, R_COS:R_COS + NT], rc[:, R_SIN:R_SIN + NT]
                sine = newt[:]

                def times(out, ps, tab):
                    return V.scalar_tensor_tensor(out=out, in0=ps, scalar=scale, in1=tab, op0=ALU.mult, op1=ALU.mult)
                link(times(dst[:, 0, :], a, cos))
                link(times(sine, b, sin))
                link(V.tensor_tensor(dst[:, 0, :], dst[:, 0, :], newt[:], ALU.subtract))
                link(times(dst[:, 1, :], a, sin))
                link(times(sine, b, cos))
                V.tensor_tensor(dst[:, 1, :], dst[:, 1, :], newt[:], ALU.add).then_inc(S["rope_done"], 1)
                dve.wait_ge(S["rope_done"], 2 * h + i + 1)

            def cross(h):
                link(V.tensor_tensor(qx[:], qT[:, :, SEQ:NT],
                                     rc[:, R_CR + h * NS:R_CR + (h + 1) * NS].unsqueeze(1).to_broadcast([P, 2, NS]), ALU.mult))

            def silu(h):
                for f in range(4):
                    n = 4 * h + f
                    e = hf[:, f % 2, :]
                    dve.wait_ge(S["silu_exp"], n + 1)
                    link(V.tensor_scalar(e, e, 1.0, None, ALU.add))
                    link(V.reciprocal(e, e))
                    t = ret_proj_tile(h) + 8 + f
                    dve.wait_ge(pair_free(t), t // 2 + 1)
                    V.tensor_tensor(gate[:, f, :], e, gate[:, f, :], ALU.mult).then_inc(S["silu_done"], 1)
                    dve.wait_ge(S["silu_done"], n + 1)

            dve.wait_ge(S["rc_in"], 16)
            rope(0, 0, qT, 1.0)
            rope(0, 1, kT, DK ** -0.5)
            silu(0)
            for h in range(RH):
                last_head = h == RH - 1
                if h:
                    dve.wait_ge(S["os_ready"], h)
                cross(h)
                at = 0
                for j in range(RT):
                    n = SEQ - j * P
                    dve.wait_ge(S["scores_ready"], 4 * h + j + 1)
                    dve.wait_ge(S[f"dec_in{h % 2}"], 16 * (h // 2 + 1))
                    if h and j == 0:
                        dve.wait_ge(S["o_ready"], 4 * h)
                    V.tensor_tensor(att[:, at:at + n], bk[j][:, 0:n], dec[:, h % 2, 0:n], ALU.mult).then_inc(S["decayed"], 1)
                    at += n
                V.tensor_tensor(atts[:], bk[3][0:NS, P:P + NS], rc[0:NS, R_DS + h * NS:R_DS + (h + 1) * NS], ALU.mult).then_inc(S["decayed"], 1)
                dve.wait_ge(S["tr_evac"], 8 * h + 8)
                def decayed_keys(b):
                    n = h * DEC_B + b
                    if n >= 2:
                        dve.wait_ge(S["upd_ready"], 2 * (n - 1))
                    V.tensor_scalar(kb[:, b % 2, :], ks[:], rc[0:NS, R_KS + h * DEC_B + b:R_KS + h * DEC_B + b + 1], None, ALU.mult)\
                        .then_inc(S["kb_ready"], 1)

                decayed_keys(0)
                for b in range(DEC_B):
                    n = h * DEC_B + b
                    if b in (2, 4, 6):
                        block_out()
                    for d in range(2):
                        dve.wait_ge(S["upd_ready"], 2 * n + d + 1)
                        s = st[:, n % 2, d, :]
                        V.scalar_tensor_tensor(out=s, in0=s, scalar=rc[:, R_CD + h:R_CD + h + 1], in1=bk[1][:], op0=ALU.mult, op1=ALU.add)\
                            .then_inc(S["upd_done"], 1)
                    if b + 1 < DEC_B:
                        decayed_keys(b + 1)
                    if b % 2:
                        block_rows()
                    if b == 1 and not last_head:
                        rope(h + 1, 0, qT, 1.0)
                    if b == 3 and not last_head:
                        rope(h + 1, 1, kT, DK ** -0.5)
                block_out()
                variance(1.0 / DV)
                refine()
                for e in range(5):
                    if e < 4:
                        link(V.tensor_tensor(oT[:, e, :], oT[:, e, :], rstd[:], ALU.mult))
                        V.tensor_tensor(oT[:, e, :], oT[:, e, :], gate[:, e, :], ALU.mult).then_inc(S["gated"], 1)
                    if e:
                        dve.wait_ge(S["og_hi_ready"], 4 * h + e)
                        V.tensor_tensor(og_lo[:, e - 1, :], oT[:, e - 1, :], og_hi[:, e - 1, :].bitcast(F32), ALU.subtract).then_inc(S["og_ready"], 1)
                if not last_head:
                    silu(h + 1)
                if h == 0:
                    gate_vector(2 * DT)
                residual(ret_out_tile(h), lambda k: out_done(h, k), 2 * DT)
                block_rows()
                block_out()

            def feed_forward(layer, g):
                gate_vector(g)
                for half in range(2):
                    u = 2 * layer + half
                    out0 = place_of["g", u, 0] * SLAB
                    t0 = ff_tile(layer, half)
                    for m in range(FFT):
                        if m in (4, 9) and layer == 0:
                            block_rows()
                        if m in (5, 10) and layer == 0:
                            block_out()
                        n = u * FFT + m
                        e = sig[:, n % 2, :]
                        dve.wait_ge(S["silu_exp"], 4 * RH + n + 1)
                        link(V.tensor_scalar(e, e, 1.0, None, ALU.add))
                        link(V.reciprocal(e, e))
                        if n >= 2:
                            dve.wait_ge(S["hid_hi_ready"], n - 1)
                        dve.wait_ge(pair_free(t0 + 2 * m), (t0 + 2 * m) // 2 + 1)
                        link(V.tensor_tensor(hid[:, n % 2, :], e, xs[:, n % 2, :], ALU.mult))
                        wait_tile(dve, hidden_done(u, 2 * m + 1))
                        V.tensor_tensor(two(hid[:, n % 2, :]), two(hid[:, n % 2, :]), pj[(t0 + 2 * m + 1) % 2][:, :, 0:HALF], ALU.mult)\
                            .then_inc(S["hid_full"], 1)
                        dve.wait_ge(S["hid_full"], n + 1)
                        dve.sem_inc(pair_free(t0 + 2 * m + 1), 1)
                        dve.wait_ge(S["hid_hi_ready"], n + 1)
                        V.tensor_tensor(hid_lo[:, m, :], hid[:, n % 2, :], hid_hi[:, m, :].bitcast(F32), ALU.subtract).then_inc(S["hid_ready"], 1)
                    residual(t0 + 2 * FFT, lambda k: out0 + FFT * (k + 1), g)

            states_saved(dve)
            dve.wait_ge(S["sp_saved"], 16 * 2 * RH)
            norm(1, V_FFN, 3 * DT, 4 * DT)
            feed_forward(0, 5 * DT)
            norm(2, V_KV, 12 * DT, 13 * DT)

            def head_rows(k, dst, g):
                variance(1.0 / HD)
                refine()
                dve.wait_ge(S["fk_raw"], k + 1)
                V.scalar_tensor_tensor(out=dst, in0=fraw[:, k % 2, :], scalar=g, in1=rstd[:], op0=ALU.mult, op1=ALU.mult).then_inc(S["fk_done"], 1)

            for p in range(NPAIR):
                head_rows(p, fkT[:, p, :], vec[:, V_KN:V_KN + 1])

            n = T_KV + 2 * NPAIR
            wait_tile(dve, (W_KV + 17) * SLAB)
            z, u, s2, acc = (lfa[:, i, :] for i in range(4))
            link(V.tensor_scalar(two(z), pj[n % 2][0:FH, :, 0:HALF], vec[0:FH, V_BF:V_BF + 1], None, ALU.add))
            dve.sem_inc(pair_free(n), 1)
            link(V.tensor_scalar(u, z, -1.0, None, ALU.mult))
            V.tensor_tensor(u, u, z, ALU.max).then_inc(S["lf_raw"], 1)
            norm(3, V_ATT, 6 * DT, 7 * DT)
            run = lfa[:, 1, SEQ:NT].rearrange("p (b t) -> p b t", b=DEC_B)

            def series(*odds):
                for odd in odds:
                    link(V.tensor_tensor(acc, acc, s2, ALU.mult))
                    link(V.tensor_scalar(acc, acc, 1.0 / odd, None, ALU.add))

            def forget(part):
                if part == 0:
                    dve.wait_ge(S["lf_exp"], 1)
                    link(V.tensor_scalar(s2, u, 2.0, None, ALU.add))
                    link(V.reciprocal(s2, s2))
                    link(V.tensor_tensor(u, u, s2, ALU.mult))
                if part == 1:
                    link(V.tensor_tensor(s2, u, u, ALU.mult))
                    link(V.tensor_scalar(acc, s2, 1.0 / 17, 1.0 / 15, ALU.mult, ALU.add))
                    series(13)
                if part == 2:
                    series(11, 9)
                if part == 3:
                    series(7, 5)
                if part == 4:
                    series(3, 1)
                if part == 5:
                    link(V.tensor_tensor(acc, acc, u, ALU.mult))
                    link(V.tensor_scalar(z, z, 0.0, None, ALU.min))
                    V.scalar_tensor_tensor(out=lf[:], in0=acc, scalar=-2.0, in1=z, op0=ALU.mult, op1=ALU.add).then_inc(S["lf_done"], 1)
                    dve.wait_ge(S["lf_done"], 1)
                if part == 6:
                    link(V.memset(lfa[:, 0, 0:SEQ], 1.0))
                    link(V.tensor_tensor_scan(lfa[:, 1, 0:SEQ], lfa[:, 0, 0:SEQ], lf[:, 0:SEQ], 0.0, ALU.mult, ALU.add))
                    link(V.tensor_copy(lfa[:, 1, SEQ:NT], lf[:, SEQ:NT]))
                    for t in range(1, DEC_T):
                        link(V.tensor_tensor(run[:, :, t:t + 1], run[:, :, t:t + 1], run[:, :, t - 1:t], ALU.add))
                    V.tensor_scalar(negF[:], lfa[:, 1, :], -1.0, None, ALU.mult).then_inc(S["nF_ready"], 1)
                if part == 7:
                    dve.wait_ge(S["plf_in"], 16 * UNITS)
                    link(V.memset(suf[:, :, NPG - 1, :], 0.0))
                    for g in range(NPG - 2, -1, -1):
                        link(V.tensor_tensor(suf[:, :, g, :], suf[:, :, g + 1, :], plf[:, :, g + 1, :], ALU.add))
                    dve.sem_inc(S["suf_ready"], 1)

            link(V.tensor_scalar(m0[:], vec[:, V_QN:V_QN + 1], HD ** -0.5, None, ALU.mult))
            for p in range(NPAIR):
                forget(p)
                head_rows(NPAIR + p, fqT[:, p, :], m0[:])
            V.tensor_copy(idb[:], ident).then_inc(S["idb_ready"], 1)
            V.tensor_copy(cmb[:], cst[:, C_CM:C_CM + P]).then_inc(S["idb_ready"], 1)

            dve.wait_ge(S["R_psum"], 2)
            dve.wait_ge(S["fk_done"], 2 * NPAIR)
            V.tensor_scalar(qd_hi[:], ones[:, 0:1].to_broadcast([P, NPAIR * (P + 8)]), 0.0, None, ALU.mult).then_inc(S["qd_zero"], 1)
            V.tensor_scalar(qd_lo[:], ones[:, 0:1].to_broadcast([P, NPAIR * (P + 8)]), 0.0, None, ALU.mult).then_inc(S["qd_zero"], 1)
            V.memset(qbd[:], 0.0).then_inc(S["qbd_ready"], 1)
            dve.wait_ge(S["qbd_ready"], 1)
            for p in range(NPAIR):
                for j in range(2):
                    r = slice(j * HD, (j + 1) * HD)
                    V.tensor_copy(qbd[r, p, :, j * DEC_T:(j + 1) * DEC_T], sample(fqT[r, p, SEQ:NT])).then_inc(S["qbd_ready"], 1)

            def top(t):
                n = (t % 4 + 1) * P
                dve.wait_ge(S["s_psum"], t + 1)
                h = t // RT
                dve.wait_ge(S[f"bias_in{h % 2}"], 16 * (h // 2 + 1))
                if t >= 4:
                    dve.wait_ge(S["pT_psum"], t - 3)
                link(V.tensor_tensor_reduce(out=pr[:, t % 4, 0:n], in0=s_psum(t)[:, 0:n], in1=bias[:, (t // 4) % 2, 0:n], scale=1.0, scalar=-3e38,
                                            op0=ALU.add, op1=ALU.max, accum_out=mx[:, t:t + 1]))
                V.tensor_scalar(nmx[:, t:t + 1], mx[:, t:t + 1], -1.0, None, ALU.mult).then_inc(S["s_max"], 1)

            def s_psum(t):
                return pj[0][:, t % 2, :]

            def unit_sum(t):
                n = (t % 4 + 1) * P
                dve.wait_ge(S["p_exp"], t + 1)
                link(V.reciprocal(rsi[:, t:t + 1], rs[:, t:t + 1]))
                V.tensor_scalar(pr[:, t % 4, 0:n], pr[:, t % 4, 0:n], rsi[:, t:t + 1], None, ALU.mult).then_inc(S["p_done"], 1)

            dve.wait_ge(S["sn_psum"], 1)
            new = bk[3][0:NS, :].rearrange("p (a b c t) -> p b a c t", a=NPAIR, b=DEC_B, c=2)
            nf = nFs[:].rearrange("p (a c) -> p a c", c=2).unsqueeze(3).to_broadcast([NS, NPAIR, 2, DEC_T])
            for b in range(DEC_B):
                V.tensor_tensor(sn[:, b], new[:, b], nf, ALU.add).then_inc(S["sn_done"], 1)
                dve.wait_ge(S["sn_done"], 2 * b + 1)
                V.tensor_tensor(sn[:, b].rearrange("p a c t -> p (a c) t"), sn[:, b].rearrange("p a c t -> p (a c) t"),
                                cst[0:NS, C_NM + b * DEC_T:C_NM + (b + 1) * DEC_T].unsqueeze(1).to_broadcast([NS, FH, DEC_T]), ALU.add)\
                    .then_inc(S["sn_done"], 1)
            dve.wait_ge(S["sn_done"], 2 * DEC_B)

            def diag(ap):
                return ap.rearrange("p (a n) -> p a n", n=P + 8)[:, :, 0:8]

            def queries_lo(b):
                dve.wait_ge(S["qd_hi_ready"], b + 1)
                V.tensor_tensor(diag(qd_lo[:]), qbd[:, :, b, :], diag(qd_hi[:].bitcast(F32)), ALU.subtract).then_inc(S["qd_ready"], 1)

            def spread_sums(n):
                if n >= 2:
                    wait_tile(dve, (W_PAST + 2 * (n - 1)) * SLAB)
                V.tensor_copy(Rx[:, n % 2].rearrange("p g (h t) -> p g h t", t=DEC_T),
                              Rb[:, n // 4, 2 * (n % 4):2 * (n % 4) + 2, :].unsqueeze(3).to_broadcast([P, 2, FH, DEC_T])).then_inc(S["Rx_ready"], 1)

            def scores_out(n):
                c = n % 4
                wait_tile(dve, (W_PAST + 2 * (n + 1)) * SLAB)
                V.tensor_copy(ss[n // 4 % 2][:, c * 256:(c + 1) * 256], bk[1][0:64, 0:256]).then_inc(S["ks_out"], 1)

            def new_out(b):
                dve.wait_ge(S["snT_psum"], b + 1)
                V.tensor_copy(ss[b % 2][:, PAST:PAST + NS], bk[2][0:64, 0:NS]).then_inc(S["snT_out"], 1)

            def row_max(b):
                dve.wait_ge(S["snT_out"], b + 1)
                dve.wait_ge(S["ks_out"], 4 * b + 4)
                link(V.tensor_reduce(nm[:, b:b + 1], ss[b % 2][:], AX.X, ALU.max))
                V.tensor_scalar(nm[:, b:b + 1], nm[:, b:b + 1], -1.0, None, ALU.mult).then_inc(S["sm_ready"], 1)

            def row_sum(b):
                dve.wait_ge(S["s_exp"], b + 1)
                link(V.reciprocal(li[:, b:b + 1], ls[:, b:b + 1]))
                V.tensor_scalar(dg[:], cst[0:64, C_ID:C_ID + 64], li[:, b:b + 1], None, ALU.mult).then_inc(S["dg_ready"], 1)

            def weights_lo(b):
                dve.wait_ge(S["sT_hi"], b + 1)
                V.tensor_tensor(sT[:, b % 2, :, 64:128], bk[2][:].rearrange("p (k n) -> p k n", n=64),
                                sT[:, b % 2, :, 0:64].bitcast(F32), ALU.subtract).then_inc(S["sT_ready"], 1)

            def values_lo(v):
                dve.wait_ge(S["v_hi_ready"], v + 1)
                V.tensor_tensor(v_lo[:, v % 2, :], vraw[:, v % VR, :], v_hi[:, v % 2, :].bitcast(F32), ALU.subtract).then_inc(S["v_lo_ready"], 1)

            def heads_out(n):
                b, half = n // 2, n % 2
                dve.wait_ge(S["back_psum"], n + 1)
                for j in range(2):
                    r = slice(j * HD, (j + 1) * HD)
                    o = bk[2][r, 0:32].rearrange("p (a c t) -> p a c t", c=2, t=DEC_T)[:, :, j, :]
                    V.tensor_copy(foT[r, 4 * half:4 * half + 4, SEQ + b * DEC_T:SEQ + (b + 1) * DEC_T], o).then_inc(S["so_done"], 1)

            for t in range(STEPS + 1):
                b, g = t // NPG, t % NPG
                if g == 0 and b < DEC_B:
                    queries_lo(b)
                if 0 < t <= UNITS and t % 2 == 0:
                    scores_out(t // 2 - 1)
                if t < UNITS and t % 2 == 0:
                    spread_sums(t // 2)
                if t > VLAG + 1 and (t - VLAG - 1) % 4 == 0:
                    heads_out((t - VLAG - 1) // 4 - 1)
                if t < TQ:
                    top(t)
                if 0 <= t - 1 < TQ:
                    unit_sum(t - 1)
                if 1 <= b <= DEC_B:
                    if g == 0:
                        row_max(b - 1)
                    if g == 1:
                        row_sum(b - 1)
                    if g == 2:
                        weights_lo(b - 1)
                if b < DEC_B and g == 7:
                    new_out(b)
                if 0 <= t - VLAG + 1 < UNITS:
                    values_lo(t - VLAG + 1)
            dve.wait_ge(S["so_done"], 4 * DEC_B)
            for p in range(NPAIR):
                dve.wait_ge(S["fo_hi_ready"], p + 1)
                V.tensor_tensor(h_lo[:, p, :], foT[:, p, :], h_hi[:, p, :].bitcast(F32), ALU.subtract).then_inc(S["fo_ready"], 1)
            gate_vector(8 * DT)
            residual(T_O, lambda k: (W_O + k + 1) * SLAB, 8 * DT)
            keys_saved(dve)
            norm(4, V_FFN + DT, 9 * DT, 10 * DT)
            feed_forward(1, 11 * DT)


def weight_tiles(w):
    k, n = w.shape
    return w.reshape(k // P, P, n // P, P).transpose(2, 0, 1, 3).reshape(-1, P, P)


def slabs(tiles):
    return np.ascontiguousarray(tiles.reshape(-1, SLAB, P, P).transpose(0, 2, 1, 3)).reshape(-1, P, SLAB * P)


def columns(v):
    return v.reshape(-1, P).T


def feature_major(a):
    return a.T.reshape(-1, P, a.shape[0]).transpose(1, 0, 2)


def token_major(a, lo, hi):
    return a[:, :, lo:hi].transpose(2, 1, 0).reshape(hi - lo, -1)


def kernel(x_prompt, x_sample, cache_k, cache_v, cache_logf, state_ret, page_table, c_prompt, c_sample, w_mod, b_mod,
           ret_norm_g, w_ret_in, w_ret_out, attn_norm_g, w_q, q_norm_g, w_o, ffn_norm_g, w_ffn_in, w_ffn_out,
           kv_norm_g, w_kvmod, b_kvmod, w_kvf, b_f, k_norm_g):
    import concourse.bacc as bacc
    from concourse.bass_utils import run_bass_kernel_spmd

    a = {k: np.asarray(v) for k, v in dict(locals()).items() if k not in ("bacc", "run_bass_kernel_spmd")}
    win, wout = a["w_ret_in"][0], a["w_ret_out"][0]

    def head_in(h):
        cols = [win[:, h * DK:(h + 1) * DK], win[:, D + h * DK:D + (h + 1) * DK],
                win[:, 2 * D + h * DV:2 * D + (h + 1) * DV], win[:, 4 * D + h * DV:4 * D + (h + 1) * DV]]
        return weight_tiles(np.concatenate(cols, axis=1))

    def head_out(h):
        return weight_tiles(wout[h * DV:(h + 1) * DV])

    def ffn(l):
        w, wo, out = a["w_ffn_in"][l], a["w_ffn_out"][l], []
        for half in range(2):
            hidden = []
            for m in range(half * FFT, (half + 1) * FFT):
                hidden.append(weight_tiles(w[:, m * P:(m + 1) * P]))
                hidden.append(weight_tiles(w[:, FF + m * P:FF + (m + 1) * P]))
            out.append((np.concatenate(hidden), weight_tiles(wo[half * FFT * P:(half + 1) * FFT * P])))
        return out

    kvf = np.concatenate([a["w_kvf"], np.zeros((D, P - FH), np.float32)], axis=1)
    wm = np.concatenate([a["w_mod"][0], a["w_mod"][1], a["w_kvmod"]], axis=1)
    wm = iter(wm.reshape(MBLK, 2, P, -1, SEQ).transpose(3, 0, 2, 1, 4).reshape(-1, P, 2 * SEQ))
    tiles_of = {("p", h): head_in(h) for h in range(RH)} | {("o", h): head_out(h) for h in range(RH)}
    for u, (hidden, out) in enumerate(ffn(0) + ffn(1)):
        tiles_of["f", u], tiles_of["g", u] = hidden, out
    tiles_of |= {("k", 0): weight_tiles(kvf), ("q", 0): weight_tiles(a["w_q"][0]), ("a", 0): weight_tiles(a["w_o"][0])}
    stream = [next(wm) if kind == "m" else slabs(tiles_of[kind, h][i * SLAB:(i + 1) * SLAB])[0]
              for kind, h, i in slab_order() if kind != "past"]
    n_pool = a["cache_k"].shape[0]
    cst, rc, dec = constants()
    pad = np.concatenate([a["b_f"], np.zeros(P - FH, np.float32)])
    vec = np.concatenate([columns(v) for v in (
        a["b_mod"][0], a["b_mod"][1], a["b_kvmod"], a["ret_norm_g"][0], a["attn_norm_g"][0], a["ffn_norm_g"][0], a["ffn_norm_g"][1],
        a["kv_norm_g"], np.concatenate([a["q_norm_g"][0]] * 2), np.concatenate([a["k_norm_g"]] * 2), pad)], axis=1)
    ins = {
        "xT": feature_major(np.concatenate([a["x_prompt"][0], a["x_sample"].reshape(NS, D)], axis=0)),
        "cT": feature_major(np.concatenate([a["c_prompt"], a["c_sample"]], axis=0)),
        "w": np.stack(stream),
        "vec": vec, "cst": cst, "rc": rc, "dec": dec,
        "state": a["state_ret"][0].reshape(DEC_B, RH, 2, P, DV).transpose(1, 0, 3, 2, 4),
        "kc": a["cache_k"].reshape(n_pool, PAGE, NPAIR, P).transpose(0, 3, 2, 1).reshape(n_pool, P, D),
        "vc": a["cache_v"].reshape(n_pool, PAGE, D),
        "lf": a["cache_logf"],
        "table": a["page_table"].reshape(1, -1),
    }
    outs = {"o_x": (P, DT, NT), "o_k": (P, NPAIR, NT), "o_v": (P, NPAIR, NT), "o_lf": (FH, NT),
            "st_p": (RH, P, 2, DV), "st_s": (RH, DEC_B, P, 2, DV)}
    nc = bacc.Bacc("TRN2", target_bir_lowering=False, num_devices=1)
    A, arrays = {}, {}
    for name, v in ins.items():
        v = np.ascontiguousarray(v)
        arrays[f"in_{name}"] = v
        A[name] = nc.dram_tensor(f"in_{name}", v.shape, mybir.dt.from_np(v.dtype), kind="ExternalInput").ap()
    for name, shape in outs.items():
        A[name] = nc.dram_tensor(f"out_{name}", shape, F32, kind="ExternalOutput").ap()
    A["nF"] = nc.dram_tensor("neg_running_sums", (FH, SEQ), F32, kind="Internal").ap()
    program(nc, A)
    r = run_bass_kernel_spmd(nc, [arrays], core_ids=[0]).results[0]
    y, k, v, lf = (r[f"out_{n}"] for n in ("o_x", "o_k", "o_v", "o_lf"))
    sp = np.ascontiguousarray(r["out_st_p"].transpose(0, 2, 1, 3)).reshape(1, 1, RH, DK, DV)
    ss = np.ascontiguousarray(r["out_st_s"].transpose(1, 0, 3, 2, 4)).reshape(1, DEC_B, RH, DK, DV)
    return (token_major(y, 0, SEQ).reshape(1, SEQ, D), token_major(y, SEQ, NT).reshape(DEC_B, DEC_T, D), sp, ss,
            token_major(k, 0, SEQ).reshape(1, SEQ, FH, HD), token_major(v, 0, SEQ).reshape(1, SEQ, FH, HD),
            np.ascontiguousarray(lf[:, 0:SEQ].T).reshape(1, SEQ, FH),
            token_major(k, SEQ, NT).reshape(DEC_B, DEC_T, FH, HD), token_major(v, SEQ, NT).reshape(DEC_B, DEC_T, FH, HD),
            np.ascontiguousarray(lf[:, SEQ:NT].T).reshape(DEC_B, DEC_T, FH))
```
